# Optimizing a Trainium2 kernel written in Bass

```python
import jax, jax.numpy as jnp
from jax import lax
import numpy as np

D_MODEL = 1024
BATCH = 1
SEQ = 256
DEPTH = 1

CHUNK = 64
Q_BLOCK = 128
NORM_EPS = 1e-6
FOX_HEADS = 8
FOX_HEAD_DIM = 64
FOX_WIDTH = FOX_HEADS * FOX_HEAD_DIM
MLA_HEADS = 8
MLA_NOPE_DIM = 64
MLA_ROPE_DIM = 32
MLA_V_DIM = 64
MLA_Q_RANK = 256
MLA_KV_RANK = 128
MLA_QK_DIM = MLA_NOPE_DIM + MLA_ROPE_DIM
MLA_WIDTH = MLA_HEADS * MLA_V_DIM
ROPE_THETA = 10000.0
N_BRANCHES = 2
N_EXPERTS = 32
TOP_K = 4
EXPERT_FF = 1024
SWIGLU_LIMIT = 7.0
SWIGLU_ALPHA = 1.702
EXPERT_BLOCK = 256

IN_SIZES = (FOX_WIDTH, FOX_WIDTH, FOX_WIDTH, FOX_HEADS, MLA_Q_RANK, MLA_KV_RANK + MLA_ROPE_DIM, N_BRANCHES * D_MODEL)
IN_COLS = FOX_WIDTH * 3 + FOX_HEADS + MLA_Q_RANK + MLA_KV_RANK + MLA_ROPE_DIM + N_BRANCHES * D_MODEL

kernel_name = 'hybrid_fox_mla_gated_moe_block'

def rms_norm(x, g):
    xf = x.astype(jnp.float32)
    y = xf * lax.rsqrt(jnp.mean(xf * xf, axis=-1, keepdims=True) + NORM_EPS)
    return (y * g.astype(jnp.float32)).astype(x.dtype)

def apply_rope(x, cos, sin):
    x1, x2 = jnp.split(x, 2, axis=-1)
    return jnp.concatenate([x1 * cos - x2 * sin, x2 * cos + x1 * sin], axis=-1).astype(x.dtype)

def blocked_attention(q, k, v, scale, log_f_cum=None):
    S = q.shape[1]
    neg = jnp.finfo(jnp.float32).min
    outs = []
    for i in range(S // Q_BLOCK):
        q0, q1 = i * Q_BLOCK, (i + 1) * Q_BLOCK
        s = jnp.einsum('bqhd,bkhd->bhqk', q[:, q0:q1], k[:, :q1]).astype(jnp.float32) * scale
        tq = jnp.arange(q0, q1)[:, None]
        tk = jnp.arange(q1)[None, :]
        if log_f_cum is None:
            allowed = (tk // CHUNK) <= (tq // CHUNK)
        else:
            allowed = tk <= tq
            s = s + (log_f_cum[:, :, q0:q1, None] - log_f_cum[:, :, None, :q1])
        p = jax.nn.softmax(jnp.where(allowed, s, neg), axis=-1)
        outs.append(jnp.einsum('bhqk,bkhd->bqhd', p.astype(v.dtype), v[:, :q1]))
    return jnp.concatenate(outs, axis=1)

def token_mixer(h, positions, w_in, b_fgate, g_q_a, w_q_b, g_kv_a, w_kv_b, w_fox_out, w_mla_out, b_merge, w_o):
    B, S, _ = h.shape
    proj = h @ w_in
    q_f, k_f, v_f, f_logit, q_lat, kv_lat, gate_logit = jnp.split(proj, list(np.cumsum(IN_SIZES)[:-1]), axis=-1)

    qf = q_f.reshape(B, S, FOX_HEADS, FOX_HEAD_DIM)
    kf = k_f.reshape(B, S, FOX_HEADS, FOX_HEAD_DIM)
    vf = v_f.reshape(B, S, FOX_HEADS, FOX_HEAD_DIM)
    log_f = jax.nn.log_sigmoid(f_logit.astype(jnp.float32) + b_fgate.astype(jnp.float32))
    log_f_cum = jnp.cumsum(log_f, axis=1).transpose(0, 2, 1)
    y_fox = blocked_attention(qf, kf, vf, FOX_HEAD_DIM ** -0.5, log_f_cum).reshape(B, S, FOX_WIDTH)

    q = (rms_norm(q_lat, g_q_a) @ w_q_b).reshape(B, S, MLA_HEADS, MLA_QK_DIM)
    q_nope, q_pe = q[..., :MLA_NOPE_DIM], q[..., MLA_NOPE_DIM:]
    c_kv, k_pe = kv_lat[..., :MLA_KV_RANK], kv_lat[..., MLA_KV_RANK:]
    kv = (rms_norm(c_kv, g_kv_a) @ w_kv_b).reshape(B, S, MLA_HEADS, MLA_NOPE_DIM + MLA_V_DIM)
    k_nope, v_m = kv[..., :MLA_NOPE_DIM], kv[..., MLA_NOPE_DIM:]
    half = MLA_ROPE_DIM // 2
    inv_freq = ROPE_THETA ** (-jnp.arange(half, dtype=jnp.float32) / half)
    ang = positions.astype(jnp.float32)[..., None] * inv_freq
    cos, sin = jnp.cos(ang), jnp.sin(ang)
    q_pe = apply_rope(q_pe, cos[:, :, None, :], sin[:, :, None, :])
    k_pe = apply_rope(k_pe, cos, sin)
    q_m = jnp.concatenate([q_nope, q_pe], axis=-1)
    k_m = jnp.concatenate([k_nope, jnp.broadcast_to(k_pe[:, :, None, :], (B, S, MLA_HEADS, MLA_ROPE_DIM))], axis=-1)
    y_mla = blocked_attention(q_m, k_m, v_m, MLA_QK_DIM ** -0.5, None).reshape(B, S, MLA_WIDTH)

    gates = jax.nn.sigmoid(gate_logit.reshape(B, S, N_BRANCHES, D_MODEL) + b_merge)
    merged = gates[:, :, 0] * (y_fox @ w_fox_out) + gates[:, :, 1] * (y_mla @ w_mla_out)
    return merged @ w_o

def expert_ffn(xb, w_gu, b_gu, w_d, b_d):
    gu = xb @ w_gu + b_gu
    gate = jnp.minimum(gu[..., :EXPERT_FF], SWIGLU_LIMIT)
    up = jnp.clip(gu[..., EXPERT_FF:], -SWIGLU_LIMIT, SWIGLU_LIMIT)
    glu = gate * jax.nn.sigmoid(SWIGLU_ALPHA * gate)
    return ((up + 1.0) * glu) @ w_d + b_d

def moe_ffn(h, w_router, b_router, w_gu, b_gu, w_d, b_d):
    B, S, D = h.shape
    N = B * S
    A = N * TOP_K
    t = h.reshape(N, D)
    logits = (t @ w_router).astype(jnp.float32) + b_router.astype(jnp.float32)
    top_val, top_idx = lax.top_k(logits, TOP_K)
    top_w = jax.nn.softmax(top_val, axis=-1)
    flat_e = top_idx.reshape(A)
    flat_w = top_w.reshape(A)
    order = jnp.argsort(flat_e)
    sorted_e = flat_e[order]
    sorted_tok = (order // TOP_K).astype(jnp.int32)
    counts = jnp.zeros((N_EXPERTS,), jnp.int32).at[flat_e].add(1)
    padded = (counts + EXPERT_BLOCK - 1) // EXPERT_BLOCK * EXPERT_BLOCK
    pad_end = jnp.cumsum(padded)
    pad_start = pad_end - padded
    start = jnp.cumsum(counts) - counts
    row = pad_start[sorted_e] + (jnp.arange(A, dtype=jnp.int32) - start[sorted_e])
    R = A + N_EXPERTS * EXPERT_BLOCK
    n_blocks = R // EXPERT_BLOCK
    row_tok = jnp.zeros((R,), jnp.int32).at[row].set(sorted_tok)
    row_w = jnp.zeros((R,), jnp.float32).at[row].set(flat_w[order])
    block_e = jnp.minimum(jnp.searchsorted(pad_end, jnp.arange(n_blocks, dtype=jnp.int32) * EXPERT_BLOCK, side='right'), N_EXPERTS - 1)
    xs = t[row_tok].reshape(n_blocks, EXPERT_BLOCK, D)
    ys = lax.map(lambda a: expert_ffn(a[0], w_gu[a[1]], b_gu[a[1]], w_d[a[1]], b_d[a[1]]), (xs, block_e))
    ys = ys.reshape(R, D) * row_w[:, None].astype(ys.dtype)
    return jax.ops.segment_sum(ys, row_tok, num_segments=N).reshape(B, S, D)

def setup_inputs(seed: int = 0) -> dict:
    key = jax.random.key(seed)
    ks = jax.random.split(key, 24)
    f32 = jnp.float32
    L = DEPTH

    def nrm(k, shape, scale):
        return jax.random.normal(k, shape, f32) * scale

    def gain(k, shape):
        return 1.0 + 0.05 * jax.random.normal(k, shape, f32)

    x = jax.random.normal(ks[0], (BATCH, SEQ, D_MODEL), f32)
    offsets = jax.random.randint(ks[1], (BATCH, 1), 0, 8192, dtype=jnp.int32)
    positions = offsets + jnp.arange(SEQ, dtype=jnp.int32)[None, :]
    return {
        'x': x,
        'positions': positions,
        'g_attn_norm': gain(ks[2], (L, D_MODEL)),
        'w_in': nrm(ks[3], (L, D_MODEL, IN_COLS), D_MODEL ** -0.5),
        'b_fgate': 3.0 + 0.5 * jax.random.normal(ks[4], (L, FOX_HEADS), f32),
        'g_q_a': gain(ks[5], (L, MLA_Q_RANK)),
        'w_q_b': nrm(ks[6], (L, MLA_Q_RANK, MLA_HEADS * MLA_QK_DIM), MLA_Q_RANK ** -0.5),
        'g_kv_a': gain(ks[7], (L, MLA_KV_RANK)),
        'w_kv_b': nrm(ks[8], (L, MLA_KV_RANK, MLA_HEADS * (MLA_NOPE_DIM + MLA_V_DIM)), MLA_KV_RANK ** -0.5),
        'w_fox_out': nrm(ks[9], (L, FOX_WIDTH, D_MODEL), FOX_WIDTH ** -0.5),
        'w_mla_out': nrm(ks[10], (L, MLA_WIDTH, D_MODEL), MLA_WIDTH ** -0.5),
        'b_merge': nrm(ks[11], (L, N_BRANCHES, D_MODEL), 0.1),
        'w_o': nrm(ks[12], (L, D_MODEL, D_MODEL), D_MODEL ** -0.5),
        'g_ffn_norm': gain(ks[13], (L, D_MODEL)),
        'w_router': nrm(ks[14], (L, D_MODEL, N_EXPERTS), D_MODEL ** -0.5),
        'b_router': nrm(ks[15], (L, N_EXPERTS), 0.01),
        'w_gu': nrm(ks[16], (L, N_EXPERTS, D_MODEL, 2 * EXPERT_FF), D_MODEL ** -0.5),
        'b_gu': nrm(ks[17], (L, N_EXPERTS, 2 * EXPERT_FF), 0.01),
        'w_down': nrm(ks[18], (L, N_EXPERTS, EXPERT_FF, D_MODEL), EXPERT_FF ** -0.5),
        'b_down': nrm(ks[19], (L, N_EXPERTS, D_MODEL), 0.01),
        'g_final': gain(ks[20], (D_MODEL,)),
    }

def reference(x, positions, g_attn_norm, w_in, b_fgate, g_q_a, w_q_b, g_kv_a, w_kv_b, w_fox_out, w_mla_out, b_merge, w_o, g_ffn_norm, w_router, b_router, w_gu, b_gu, w_down, b_down, g_final):
    for l in range(DEPTH):
        h = rms_norm(x, g_attn_norm[l])
        x = x + token_mixer(h, positions, w_in[l], b_fgate[l], g_q_a[l], w_q_b[l], g_kv_a[l], w_kv_b[l], w_fox_out[l], w_mla_out[l], b_merge[l], w_o[l])
        h = rms_norm(x, g_ffn_norm[l])
        x = x + moe_ffn(h, w_router[l], b_router[l], w_gu[l], b_gu[l], w_down[l], b_down[l])
    return rms_norm(x, g_final)


_drawn_inputs = setup_inputs


def setup_inputs(seed=0):
    import zlib

    import numpy as np

    out = dict(_drawn_inputs(seed))
    spreads = {}
    factors = {'b_gu': 8.0, 'b_down': 8.0}
    for name, (base, spread) in spreads.items():
        noise = np.random.default_rng([zlib.crc32(name.encode()), seed]).standard_normal(out[name].shape)
        drawn = base * np.exp(spread * noise) if base else spread * noise
        out[name] = __import__('jax').numpy.asarray(drawn.astype(out[name].dtype))
    for name, factor in factors.items():
        out[name] = (out[name] * factor).astype(out[name].dtype)
    return out
```

```python
from contextlib import ExitStack

import numpy as np

import concourse.bass as bass
from concourse import mybir

F32 = mybir.dt.float32
I32 = mybir.dt.int32
U32 = mybir.dt.uint32
ALU = mybir.AluOpType
ACT = mybir.ActivationFunctionType
AX_X = mybir.AxisListType.X

P = 128
D = 1024
SEQ = 256
TT = SEQ // P
KT = D // P
HEADS = 8
HD = 64
FOX = HEADS * HD
ROPE = 32
HALF = ROPE // 2
QK = HD + ROPE
Q_RANK = 256
KV_RANK = 128
NE = 32
TOPK = 4
FF = 1024
LIMIT = 7.0
ALPHA = 1.702
EPS = 1e-6
THETA = 10000.0
MASKED = -1e30
COL_SMALL = 3 * FOX
N_SMALL = HEADS + Q_RANK + KV_RANK + ROPE
COL_GATE = COL_SMALL + N_SMALL

SLOT = 4096
RING = 8
PRE = 13
PER_E = 6
UNROLL = 4
FEW = 64

TWO_PI = [6.28125, 0.001934051513671875, 1.2509822845458984e-06, 3.1886e-09]
TWO_PI[3] = 2.0 * float(np.pi) - sum(TWO_PI[:3])
MAGIC = 12582912.0

USES = ([("vecT", 7)] + [(f"xT{i}", i) for i in range(4)] + [("small0", 4), ("small1", 5)]
        + [(f"qk{i}", 6 + i % 2) for i in range(8)] + [("v0", 0), ("v1", 1)]
        + [("cT", 2), ("qlT", 3), ("ckT", 4), ("kpT", 5)]
        + [("qb0", 0), ("qc0", 1), ("qb1", 2), ("qc1", 3)]
        + [(f"kn{i}", 4 + i) for i in range(4)] + [("vm0", 4), ("vm1", 5)]
        + [(f"qmT{i}", 6 + i % 2) for i in range(4)])
for _i in range(2 * HEADS + 1):
    if _i < 2 * HEADS:
        USES += [(f"sc{_i}", _i % 2), (f"gate{_i}", 2 + _i % 2)]
    if _i:
        USES += [(f"pT{_i - 1}", 4 + (_i - 1) % 2), (f"pv{_i - 1}", 6 + (_i - 1) % 2)]
USES += ([(f"fo{i}", i) for i in range(4)] + [(f"mo{i}", 4 + i) for i in range(4)]
         + [(f"o{i}", i) for i in range(4)] + [(f"hT{i}", 4 + i) for i in range(4)]
         + [("rl0", 0), ("rl1", 1), ("pos", 2), ("wT", 3), ("bgT", 4)])
BANK, NTH = {}, {}
_n = [0] * 8
for _name, _b in USES:
    BANK[_name], NTH[_name] = _b, _n[_b]
    _n[_b] += 1
BANK_USES = list(_n)
CHUNK_END = ["small1", "vm1", "qk3", "qk7", "v1", "gate3", "gate7", "gate11", "gate15", "fo3", "mo3",
             "o3", "o3"]
CONSTS = 50
CONSTS_PE = 16
OWN_PER_E = 4
C_SMALL, C_QKV, C_Q, C_K, C_V, C_G, C_FO, C_MO, C_O = 0, 1, 2, 3, 4, 5, 9, 10, 11


def build(nc, x_in, pos_in, g_attn, w_in, b_fgate, g_q_a, w_q_b, g_kv_a, w_kv_b, w_fox_out, w_mla_out,
          b_merge, w_o, g_ffn, w_router, b_router, w_gu, b_gu, w_down, b_down, g_final, out):
    ctx = ExitStack()

    def sb(name, shape, dt=F32):
        return ctx.enter_context(nc.sbuf_tensor(name, shape, dt))

    def sem(name):
        return ctx.enter_context(nc.semaphore(name))

    ring = sb("ring", [P, RING, SLOT])
    arena = sb("arena", [P, 16384])
    x = sb("x", [P, TT, D])
    hn = sb("hn", [P, TT, D])
    ident = sb("ident", [P, P])
    upto = sb("upto", [P, P])
    below = sb("below", [P, P])
    ones = sb("ones", [P, P])
    mask = sb("mask", [P, 2, 3 * P])
    iota = sb("iota", [P, SEQ])
    sm = sb("sm", [P, 2, 3 * P])
    pT = sb("pT", [P, 2, 3 * P])
    tiny = sb("tiny", [P, 64])
    vecT = sb("vecT", [P, 27])
    bf = sb("bf", [P, HEADS])
    brt = sb("brt", [P, NE])
    pos_i = sb("pos_i", [P, TT], I32)
    logf = sb("logf", [P, TT, HEADS])
    cT = hn[0:HD + HEADS, 0, 768:1024]
    negI = sb("negI", [HD + HEADS, HEADS])
    posI = sb("posI", [HD + HEADS, HEADS])
    fgt = hn[:, 1, 768:768 + 6 * TT * HEADS].rearrange("p (i c) -> p i c", i=6)
    topi = sb("topi", [P, TT, 8], U32)
    most = sb("most", [1, 1], I32)
    posm = sb("posm", [P, TT, NE + 1])
    wt = sb("wt", [P, TT, NE + 1])

    def part(off, shape):
        n = int(np.prod(shape))
        v = arena[:, off:off + n]
        if len(shape) == 2:
            return v.rearrange("p (a b) -> p a b", a=shape[0])
        if len(shape) == 3:
            return v.rearrange("p (a b c) -> p a b c", a=shape[0], b=shape[1])
        return v

    hT = part(0, [KT, SEQ])
    gates = part(2048, [2 * KT, SEQ])
    qf = part(6144, [4, SEQ])
    kf = part(7168, [4, SEQ])
    vf = part(8192, [TT, FOX])
    qm = part(9216, [HEADS, SEQ])
    km = part(11264, [HEADS, SEQ])
    vm = part(13312, [TT, FOX])
    yf = part(14336, [4, SEQ])
    ym = part(15360, [4, SEQ])
    ropetmp = part(14336, [4, TT, HEADS * HALF])
    qlT = part(15360, [2, SEQ])
    ckT = part(15872, [SEQ])
    trig = part(16128, [4, TT * 2 * HALF])
    qtok = hn[:, :, 0:768]
    spj = part(9216, [TT, N_SMALL])
    kcat = part(9216 + TT * N_SMALL, [TT, QK])
    vec = part(9216 + TT * N_SMALL + TT * QK, [P])
    gbig = part(13312, [D])
    su = part(0, [TT, SEQ])
    sw = part(512, [TT, SEQ])
    pw = part(1024, [TT, SEQ])
    wtT = part(1536, [SEQ])[0:NE, :]
    xg = part(2048, [KT, SEQ])
    av = part(4096, [FF // P, SEQ])
    ysb = part(6144, [TT, D])
    gt = part(8192, [4, SEQ])
    bg_raw = part(9216, [2 * FF])
    bd_raw = part(11264, [D])
    wr = part(12800, [KT, NE])
    bgT = part(12288, [NE, 2 * FF // P])
    sg = part(13312, [4, SEQ])
    ut = part(14336, [4, SEQ])
    gl = part(15360, [4, SEQ])
    gfin = part(9216, [D])

    psum = ctx.enter_context(nc.psum_tensor("psum", [P, 8 * 512], F32))
    bank = [psum[:, 512 * b:512 * b + 512] for b in range(8)]

    def nmax(b, t):
        return tiny[:, 40 + 2 * b + t:41 + 2 * b + t]

    def rsum(b, t):
        return tiny[:, 32 + 2 * b + t:33 + 2 * b + t]

    def ntop(t):
        return tiny[:, 52 + t:53 + t]

    def tsum(t):
        return tiny[:, 44 + t:45 + t]

    def fz(i):
        return fgt[:, i, :]

    square_scratch = part(14336, [512])
    lg = part(14336, [TT, NE])
    top8 = part(14400, [TT, 8])
    topf = part(14416, [TT, 8])
    topw = part(14432, [TT, TOPK])
    chosen = part(14448, [TT, NE])
    hot = part(14528, [TT, TOPK, NE])

    mode_few = dict(
        sl=FEW, pieces=1, tiles=1, group=2, credit=2,
        gu_view=lambda ch: bank[ch % 2][:, 0:256].rearrange("p (j s) -> p j s", j=4),
        gather_view=bank[0].rearrange("p (k s) -> p k s", k=KT),
        tr_view=bank[0][:, 0:SEQ].rearrange("p (a s) -> p a s", a=1),
        rows=lambda u: (FEW * (u % 2), FEW * (u % 2) + FEW))
    mode_all = dict(
        sl=SEQ, pieces=2, tiles=2, group=1, credit=1,
        gu_view=lambda ch: psum[:, 0:1024].rearrange("p (j s) -> p j s", j=4),
        gather_view=psum[:, 0:1024].rearrange("p (k s) -> p k s", k=4),
        tr_view=bank[0].rearrange("p (a s) -> p a s", a=2),
        rows=lambda u: (0, P))

    kv_here = sem("kv_here")
    x_here = [sem(f"x_here{t}") for t in range(TT)]
    vec_here = sem("vec_here")
    late_here = sem("late_here")
    bias_here = sem("bias_here")
    gfin_here = sem("gfin_here")
    consts = sem("consts")
    slot_in = [sem(f"slot_in{s}") for s in range(RING)]
    written = [sem(f"bank_written{b}") for b in range(8)]
    read = [sem(f"bank_read{b}") for b in range(8)]
    dve_step = sem("dve_step")
    act_step = sem("act_step")
    sq_x = sem("sq_x")
    ms_x = sem("ms_x")
    rt_x = sem("rt_x")
    xn_ready = sem("xn_ready")
    f_abs = sem("f_abs")
    f_exp = sem("f_exp")
    f_one = sem("f_one")
    f_ln = sem("f_ln")
    logf_ready = sem("logf_ready")
    lat_sq = sem("lat_sq")
    lat_ms = sem("lat_ms")
    lat_rt = sem("lat_rt")
    lat_ready = sem("lat_ready")
    kpe_ready = sem("kpe_ready")
    angle_ready = sem("angle_ready")
    trig_ready = sem("trig_ready")
    q_roped = sem("q_roped")
    qm_ready = sem("qm_ready")
    max_ready = sem("max_ready")
    exp_ready = sem("exp_ready")
    prob_ready = sem("prob_ready")
    merged = sem("merged")
    gates_sig = sem("gates_sig")
    top_ready = sem("top_ready")
    top_exp = sem("top_exp")
    sel_ready = sem("sel_ready")
    wt_ready = sem("wt_ready")
    most_ready = sem("most_ready")
    s_ready = sem("s_ready")
    gu_free = sem("gu_free")
    chunk_done = sem("chunk_done")
    g_ready = sem("g_ready")
    sig_ready = sem("sig_ready")
    act_ready = sem("act_ready")
    tr_done = sem("tr_done")
    p_ready = sem("p_ready")
    gather_done = sem("gather_done")
    xg_ready = sem("xg_ready")
    y_part = sem("y_part")
    y_ready = sem("y_ready")
    scattered = sem("scattered")
    x_final = sem("x_final")
    out_ready = sem("out_ready")
    stored = sem("stored")

    def chunk_here(eng, c):
        eng.wait_ge(slot_in[c % RING], 16 * (c // RING + 1))

    def expert_chunk_here(eng, it, k):
        c = PRE + k
        eng.wait_ge(slot_in[c % RING], 16 * (c // RING + 1) + it * (16 * UNROLL * PER_E // RING))

    def take_bank(eng, name):
        if NTH[name]:
            eng.wait_ge(read[BANK[name]], NTH[name])

    def bank_full(eng, name):
        eng.wait_ge(written[BANK[name]], NTH[name] + 1)

    def was_read(eng, name):
        eng.wait_ge(read[BANK[name]], NTH[name] + 1)

    def chunk(c):
        return ring[:, c % RING, :]

    wsm = chunk(C_SMALL)[:, 0:KT * N_SMALL].rearrange("p (k n) -> p k n", k=KT)
    wqb = chunk(C_QKV)[:, 0:2 * 768].rearrange("p (k n) -> p k n", k=2)
    wkvb = chunk(C_QKV)[:, 1536:1536 + 1024].rearrange("p (h n) -> p h n", h=HEADS)

    def cols(c):
        return chunk(c).rearrange("p (k n) -> p k n", k=KT)

    def rows(c):
        return chunk(c).rearrange("p (k n) -> p k n", k=4)

    w_in_v = w_in[0].rearrange("(k p) n -> p k n", p=P)
    w_gu_v = w_gu[0].rearrange("e (k p) f -> p e k f", p=P)
    w_dn_v = w_down[0].rearrange("e (k p) n -> p e k n", p=P)

    block = ctx.enter_context(nc.Block())

    @block.sync
    def _(sp):
        x_v = x_in[0].rearrange("(t p) d -> p t d", p=P)
        for t in range(TT):
            sp.dma_start(x[:, t, :], x_v[:, t, :]).then_inc(x_here[t], 16)

        def load(c, pairs):
            for dst, src in pairs:
                sp.dma_start(dst, src).then_inc(slot_in[c % RING], 16)

        qkv = w_q_b[0].rearrange("(k p) n -> p k n", p=P)
        pre = [[(wsm, w_in_v[:, :, COL_SMALL:COL_GATE])], [(wqb, qkv)]]
        pre += [[(cols(2 + i), w_in_v[:, :, 512 * i:512 * i + 512])] for i in range(3)]
        pre += [[(cols(C_G + i), w_in_v[:, :, COL_GATE + 512 * i:COL_GATE + 512 * i + 512])] for i in range(4)]
        pre += [[(rows(C_FO), w_fox_out[0].rearrange("(k p) n -> p k n", p=P))],
                [(rows(C_MO), w_mla_out[0].rearrange("(k p) n -> p k n", p=P))]]
        wo_v = w_o[0].rearrange("(k p) n -> p k n", p=P)
        pre += [[(rows(C_O + i), wo_v[:, 4 * i:4 * i + 4, :])] for i in range(2)]
        for c in range(PRE):
            if c >= RING:
                bank_full(sp, CHUNK_END[c - RING])
            load(c, pre[c])
            if c == 1:
                sp.dma_start(wkvb, w_kv_b[0].rearrange("p (h n) -> p h n", h=HEADS)).then_inc(kv_here, 16)

        def load_expert(n, it=None):
            e, k = n // PER_E, n % PER_E
            s = (PRE + n) % RING
            ee = e if it is None else it * UNROLL + e
            if k < 4:
                c0 = (k % 2) * FF + (k // 2) * 512
                src = w_gu_v[:, bass.ds(ee, 1), :, c0:c0 + 512].rearrange("p a k f -> p (a k) f")
                dst = cols(s)
            else:
                src = w_dn_v[:, bass.ds(ee, 1), 4 * (k - 4):4 * (k - 4) + 4, :].rearrange("p a k n -> p (a k) n")
                dst = rows(s)
            sp.dma_start(dst, src).then_inc(slot_in[s], 16)

        for n in range(RING):
            bank_full(sp, CHUNK_END[PRE + n - RING])
            load_expert(n)
        body = UNROLL * PER_E
        turns = (NE * PER_E - RING) // body
        with sp.Fori(0, turns) as it:
            for n in range(RING, RING + body):
                sp.wait_ge(chunk_done, it * body + (n - RING + 1))
                load_expert(n, it)
        for n in range(RING + turns * body, NE * PER_E):
            sp.wait_ge(chunk_done, n - RING + 1)
            load_expert(n)

        out_v = out[0].rearrange("(t p) d -> p t d", p=P)
        for t in range(TT):
            sp.wait_ge(out_ready, t + 1)
            sp.dma_start(out_v[:, t, :], hn[:, t, :]).then_inc(stored, 16)
        sp.wait_ge(stored, 16 * TT)

    @block.gpsimd
    def _(pool):
        k = 0

        def step(ins):
            nonlocal k
            k += 1
            ins.then_inc(consts, 1)
            pool.wait_ge(consts, k)

        step(pool.memset(ident[:, :], 0.0))
        step(pool.affine_select(out=ident[:, :], in_=ident[:, :], compare_op=ALU.not_equal, fill=1.0,
                                base=0, pattern=[[-1, P]], channel_multiplier=1))
        step(pool.memset(ones[:, :], 1.0))
        step(pool.affine_select(out=upto[:, :], in_=ones[:, :], compare_op=ALU.is_ge, fill=0.0,
                                base=0, pattern=[[1, P]], channel_multiplier=-1))
        step(pool.affine_select(out=below[:, :], in_=ones[:, :], compare_op=ALU.is_gt, fill=0.0,
                                base=0, pattern=[[1, P]], channel_multiplier=-1))
        step(pool.memset(mask[:, :, :], 0.0))
        for b in (0, 2):
            step(pool.affine_select(out=mask[:, 0, b * P:(b + 1) * P], in_=mask[:, 0, b * P:(b + 1) * P],
                                    compare_op=ALU.is_ge, fill=MASKED, base=0, pattern=[[-1, P]],
                                    channel_multiplier=1))
            step(pool.memset(mask[0:64, 1, b * P + 64:(b + 1) * P], MASKED))
        step(pool.memset(kcat[:, :, :], 0.0))
        for lo in (0, HD):
            step(pool.tensor_scalar(negI[lo:lo + HEADS, :], ident[lo:lo + HEADS, lo:lo + HEADS], -8.0, 0.0,
                                    ALU.mult, ALU.add))
            step(pool.tensor_scalar(posI[lo:lo + HEADS, :], ident[lo:lo + HEADS, lo:lo + HEADS], 8.0, 0.0,
                                    ALU.mult, ALU.add))
        step(pool.iota(iota[:, :], [[1, SEQ]], base=0, channel_multiplier=0,
                       allow_small_or_imprecise_dtypes=True))
        for t in range(TT):
            for i in range(HALF):
                step(pool.memset(trig[:, 0, t * 2 * HALF + i:t * 2 * HALF + i + 1],
                                 float(np.float32(THETA ** (-i / HALF)))))
        step(pool.memset(posm[:, :, NE:NE + 1], -1.0))
        step(pool.memset(wt[:, :, NE:NE + 1], 0.0))
        assert k == CONSTS

    @block.scalar
    def _(act):
        act.dma_start(vec[0:8, :], g_attn[0].rearrange("(k p) -> k p", p=P)).then_inc(vec_here, 16)
        act.dma_start(vec[8:10, :], g_q_a[0].rearrange("(k p) -> k p", p=P)).then_inc(vec_here, 16)
        act.dma_start(vec[10:11, :], g_kv_a[0:1, :]).then_inc(vec_here, 16)
        act.dma_start(vec[11:27, :], b_merge[0].rearrange("b (k p) -> (b k) p", p=P)).then_inc(vec_here, 16)
        act.dma_start(bf[:, :], b_fgate[0:1, :].to_broadcast([P, HEADS])).then_inc(vec_here, 16)
        for t in range(TT):
            act.dma_start(pos_i[:, t:t + 1], pos_in[0, t * P:t * P + P].rearrange("(p a) -> p a", a=1))\
               .then_inc(vec_here, 16)

        for t in range(TT):
            act.wait_ge(x_here[t], 16)
            nc.scalar.activation(hn[:, t, :], x[:, t, :], ACT.Square, accum_out=tiny[:, t:t + 1]).then_inc(sq_x, 1)
        act.wait_ge(ms_x, 1)
        nc.scalar.activation(tiny[:, 4:6], tiny[:, 2:4], ACT.Sqrt).then_inc(rt_x, 1)

        def evac(name, dst, src, scale=None):
            bank_full(act, name)
            nc.scalar.activation(dst, src, ACT.Copy, **({} if scale is None else {"scale": scale}))\
              .then_inc(read[BANK[name]], 1)

        was_read(act, "vecT")
        for i in (2, 3):
            bank_full(act, f"xT{i}")
            nc.scalar.activation(hT[:, 2 * i, :], bank[i][:, 0:SEQ], ACT.Copy,
                                 scale=vecT[:, 2 * i:2 * i + 1]).then_inc(act_step, 1)
            nc.scalar.activation(hT[:, 2 * i + 1, :], bank[i][:, SEQ:512], ACT.Copy,
                                 scale=vecT[:, 2 * i + 1:2 * i + 2]).then_inc(read[i], 1)
        was_read(act, "small1")
        for t in range(TT):
            nc.scalar.activation(square_scratch[:, 0:Q_RANK], spj[:, t, 8:8 + Q_RANK], ACT.Square,
                                 accum_out=tiny[:, 8 + t:9 + t]).then_inc(lat_sq, 1)
            nc.scalar.activation(square_scratch[:, Q_RANK:Q_RANK + KV_RANK], spj[:, t, 264:264 + KV_RANK], ACT.Square,
                                 accum_out=tiny[:, 10 + t:11 + t]).then_inc(lat_sq, 1)
            act.wait_ge(lat_sq, 2 * t + 2)
        act.wait_ge(lat_ms, 1)
        nc.scalar.activation(tiny[:, 16:20], tiny[:, 12:16], ACT.Sqrt).then_inc(lat_rt, 1)
        for i in range(4):
            evac(f"qk{i}", qf[:, i, :], bank[6 + i % 2][:, 0:SEQ])
        act.wait_ge(f_abs, 1)
        nc.scalar.activation(fz(1), fz(0), ACT.Exp, scale=-1.0).then_inc(f_exp, 1)
        act.wait_ge(f_one, 1)
        nc.scalar.activation(fz(3), fz(2), ACT.Ln).then_inc(f_ln, 1)
        for i in range(4, 8):
            evac(f"qk{i}", kf[:, i - 4, :], bank[6 + i % 2][:, 0:SEQ])
        act.wait_ge(angle_ready, 1)
        nc.scalar.activation(trig[:, 2, :], trig[:, 0, :], ACT.Sin).then_inc(trig_ready, 1)
        for t in range(TT):
            evac(f"v{t}", vf[:, t, :], bank[t][:, :])
        bank_full(act, "cT")
        nc.scalar.activation(cT[0:HEADS, :], bank[2][0:HEADS, 0:SEQ], ACT.Copy).then_inc(act_step, 1)
        nc.scalar.activation(cT[HD:HD + HEADS, :], bank[2][HD:HD + HEADS, 0:SEQ], ACT.Copy).then_inc(read[2], 1)
        for t in range(TT):
            evac(f"qb{t}", qtok[:, t, 0:512], bank[2 * t][:, :])
            evac(f"qc{t}", qtok[:, t, 512:768], bank[2 * t + 1][:, 0:256])
        for i in range(4):
            evac(f"kn{i}", km[0:HD, 2 * i:2 * i + 2, :],
                 bank[4 + i][0:HD, :].rearrange("p (h s) -> p h s", h=2))
        for t in range(TT):
            evac(f"vm{t}", vm[:, t, :], bank[4 + t][:, :])

        for i in range(2 * HEADS):
            b = i % 2
            act.wait_ge(max_ready, i + 1)
            nc.scalar.activation(sm[:, b, 0:P], sm[:, b, 0:P], ACT.Exp, bias=nmax(b, 0),
                                 accum_out=rsum(b, 0)).then_inc(exp_ready, 1)
            nc.scalar.activation(sm[:, b, P:3 * P], sm[:, b, P:3 * P], ACT.Exp, bias=nmax(b, 1),
                                 accum_out=rsum(b, 1)).then_inc(exp_ready, 1)
            bank_full(act, f"gate{i}")
            nc.scalar.activation(gates[:, i, :], bank[2 + b][:, 0:SEQ], ACT.Identity,
                                 bias=vecT[:, 11 + i:12 + i]).then_inc(read[2 + b], 1)
        bank_full(act, f"pv{2 * HEADS - 1}")
        act.dma_start(gbig, g_ffn[0:1, :].to_broadcast([P, D])).then_inc(late_here, 16)
        act.dma_start(brt[:, :], b_router[0:1, :].to_broadcast([P, NE])).then_inc(late_here, 16)
        act.dma_start(wr, w_router[0].rearrange("(k p) n -> p k n", p=P)).then_inc(late_here, 16)
        act.dma_start(bg_raw[0:NE, :], b_gu[0]).then_inc(bias_here, 16)
        act.dma_start(bd_raw[0:NE, :], b_down[0]).then_inc(bias_here, 16)
        was_read(act, f"gate{2 * HEADS - 1}")
        for i in (0, 2, 1, 3):
            nc.scalar.activation(gates[:, 4 * i:4 * i + 4, :], gates[:, 4 * i:4 * i + 4, :], ACT.Sigmoid)\
              .then_inc(gates_sig, 1)

        for t in range(TT):
            was_read(act, f"o{2 * t}")
            was_read(act, f"o{2 * t + 1}")
            nc.scalar.activation(hn[:, t, :], x[:, t, :], ACT.Square, accum_out=tiny[:, t:t + 1]).then_inc(sq_x, 1)
        act.wait_ge(ms_x, 2)
        nc.scalar.activation(tiny[:, 4:6], tiny[:, 2:4], ACT.Sqrt).then_inc(rt_x, 1)
        for i in (1, 3):
            evac(f"hT{i}", hT[:, 2 * i:2 * i + 2, :], bank[4 + i][:, :].rearrange("p (k s) -> p k s", k=2))
        for t in range(TT):
            act.wait_ge(top_ready, t + 1)
            nc.scalar.activation(topw[:, t, :], top8[:, t, 0:TOPK], ACT.Exp, bias=ntop(t),
                                 accum_out=tsum(t)).then_inc(top_exp, 1)
        bank_full(act, "bgT")
        nc.scalar.activation(bgT.rearrange("p e j -> p j e"),
                             bank[4][:, :].rearrange("p (j e) -> p j e", e=NE), ACT.Copy).then_inc(read[4], 1)

        def experts(m):
            sl, pieces, tiles, group = m["sl"], m["pieces"], m["tiles"], m["group"]

            def take_gather(e):
                for i in range(pieces):
                    k = KT // pieces
                    act.wait_ge(gather_done, e * pieces + (i + 1))
                    nc.scalar.activation(xg[:, i * k:i * k + k, 0:sl], m["gather_view"],
                                         ACT.Copy).then_inc(xg_ready, 1)

            act.sem_inc(y_ready, 1)
            take_gather(0)
            with act.Fori(0, NE // UNROLL) as it:
                for u in range(UNROLL):
                    e = it * UNROLL + u
                    for half in range(2):
                        act.wait_ge(g_ready, e * 2 + (half + 1))
                        nc.scalar.activation(sg[:, :, 0:sl], gt[:, :, 0:sl], ACT.Sigmoid,
                                             scale=ALPHA).then_inc(sig_ready, 1)
                    if u % group == group - 1:
                        n = it * (UNROLL // group) + u // group
                        act.wait_ge(tr_done, n + 1)
                        nc.scalar.activation(pw[:, 0:tiles, :], m["tr_view"], ACT.Copy).then_inc(p_ready, 1)
                    take_gather(e + 1)
                    for st in range(tiles):
                        lo, hi = m["rows"](u)
                        if st < tiles - 1:
                            act.wait_ge(y_part, e + 1)
                        else:
                            act.wait_ge(chunk_done, e * PER_E + PER_E)
                        for half in range(2):
                            nc.scalar.activation(ysb[lo:hi, st, half * 512:half * 512 + 512],
                                                 bank[2 + half][lo:hi, :], ACT.Copy).then_inc(y_ready, 1)

        was_read(act, "bgT")
        act.dma_start(gfin, g_final.rearrange("(a d) -> a d", a=1).to_broadcast([P, D])).then_inc(gfin_here, 16)
        act.wait_ge(most_ready, 1)
        n_most = act.value_load(most[0:1, 0:1], min_val=0, max_val=SEQ)
        with act.If(n_most <= FEW):
            experts(mode_few)
        with act.Else():
            experts(mode_all)

        for t in range(TT):
            act.wait_ge(x_final, t + 1)
            nc.scalar.activation(hn[:, t, :], x[:, t, :], ACT.Square, accum_out=tiny[:, t:t + 1]).then_inc(sq_x, 1)
            act.wait_ge(ms_x, 3 + t)
            nc.scalar.activation(tiny[:, 4 + t:5 + t], tiny[:, 2 + t:3 + t], ACT.Sqrt).then_inc(rt_x, 1)

    @block.vector
    def _(dve):
        n = [0]

        def step(ins):
            n[0] += 1
            ins.then_inc(dve_step, 1)
            dve.wait_ge(dve_step, n[0])

        dve.wait_ge(sq_x, 2)
        nc.vector.tensor_scalar(tiny[:, 2:4], tiny[:, 0:2], 1.0 / D, EPS, ALU.mult, ALU.add).then_inc(ms_x, 1)
        dve.wait_ge(rt_x, 1)
        step(nc.vector.reciprocal(tiny[:, 6:8], tiny[:, 4:6]))
        for t in range(TT):
            nc.vector.tensor_scalar(hn[:, t, :], x[:, t, :], tiny[:, 6 + t:7 + t], None, ALU.mult)\
              .then_inc(xn_ready, 1)
        bank_full(dve, "vecT")
        nc.vector.tensor_copy(vecT[:, :], bank[7][:, 0:27]).then_inc(read[7], 1)
        was_read(dve, "vecT")
        for i in (0, 1):
            bank_full(dve, f"xT{i}")
            nc.vector.tensor_scalar(hT[:, 2 * i, :], bank[i][:, 0:SEQ], vecT[:, 2 * i:2 * i + 1], None,
                                    ALU.mult).then_inc(dve_step, 1)
            nc.vector.tensor_scalar(hT[:, 2 * i + 1, :], bank[i][:, SEQ:512], vecT[:, 2 * i + 1:2 * i + 2], None,
                                    ALU.mult).then_inc(read[i], 1)
            n[0] += 1

        dve.wait_ge(vec_here, 16 * 7)
        dve.wait_ge(consts, CONSTS)
        step(nc.vector.tensor_copy(tiny[:, 20:22], pos_i[:, :]))
        ang = trig[:, 0, :].rearrange("p (t f) -> p t f", t=TT)
        trn = trig[:, 1, :].rearrange("p (t f) -> p t f", t=TT)
        for t in range(TT):
            step(nc.vector.tensor_scalar(ang[:, t, 0:HALF], ang[:, t, 0:HALF], tiny[:, 20 + t:21 + t], None,
                                         ALU.mult))
        step(nc.vector.tensor_copy(ang[:, :, HALF:2 * HALF], ang[:, :, 0:HALF]))
        step(nc.vector.tensor_scalar(trn[:, :, 0:HALF], ang[:, :, 0:HALF], 1.0 / (2.0 * float(np.pi)), None,
                                     ALU.mult))
        step(nc.vector.tensor_scalar(trn[:, :, HALF:2 * HALF], ang[:, :, HALF:2 * HALF],
                                     1.0 / (2.0 * float(np.pi)), 0.25, ALU.mult, ALU.add))
        step(nc.vector.tensor_scalar(trn, trn, MAGIC, None, ALU.add))
        step(nc.vector.tensor_scalar(trn, trn, -MAGIC, None, ALU.add))
        for c in TWO_PI:
            step(nc.vector.scalar_tensor_tensor(out=ang, in0=trn, scalar=-c, in1=ang, op0=ALU.mult, op1=ALU.add))
        step(nc.vector.tensor_scalar(ang[:, :, HALF:2 * HALF], ang[:, :, HALF:2 * HALF],
                                     float(np.pi) / 2.0, None, ALU.add))
        pi = float(np.nextafter(np.float32(np.pi), np.float32(0)))
        nc.vector.tensor_scalar(ang, ang, pi, -pi, ALU.min, ALU.max).then_inc(angle_ready, 1)

        for t in range(TT):
            bank_full(dve, f"small{t}")
            nc.vector.tensor_copy(spj[:, t, :], bank[4 + t][:, 0:N_SMALL]).then_inc(read[4 + t], 1)
        was_read(dve, "small0")
        was_read(dve, "small1")
        for t in range(TT):
            step(nc.vector.tensor_tensor(logf[:, t, :], spj[:, t, 0:HEADS], bf[:, :], ALU.add))
        lf = logf[:, :, :].rearrange("p t h -> p (t h)")
        nc.vector.scalar_tensor_tensor(out=fz(0), in0=lf, scalar=-1.0, in1=lf, op0=ALU.mult,
                                       op1=ALU.max).then_inc(f_abs, 1)
        dve.wait_ge(lat_sq, 4)
        step(nc.vector.tensor_scalar(tiny[:, 12:14], tiny[:, 8:10], 1.0 / Q_RANK, EPS, ALU.mult, ALU.add))
        nc.vector.tensor_scalar(tiny[:, 14:16], tiny[:, 10:12], 1.0 / KV_RANK, EPS, ALU.mult, ALU.add)\
          .then_inc(lat_ms, 1)
        dve.wait_ge(lat_rt, 1)
        step(nc.vector.reciprocal(tiny[:, 24:28], tiny[:, 16:20]))
        for t in range(TT):
            nc.vector.tensor_scalar(spj[:, t, 8:264], spj[:, t, 8:264], tiny[:, 24 + t:25 + t], None,
                                    ALU.mult).then_inc(lat_ready, 1)
            nc.vector.tensor_scalar(spj[:, t, 264:392], spj[:, t, 264:392], tiny[:, 26 + t:27 + t], None,
                                    ALU.mult).then_inc(lat_ready, 1)
        dve.wait_ge(f_exp, 1)
        nc.vector.tensor_scalar(fz(2), fz(1), 1.0, None, ALU.add).then_inc(f_one, 1)
        dve.wait_ge(f_one, 1)
        step(nc.vector.tensor_scalar(fz(4), fz(2), -1.0, None, ALU.add))
        step(nc.vector.tensor_tensor(fz(4), fz(1), fz(4), ALU.subtract))
        step(nc.vector.reciprocal(fz(5), fz(2)))
        step(nc.vector.tensor_tensor(fz(4), fz(4), fz(5), ALU.mult))
        dve.wait_ge(f_ln, 1)
        step(nc.vector.tensor_tensor(fz(4), fz(4), fz(3), ALU.add))
        nc.vector.scalar_tensor_tensor(out=lf, in0=lf, scalar=0.0, in1=fz(4), op0=ALU.min,
                                       op1=ALU.subtract).then_inc(logf_ready, 1)

        dve.wait_ge(trig_ready, 1)
        tr = trig[:, 2, :].rearrange("p (t f) -> p t f", t=TT)
        sin, cos = tr[:, :, 0:HALF], tr[:, :, HALF:2 * HALF]
        k1, k2 = spj[:, :, 392:392 + HALF], spj[:, :, 392 + HALF:392 + ROPE]
        m = [ropetmp[:, i, :, 0:HALF] for i in range(4)]
        nc.vector.tensor_tensor(m[0], k1, cos, ALU.mult).then_inc(dve_step, 1)
        nc.vector.tensor_tensor(m[1], k2, sin, ALU.mult).then_inc(dve_step, 1)
        nc.vector.tensor_tensor(m[2], k2, cos, ALU.mult).then_inc(dve_step, 1)
        n[0] += 3
        step(nc.vector.tensor_tensor(m[3], k1, sin, ALU.mult))
        step(nc.vector.tensor_tensor(kcat[:, :, HD:HD + HALF], m[0], m[1], ALU.subtract))
        nc.vector.tensor_tensor(kcat[:, :, HD + HALF:QK], m[2], m[3], ALU.add).then_inc(kpe_ready, 1)
        bank_full(dve, "qlT")
        step(nc.vector.tensor_scalar(qlT[:, 0, :], bank[3][:, 0:SEQ], vecT[:, 8:9], None, ALU.mult))
        nc.vector.tensor_scalar(qlT[:, 1, :], bank[3][:, SEQ:512], vecT[:, 9:10], None, ALU.mult)\
          .then_inc(read[3], 1)
        bank_full(dve, "ckT")
        nc.vector.tensor_scalar(ckT, bank[4][:, 0:SEQ], vecT[:, 10:11], None, ALU.mult).then_inc(read[4], 1)
        bank_full(dve, "kpT")
        nc.vector.tensor_copy(km[HD:QK, :, :], bank[5][HD:QK, None, 0:SEQ].to_broadcast([ROPE, HEADS, SEQ]))\
          .then_inc(read[5], 1)
        for t in range(TT):
            was_read(dve, f"qb{t}")
            was_read(dve, f"qc{t}")
        for t in range(TT):
            qh = qtok[:, t, :].rearrange("p (h c) -> p h c", h=HEADS)
            q1, q2 = qh[:, :, HD:HD + HALF], qh[:, :, HD + HALF:QK]
            ct = cos[:, t, None, :].to_broadcast([P, HEADS, HALF])
            st = sin[:, t, None, :].to_broadcast([P, HEADS, HALF])
            m = [ropetmp[:, i, t, :].rearrange("p (h c) -> p h c", h=HEADS) for i in range(4)]
            nc.vector.tensor_tensor(m[0], q1, ct, ALU.mult).then_inc(dve_step, 1)
            nc.vector.tensor_tensor(m[1], q2, st, ALU.mult).then_inc(dve_step, 1)
            nc.vector.tensor_tensor(m[2], q2, ct, ALU.mult).then_inc(dve_step, 1)
            n[0] += 3
            step(nc.vector.tensor_tensor(m[3], q1, st, ALU.mult))
            step(nc.vector.tensor_tensor(q1, m[0], m[1], ALU.subtract))
            nc.vector.tensor_tensor(q2, m[2], m[3], ALU.add).then_inc(q_roped, 1)

        def qm_copy(i):
            bank_full(dve, f"qmT{i}")
            nc.vector.tensor_copy(qm[0:QK, 2 * i:2 * i + 2, :],
                                  bank[6 + i % 2][0:QK, :].rearrange("p (h s) -> p h s", h=2))\
              .then_inc(read[6 + i % 2], 1)

        for i in range(4):
            qm_copy(i)

        def softmax_max(i):
            b = i % 2
            bank_full(dve, f"sc{i}")
            if i >= 2:
                dve.wait_ge(written[BANK[f"pT{i - 2}"]], NTH[f"pT{i - 2}"] + 1)
            nc.vector.scalar_tensor_tensor(out=sm[:, b, :], in0=bank[b][:, 0:3 * P],
                                           scalar=(HD if i < HEADS else QK) ** -0.5, in1=mask[:, i // HEADS, :],
                                           op0=ALU.mult, op1=ALU.add).then_inc(read[b], 1)
            was_read(dve, f"sc{i}")
            step(nc.vector.tensor_reduce(nmax(b, 0), sm[:, b, 0:P], AX_X, ALU.max, negate=True))
            nc.vector.tensor_reduce(nmax(b, 1), sm[:, b, P:3 * P], AX_X, ALU.max, negate=True).then_inc(max_ready, 1)

        def softmax_norm(i):
            b = i % 2
            dve.wait_ge(exp_ready, 2 * i + 2)
            step(nc.vector.reciprocal(tiny[:, 36 + 2 * b:38 + 2 * b], tiny[:, 32 + 2 * b:34 + 2 * b]))
            nc.vector.tensor_scalar(sm[:, b, 0:P], sm[:, b, 0:P], tiny[:, 36 + 2 * b:37 + 2 * b], None,
                                    ALU.mult).then_inc(prob_ready, 1)
            nc.vector.tensor_scalar(sm[:, b, P:3 * P], sm[:, b, P:3 * P], tiny[:, 37 + 2 * b:38 + 2 * b], None,
                                    ALU.mult).then_inc(prob_ready, 1)

        def probs_out(i):
            b = i % 2
            bank_full(dve, f"pT{i}")
            nc.vector.tensor_copy(pT[:, b, :], bank[4 + b][:, 0:3 * P]).then_inc(read[4 + b], 1)

        def head_out(i):
            b, h = i % 2, i % HEADS
            y = yf if i < HEADS else ym
            lo = HD * (h % 2)
            bank_full(dve, f"pv{i}")
            nc.vector.tensor_copy(y[lo:lo + HD, h // 2, :], bank[6 + b][lo:lo + HD, 0:SEQ]).then_inc(read[6 + b], 1)

        for i in range(2 * HEADS + 1):
            if i < 2 * HEADS:
                softmax_max(i)
            if i:
                probs_out(i - 1)
            if i < 2 * HEADS:
                softmax_norm(i)
            if i:
                head_out(i - 1)

        g4 = lambda a: gates[:, a:a + 2, :].rearrange("p k s -> p (k s)")
        for i in range(4):
            dve.wait_ge(gates_sig, 1 + (i >= 2) * 2)
            bank_full(dve, f"fo{i}")
            nc.vector.tensor_tensor(g4(2 * i), bank[i][:, :], g4(2 * i), ALU.mult).then_inc(read[i], 1)
        for i in range(4):
            dve.wait_ge(gates_sig, 4)
            bank_full(dve, f"mo{i}")
            nc.vector.tensor_tensor(g4(8 + 2 * i), bank[4 + i][:, :], g4(8 + 2 * i), ALU.mult).then_inc(read[4 + i], 1)
            was_read(dve, f"mo{i}")
            was_read(dve, f"fo{i}")
            nc.vector.tensor_tensor(hT[:, 2 * i:2 * i + 2, :].rearrange("p k s -> p (k s)"), g4(2 * i),
                                    g4(8 + 2 * i), ALU.add).then_inc(merged, 1)

        for i in range(4):
            t, c = i // 2, (i % 2) * 512
            bank_full(dve, f"o{i}")
            nc.vector.tensor_tensor(x[:, t, c:c + 512], bank[i][:, :], x[:, t, c:c + 512], ALU.add)\
              .then_inc(read[i], 1)
        dve.wait_ge(sq_x, 4)
        nc.vector.tensor_scalar(tiny[:, 2:4], tiny[:, 0:2], 1.0 / D, EPS, ALU.mult, ALU.add).then_inc(ms_x, 1)
        dve.wait_ge(rt_x, 2)
        step(nc.vector.reciprocal(tiny[:, 6:8], tiny[:, 4:6]))
        dve.wait_ge(late_here, 48)
        for t in range(TT):
            nc.vector.scalar_tensor_tensor(out=hn[:, t, :], in0=x[:, t, :], scalar=tiny[:, 6 + t:7 + t],
                                           in1=gbig, op0=ALU.mult, op1=ALU.mult).then_inc(xn_ready, 1)
        for i in (0, 2):
            bank_full(dve, f"hT{i}")
            nc.vector.tensor_copy(hT[:, 2 * i:2 * i + 2, :], bank[4 + i][:, :].rearrange("p (k s) -> p k s", k=2))\
              .then_inc(read[4 + i], 1)

        for t in range(TT):
            bank_full(dve, f"rl{t}")
            nc.vector.tensor_tensor(lg[:, t, :], bank[t][:, 0:NE], brt[:, :], ALU.add).then_inc(read[t], 1)
            was_read(dve, f"rl{t}")
            step(nc.vector.max(top8[:, t, :], lg[:, t, :]))
            nc.vector.tensor_scalar(ntop(t), top8[:, t, 0:1], -1.0, None, ALU.mult).then_inc(top_ready, 1)
            step(nc.vector.max_index(topi[:, t, :], top8[:, t, :], lg[:, t, :]))
            step(nc.vector.tensor_copy(topf[:, t, :], topi[:, t, :]))
            step(nc.vector.tensor_tensor(hot[:, t, :, :], iota[:, None, 0:NE].to_broadcast([P, TOPK, NE]),
                                         topf[:, t, 0:TOPK, None].to_broadcast([P, TOPK, NE]), ALU.is_equal))
            nc.vector.tensor_reduce(chosen[:, t, :], hot[:, t, :, :].rearrange("p k e -> p e k"), AX_X, ALU.add)\
              .then_inc(sel_ready, 1)
        dve.wait_ge(top_exp, TT)
        step(nc.vector.reciprocal(tiny[:, 46:48], tiny[:, 44:46]))
        for t in range(TT):
            step(nc.vector.tensor_scalar(topw[:, t, :], topw[:, t, :], tiny[:, 46 + t:47 + t], None, ALU.mult))
            step(nc.vector.tensor_tensor(hot[:, t, :, :], hot[:, t, :, :],
                                         topw[:, t, :, None].to_broadcast([P, TOPK, NE]), ALU.mult))
            nc.vector.tensor_reduce(wt[:, t, 0:NE], hot[:, t, :, :].rearrange("p k e -> p e k"), AX_X, ALU.add)\
              .then_inc(wt_ready, 1)
        bank_full(dve, "pos")
        nc.vector.reduce_max(tiny[0:1, 48:49], bank[2][0:1, 64:96], AX_X).then_inc(dve_step, 1)
        n[0] += 1
        for t in range(TT):
            ins = nc.vector.scalar_tensor_tensor(out=posm[:, t, 0:NE], in0=bank[2][:, 32 * t:32 * t + 32], scalar=1.0,
                                                 in1=chosen[:, t, :], op0=ALU.add, op1=ALU.mult)
            if t < TT - 1:
                step(ins)
            else:
                ins.then_inc(read[2], 1)
        was_read(dve, "pos")
        nc.vector.tensor_copy(most[:, :], tiny[0:1, 48:49]).then_inc(most_ready, 1)
        step(nc.vector.tensor_scalar(posm[:, :, 0:NE], posm[:, :, 0:NE], -1.0, None, ALU.add))
        dve.wait_ge(wt_ready, TT)
        bank_full(dve, "wT")
        nc.vector.tensor_copy(wtT[:, :], bank[3][0:NE, 0:SEQ]).then_inc(read[3], 1)
        was_read(dve, "bgT")
        dve.wait_ge(most_ready, 1)
        n_most = dve.value_load(most[0:1, 0:1], min_val=0, max_val=SEQ)

        def experts(m):
            sl, pieces, tiles, group = m["sl"], m["pieces"], m["tiles"], m["group"]
            base = n[0]
            k = [0]

            def own(it, ins):
                k[0] += 1
                ins.then_inc(dve_step, 1)
                dve.wait_ge(dve_step, it * (OWN_PER_E * UNROLL) + (base + k[0]))

            def slots(e, u):
                off = (u % group) * sl
                for t in range(TT):
                    nc.vector.tensor_scalar(su[:, t, 0:sl], iota[:, 0:sl], posm[:, t, bass.ds(e, 1)], None,
                                            ALU.is_equal).then_inc(s_ready, 1)
                    nc.vector.tensor_scalar(sw[:, t, off:off + sl], iota[:, 0:sl], posm[:, t, bass.ds(e, 1)],
                                            wt[:, t, bass.ds(e, 1)], ALU.is_equal, ALU.mult).then_inc(s_ready, 1)

            dve.sem_inc(gu_free, m["credit"])
            slots(0, 0)
            with dve.Fori(0, NE // UNROLL) as it:
                for u in range(UNROLL):
                    e = it * UNROLL + u
                    for half in range(2):
                        def bias(j):
                            return bgT[:, bass.ds(e, 1), j:j + 4].rearrange("p a j -> p (a j)")[:, :, None]\
                                .to_broadcast([P, 4, sl])

                        dve.wait_ge(chunk_done, e * PER_E + (2 * half + 1))
                        nc.vector.tensor_tensor(gt[:, :, 0:sl], m["gu_view"](2 * half), bias(4 * half), ALU.add)\
                          .then_inc(gu_free, 1)
                        dve.wait_ge(gu_free, e * 4 + (m["credit"] + 2 * half + 1))
                        nc.vector.tensor_scalar(gt[:, :, 0:sl], gt[:, :, 0:sl], LIMIT, None, ALU.min)\
                          .then_inc(g_ready, 1)
                        dve.wait_ge(chunk_done, e * PER_E + (2 * half + 2))
                        nc.vector.tensor_tensor(ut[:, :, 0:sl], m["gu_view"](2 * half + 1), bias(8 + 4 * half),
                                                ALU.add).then_inc(gu_free, 1)
                        dve.wait_ge(gu_free, e * 4 + (m["credit"] + 2 * half + 2))
                        own(it, nc.vector.tensor_scalar(ut[:, :, 0:sl], ut[:, :, 0:sl], LIMIT, -LIMIT, ALU.min,
                                                        ALU.max))
                        dve.wait_ge(sig_ready, e * 2 + (half + 1))
                        own(it, nc.vector.tensor_tensor(gl[:, :, 0:sl], gt[:, :, 0:sl], sg[:, :, 0:sl], ALU.mult))
                        nc.vector.scalar_tensor_tensor(out=av[:, 4 * half:4 * half + 4, 0:sl], in0=ut[:, :, 0:sl],
                                                       scalar=1.0, in1=gl[:, :, 0:sl], op0=ALU.add, op1=ALU.mult)\
                          .then_inc(act_ready, 1)
                        dve.wait_ge(act_ready, e * 2 + (half + 1))
                    dve.wait_ge(gather_done, (e + 1) * pieces)
                    if u % group == group - 1:
                        dve.wait_ge(tr_done, it * (UNROLL // group) + (u // group + 1))
                    slots(e + 1, u + 1)
            assert k[0] == OWN_PER_E * UNROLL
            dve.wait_ge(scattered, NE // group)

        with dve.If(n_most <= FEW):
            experts(mode_few)
        with dve.Else():
            experts(mode_all)
        n[0] += OWN_PER_E * NE

        dve.wait_ge(gfin_here, 16)
        for t in range(TT):
            step(nc.vector.tensor_tensor(x[:, t, 0:512], bank[4 + 2 * t][:, :], x[:, t, 0:512], ALU.add))
            nc.vector.tensor_tensor(x[:, t, 512:1024], bank[5 + 2 * t][:, :], x[:, t, 512:1024], ALU.add)\
              .then_inc(x_final, 1)
        for t in range(TT):
            dve.wait_ge(sq_x, 5 + t)
            nc.vector.tensor_scalar(tiny[:, 2 + t:3 + t], tiny[:, t:t + 1], 1.0 / D, EPS, ALU.mult, ALU.add)\
              .then_inc(ms_x, 1)
            dve.wait_ge(rt_x, 3 + t)
            step(nc.vector.reciprocal(tiny[:, 6 + t:7 + t], tiny[:, 4 + t:5 + t]))
            nc.vector.scalar_tensor_tensor(out=hn[:, t, :], in0=x[:, t, :], scalar=tiny[:, 6 + t:7 + t],
                                           in1=gfin, op0=ALU.mult, op1=ALU.mult).then_inc(out_ready, 1)

    @block.tensor
    def _(pe):
        def mm(o, lhsT, rhs, start=True, stop=True):
            return nc.tensor.matmul(o, lhsT, rhs, start=start, stop=stop, skip_group_check=True)

        def filled(name, ins):
            ins.then_inc(written[BANK[name]], 1)

        pe.wait_ge(consts, CONSTS_PE)
        pe.wait_ge(vec_here, 16 * 7)
        filled("vecT", nc.tensor.transpose(bank[7][:, 0:27], vec[0:27, :], ident[0:27, 0:27]))

        def to_features(prefix, banks):
            for i in range(4):
                take_bank(pe, f"{prefix}{i}")
                for k in (2 * i, 2 * i + 1):
                    for t in range(TT):
                        ins = nc.tensor.transpose(bank[banks + i][:, (k % 2) * SEQ + t * P:(k % 2) * SEQ + t * P + P],
                                                  hn[:, t, k * P:k * P + P], ident[:, :])
                filled(f"{prefix}{i}", ins)

        pe.wait_ge(xn_ready, 2)
        to_features("xT", 0)
        for i in range(4):
            was_read(pe, f"xT{i}")
        chunk_here(pe, C_SMALL)
        for t in range(TT):
            for k in range(KT):
                ins = mm(bank[4 + t][:, 0:N_SMALL], hT[:, k, t * P:t * P + P], wsm[:, k, :], k == 0, k == KT - 1)
            filled(f"small{t}", ins)
        for i in range(8):
            if i % 4 == 0:
                chunk_here(pe, C_Q + i // 4)
            take_bank(pe, f"qk{i}")
            for k in range(KT):
                ins = mm(bank[6 + i % 2][:, 0:SEQ], cols(C_Q + i // 4)[:, k, (i % 4) * P:(i % 4) * P + P],
                         hT[:, k, :], k == 0, k == KT - 1)
            filled(f"qk{i}", ins)
        chunk_here(pe, C_V)
        for t in range(TT):
            take_bank(pe, f"v{t}")
            for k in range(KT):
                ins = mm(bank[t][:, :], hT[:, k, t * P:t * P + P], cols(C_V)[:, k, :], k == 0, k == KT - 1)
            filled(f"v{t}", ins)
        pe.wait_ge(logf_ready, 1)
        take_bank(pe, "cT")
        for lo in (0, HD):
            mm(bank[2][lo:lo + HEADS, 0:P], logf[:, 0, :], upto[:, :])
            mm(bank[2][lo:lo + HEADS, P:SEQ], logf[:, 0, :], ones[:, :], True, False)
            ins = mm(bank[2][lo:lo + HEADS, P:SEQ], logf[:, 1, :], upto[:, :], False, True)
        filled("cT", ins)
        pe.wait_ge(lat_ready, 4)
        take_bank(pe, "qlT")
        for r in range(2):
            for t in range(TT):
                ins = nc.tensor.transpose(bank[3][:, r * SEQ + t * P:r * SEQ + t * P + P],
                                          spj[:, t, 8 + r * P:8 + r * P + P], ident[:, :])
        filled("qlT", ins)
        take_bank(pe, "ckT")
        for t in range(TT):
            ins = nc.tensor.transpose(bank[4][:, t * P:t * P + P], spj[:, t, 264:392], ident[:, :])
        filled("ckT", ins)
        pe.wait_ge(kpe_ready, 1)
        take_bank(pe, "kpT")
        for t in range(TT):
            ins = nc.tensor.transpose(bank[5][0:QK, t * P:t * P + P], kcat[:, t, :], ident[:, :])
        filled("kpT", ins)
        was_read(pe, "qlT")
        chunk_here(pe, C_QKV)
        for t in range(TT):
            for name, b, lo, w in ((f"qb{t}", 2 * t, 0, 512), (f"qc{t}", 2 * t + 1, 512, 256)):
                take_bank(pe, name)
                for r in range(2):
                    ins = mm(bank[b][:, 0:w], qlT[:, r, t * P:t * P + P], wqb[:, r, lo:lo + w], r == 0, r == 1)
                filled(name, ins)
        was_read(pe, "ckT")
        pe.wait_ge(kv_here, 16)
        for i in range(4):
            take_bank(pe, f"kn{i}")
            for h in (2 * i, 2 * i + 1):
                ins = mm(bank[4 + i][0:HD, (h % 2) * SEQ:(h % 2) * SEQ + SEQ], wkvb[:, h, 0:HD], ckT)
            filled(f"kn{i}", ins)
        for t in range(TT):
            take_bank(pe, f"vm{t}")
            filled(f"vm{t}", mm(bank[4 + t].rearrange("p (h c) -> p h c", h=HEADS), ckT[:, t * P:t * P + P],
                                wkvb[:, :, HD:2 * HD]))
        pe.wait_ge(q_roped, TT)
        for i in range(4):
            take_bank(pe, f"qmT{i}")
            for h in (2 * i, 2 * i + 1):
                for t in range(TT):
                    ins = nc.tensor.transpose(bank[6 + i % 2][0:QK, (h % 2) * SEQ + t * P:(h % 2) * SEQ + t * P + P],
                                              qtok[:, t, h * QK:h * QK + QK], ident[:, :])
            filled(f"qmT{i}", ins)

        def scores(i):
            b, h = i % 2, i % HEADS
            take_bank(pe, f"sc{i}")
            for t in range(TT):
                o = bank[b][:, t * P:t * P + (t + 1) * P]
                tq, tk = slice(t * P, t * P + P), slice(0, (t + 1) * P)
                if i < HEADS:
                    lo = HD * (h % 2)
                    hd, hs = slice(lo, lo + HD), slice(lo, lo + HEADS)
                    mm(o, qf[hd, h // 2, tq], kf[hd, h // 2, tk], True, False)
                    mm(o, negI[hs, h:h + 1].to_broadcast([HEADS, P]), cT[hs, tk], False, False)
                    ins = mm(o, cT[hs, tq], posI[hs, h:h + 1].to_broadcast([HEADS, (t + 1) * P]), False, True)
                else:
                    ins = mm(o, qm[0:QK, h, tq], km[0:QK, h, tk])
            filled(f"sc{i}", ins)

        def turn_probs(i):
            b = i % 2
            pe.wait_ge(prob_ready, 2 * i + 2)
            take_bank(pe, f"pT{i}")
            for c in range(3):
                ins = nc.tensor.transpose(bank[4 + b][:, c * P:c * P + P], sm[:, b, c * P:c * P + P], ident[:, :])
            filled(f"pT{i}", ins)

        def gate_tile(i):
            if i % 4 == 0:
                chunk_here(pe, C_G + i // 4)
            take_bank(pe, f"gate{i}")
            for k in range(KT):
                ins = mm(bank[2 + i % 2][:, 0:SEQ], cols(C_G + i // 4)[:, k, (i % 4) * P:(i % 4) * P + P],
                         hT[:, k, :], k == 0, k == KT - 1)
            filled(f"gate{i}", ins)

        def mix_values(i):
            b, h = i % 2, i % HEADS
            v = vf if i < HEADS else vm
            lo = HD * (h % 2)
            was_read(pe, f"pT{i}")
            take_bank(pe, f"pv{i}")
            mm(bank[6 + b][lo:lo + HD, 0:SEQ], v[:, 0, h * HD:h * HD + HD], pT[:, b, 0:SEQ], True, False)
            filled(f"pv{i}", mm(bank[6 + b][lo:lo + HD, P:SEQ], v[:, 1, h * HD:h * HD + HD], pT[:, b, SEQ:3 * P],
                                False, True))

        for name in ("qk6", "qk7", "v1", "cT", "vm1", "qmT3", "kn3", "kpT"):
            was_read(pe, name)
        for i in range(2 * HEADS + 1):
            if i < 2 * HEADS:
                scores(i)
            if i:
                turn_probs(i - 1)
            if i < 2 * HEADS:
                gate_tile(i)
            if i:
                mix_values(i - 1)

        for tag, c, y, b0, first in (("fo", C_FO, yf, 0, 0), ("mo", C_MO, ym, 4, HEADS)):
            chunk_here(pe, c)
            was_read(pe, f"pv{first + HEADS - 2}")
            was_read(pe, f"pv{first + HEADS - 1}")
            for i in range(4):
                take_bank(pe, f"{tag}{i}")
                for j in (2 * i, 2 * i + 1):
                    for k in range(4):
                        ins = mm(bank[b0 + i][:, (j % 2) * SEQ:(j % 2) * SEQ + SEQ], rows(c)[:, k, j * P:j * P + P],
                                 y[:, k, :], k == 0, k == 3)
                filled(f"{tag}{i}", ins)
        pe.wait_ge(merged, 4)
        chunk_here(pe, C_O)
        chunk_here(pe, C_O + 1)
        for i in range(4):
            t, c = i // 2, (i % 2) * 512
            take_bank(pe, f"o{i}")
            for k in range(KT):
                ins = mm(bank[i][:, :], hT[:, k, t * P:t * P + P], rows(C_O + k // 4)[:, k % 4, c:c + 512],
                         k == 0, k == KT - 1)
            filled(f"o{i}", ins)
        pe.wait_ge(xn_ready, 4)
        to_features("hT", 4)
        for i in range(4):
            was_read(pe, f"hT{i}")
        pe.wait_ge(late_here, 48)
        for t in range(TT):
            take_bank(pe, f"rl{t}")
            for k in range(KT):
                ins = mm(bank[t][:, 0:NE], hT[:, k, t * P:t * P + P], wr[:, k, :], k == 0, k == KT - 1)
            filled(f"rl{t}", ins)
        pe.wait_ge(bias_here, 32)
        take_bank(pe, "bgT")
        for j in range(2 * FF // P):
            ins = nc.tensor.transpose(bank[4][:, NE * j:NE * j + NE], bg_raw[0:NE, j * P:j * P + P],
                                      ident[0:NE, 0:NE])
        filled("bgT", ins)
        pe.wait_ge(sel_ready, TT)
        take_bank(pe, "pos")
        mm(bank[2][:, 0:NE], below[:, :], chosen[:, 0, :])
        mm(bank[2][:, NE:2 * NE], ones[:, :], chosen[:, 0, :], True, False)
        mm(bank[2][:, NE:2 * NE], below[:, :], chosen[:, 1, :], False, True)
        mm(bank[2][0:1, 64:96], ones[:, 0:1], chosen[:, 0, :], True, False)
        filled("pos", mm(bank[2][0:1, 64:96], ones[:, 0:1], chosen[:, 1, :], False, True))
        pe.wait_ge(wt_ready, TT)
        take_bank(pe, "wT")
        for t in range(TT):
            ins = nc.tensor.transpose(bank[3][0:NE, t * P:t * P + P], wt[:, t, 0:NE], ident[:, :])
        filled("wT", ins)
        was_read(pe, "wT")
        was_read(pe, "bgT")
        for t in range(TT):
            for half in range(2):
                mm(bank[4 + 2 * t + half][:, :], wtT[:, t * P:t * P + P], bd_raw[0:NE, half * 512:half * 512 + 512],
                   True, False)
        pe.wait_ge(most_ready, 1)
        n_most = pe.value_load(most[0:1, 0:1], min_val=0, max_val=SEQ)

        def experts(m):
            sl, pieces, tiles, group = m["sl"], m["pieces"], m["tiles"], m["group"]

            def gather(e):
                pe.wait_ge(s_ready, e * 4 + 4)
                for i in range(pieces):
                    if i:
                        pe.wait_ge(xg_ready, e * pieces + i)
                    for k in range(KT // pieces):
                        f = (i * (KT // pieces) + k) * P
                        for t in range(TT):
                            ins = mm(m["gather_view"][:, k, :], hn[:, t, f:f + P], su[:, t, 0:sl], t == 0, t == TT - 1)
                    ins.then_inc(gather_done, 1)

            def down(u, st, c):
                s = (PRE + u * PER_E + 4 + c) % RING
                lo, hi = m["rows"](u)
                for half in range(2):
                    for j in range(4):
                        ins = mm(bank[2 + half][lo:hi, :], av[:, 4 * c + j, st * P:st * P + hi - lo],
                                 rows(s)[:, j, half * 512:half * 512 + 512], c == 0 and j == 0, c == 1 and j == 3)
                return ins

            def scatter(it, u):
                pe.wait_ge(y_ready, it * (2 * tiles * UNROLL) + (1 + 2 * tiles * (u + 1)))
                pe.wait_ge(p_ready, it * (UNROLL // group) + (u // group + 1))
                for st in range(tiles):
                    for half in range(2):
                        for t in range(TT):
                            ins = mm(bank[4 + 2 * t + half][:, :], pw[:, st, t * P:t * P + P],
                                     ysb[:, st, half * 512:half * 512 + 512], False, False)
                ins.then_inc(scattered, 1)

            gather(0)
            with pe.Fori(0, NE // UNROLL) as it:
                for u in range(UNROLL):
                    e = it * UNROLL + u
                    pe.wait_ge(xg_ready, e * pieces + pieces)
                    for ch in range(4):
                        s = (PRE + u * PER_E + ch) % RING
                        expert_chunk_here(pe, it, u * PER_E + ch)
                        pe.wait_ge(gu_free, e * 4 + (ch + 1))
                        for j in range(4):
                            for k in range(KT):
                                ins = mm(m["gu_view"](ch)[:, j, :], cols(s)[:, k, j * P:j * P + P], xg[:, k, 0:sl],
                                         k == 0, k == KT - 1)
                        ins.then_inc(chunk_done, 1)
                        if ch == 0 and group == 2 and u == 2:
                            scatter(it, 1)
                    if u % group == group - 1:
                        pe.wait_ge(gu_free, e * 4 + 5)
                        for st in range(tiles):
                            for t in range(TT):
                                ins = nc.tensor.transpose(m["tr_view"][:, st, t * P:t * P + P],
                                                          sw[:, t, st * P:st * P + P], ident[:, :])
                        ins.then_inc(tr_done, 1)
                    pe.wait_ge(act_ready, e * 2 + 1)
                    expert_chunk_here(pe, it, u * PER_E + 4)
                    pe.wait_ge(y_ready, e * (2 * tiles) + 1)
                    ins = down(u, 0, 0)
                    if tiles == 1:
                        ins.then_inc(chunk_done, 1)
                    if u % group == group - 1:
                        pe.wait_ge(p_ready, it * (UNROLL // group) + (u // group + 1))
                    pe.wait_ge(gu_free, e * 4 + 5)
                    gather(e + 1)
                    pe.wait_ge(act_ready, e * 2 + 2)
                    expert_chunk_here(pe, it, u * PER_E + 5)
                    down(u, 0, 1).then_inc(chunk_done if tiles == 1 else y_part, 1)
                    if tiles == 2:
                        pe.wait_ge(y_ready, e * (2 * tiles) + 3)
                        down(u, 1, 0).then_inc(chunk_done, 1)
                        down(u, 1, 1).then_inc(chunk_done, 1)
                    if group == 1 or u == UNROLL - 1:
                        scatter(it, u)

        with pe.If(n_most <= FEW):
            experts(mode_few)
        with pe.Else():
            experts(mode_all)

    ctx.close()


_INS = ["x", "positions", "g_attn_norm", "w_in", "b_fgate", "g_q_a", "w_q_b", "g_kv_a", "w_kv_b", "w_fox_out",
        "w_mla_out", "b_merge", "w_o", "g_ffn_norm", "w_router", "b_router", "w_gu", "b_gu", "w_down", "b_down",
        "g_final"]


def kernel(**inputs):
    import numpy as _np
    import concourse.bacc as _bacc
    from concourse import mybir as _mybir
    from concourse.bass_utils import run_bass_kernel_spmd as _run

    nc = _bacc.Bacc("TRN2", target_bir_lowering=False, num_devices=1, dynamic_dma_scratch_size=1024)
    arrays, args = {}, []
    for name in _INS:
        a = _np.ascontiguousarray(inputs[name])
        arrays[f"in_{name}"] = a
        args.append(nc.dram_tensor(f"in_{name}", a.shape, _mybir.dt.from_np(a.dtype), kind="ExternalInput").ap())
    args.append(nc.dram_tensor("out_0", (1, 256, 1024), _mybir.dt.float32, kind="ExternalOutput").ap())
    build(nc, *args)
    r = _run(nc, [arrays], core_ids=[0])
    return r.results[0]["out_0"]
```

```python
from contextlib import ExitStack

import numpy as np

import concourse.bass as bass
from concourse import mybir

F32 = mybir.dt.float32
I32 = mybir.dt.int32
U32 = mybir.dt.uint32
ALU = mybir.AluOpType
ACT = mybir.ActivationFunctionType
AX_X = mybir.AxisListType.X

P = 128
D = 1024
SEQ = 256
TT = SEQ // P
KT = D // P
HEADS = 8
HD = 64
FOX = HEADS * HD
ROPE = 32
HALF = ROPE // 2
QK = HD + ROPE
Q_RANK = 256
KV_RANK = 128
NE = 32
TOPK = 4
FF = 1024
LIMIT = 7.0
ALPHA = 1.702
EPS = 1e-6
THETA = 10000.0
MASKED = -1e30
COL_SMALL = 3 * FOX
N_SMALL = HEADS + Q_RANK + KV_RANK + ROPE
COL_GATE = COL_SMALL + N_SMALL

SLOT = 4096
RING = 8
PRE = 13
PER_E = 6
UNROLL = 4
BODY = UNROLL * PER_E
AHEAD = RING + 2
SLOT_AT = [(PRE + p) % RING for p in range(RING)] + [8, 9]
SLOT_AT += [SLOT_AT[_q] for _q in (0, 1, 2, 3, 4, 5, 6, 7, 0, 1, 2, 3, 8, 9)]
FEW = 64

TWO_PI = [6.28125, 0.001934051513671875, 1.2509822845458984e-06, 3.1886e-09]
TWO_PI[3] = 2.0 * float(np.pi) - sum(TWO_PI[:3])
MAGIC = 12582912.0

USES = ([(f"xT{i}", i) for i in range(4)] + [("vecT", 7)] + [("small0", 4), ("small1", 5)]
        + [(f"qk{i}", 6 + i % 2) for i in range(8)] + [("v0", 0), ("v1", 1)]
        + [("cT", 2), ("qlT", 3), ("ckT", 4), ("kpT", 5)]
        + [("qb0", 0), ("qc0", 1), ("qb1", 2), ("qc1", 3)]
        + [(f"kn{i}", 4 + i) for i in range(4)] + [("vm0", 4), ("vm1", 5)]
        + [(f"qmT{i}", 6 + i % 2) for i in range(4)])
for _i in range(2 * HEADS + 1):
    if _i < 2 * HEADS:
        USES += [(f"sc{_i}", _i % 2), (f"gate{_i}", 2 + _i % 2)]
    if _i:
        USES += [(f"pT{_i - 1}", 4 + (_i - 1) % 2)]
    if _i and _i % 2 == 0:
        USES += [(f"pv{_i // 2 - 1}", 6 + (_i // 2 - 1) % 2)]
USES += ([(f"fo{i}", i) for i in range(4)] + [(f"mo{i}", 4 + i) for i in range(4)]
         + [(f"o{i}", i) for i in range(4)] + [(f"hT{i}", 4 + i) for i in range(4)]
         + [("rl0", 0), ("rl1", 1), ("pos", 2), ("wT", 3), ("bgT", 4)])
BANK, NTH = {}, {}
_n = [0] * 8
for _name, _b in USES:
    BANK[_name], NTH[_name] = _b, _n[_b]
    _n[_b] += 1
BANK_USES = list(_n)
CHUNK_END = ["small1", "vm1", "qk3", "qk7", "v1", "gate3", "gate7", "gate11", "gate15", "fo3", "mo3",
             "o3", "o3"]
CONSTS = 50
CONSTS_PE = 16
C_SMALL, C_QKV, C_Q, C_K, C_V, C_G, C_FO, C_MO, C_O = 0, 1, 2, 3, 4, 5, 9, 10, 11


def build(nc, x_in, pos_in, g_attn, w_in, b_fgate, g_q_a, w_q_b, g_kv_a, w_kv_b, w_fox_out, w_mla_out,
          b_merge, w_o, g_ffn, w_router, b_router, w_gu, b_gu, w_down, b_down, g_final, out):
    ctx = ExitStack()

    def sb(name, shape, dt=F32):
        return ctx.enter_context(nc.sbuf_tensor(name, shape, dt))

    def sem(name):
        return ctx.enter_context(nc.semaphore(name))

    ring = sb("ring", [P, RING, SLOT])
    arena = sb("arena", [P, 16384])
    x = sb("x", [P, TT, D])
    hn = sb("hn", [P, TT, D])
    ident = sb("ident", [P, P])
    upto = sb("upto", [P, P])
    below = sb("below", [P, P])
    ones = sb("ones", [P, P])
    mask = sb("mask", [P, 2, 3 * P])
    iota = sb("iota", [P, SEQ])
    sm = sb("sm", [P, 2, 3 * P])
    pT = sb("pT", [P, 2, 3 * P])
    tiny = sb("tiny", [P, 64])
    vecT = sb("vecT", [P, 27])
    bf = sb("bf", [P, HEADS])
    brt = sb("brt", [P, NE])
    pos_i = sb("pos_i", [P, TT], I32)
    logf = sb("logf", [P, TT, HEADS])
    cT = hn[0:HD + HEADS, 0, 768:1024]
    negI = sb("negI", [HD + HEADS, HEADS])
    posI = sb("posI", [HD + HEADS, HEADS])
    fgt = hn[:, 1, 768:768 + 6 * TT * HEADS].rearrange("p (i c) -> p i c", i=6)
    topi = sb("topi", [P, TT, 8], U32)
    most = sb("most", [1, 1], I32)
    posm = sb("posm", [P, TT, NE + 2])
    wt = sb("wt", [P, TT, NE + 2])

    def part(off, shape):
        n = int(np.prod(shape))
        v = arena[:, off:off + n]
        if len(shape) == 2:
            return v.rearrange("p (a b) -> p a b", a=shape[0])
        if len(shape) == 3:
            return v.rearrange("p (a b c) -> p a b c", a=shape[0], b=shape[1])
        return v

    hT = part(0, [KT, SEQ])
    gates = part(2048, [2 * KT, SEQ])
    qf = part(6144, [4, SEQ])
    kf = part(7168, [4, SEQ])
    vf = part(8192, [TT, FOX])
    qm = part(9216, [HEADS, SEQ])
    km = part(11264, [HEADS, SEQ])
    vm = part(13312, [TT, FOX])
    yf = part(14336, [4, SEQ])
    ym = part(15360, [4, SEQ])
    ropetmp = part(14336, [4, TT, HEADS * HALF])
    qlT = part(15360, [2, SEQ])
    ckT = part(15872, [SEQ])
    trig = part(16128, [4, TT * 2 * HALF])
    qtok = hn[:, :, 0:768]
    spj = part(9216, [TT, N_SMALL])
    kcat = part(9216 + TT * N_SMALL, [TT, QK])
    vec = part(9216 + TT * N_SMALL + TT * QK, [P])
    gbig = part(5120, [D])
    extra = [arena[:, 6144 + SLOT * i:6144 + SLOT * (i + 1)] for i in range(2)]
    su = part(0, [TT, P])
    sw = part(256, [TT, P])
    pw = part(512, [SEQ])
    xg = part(1024, [KT, P])
    av = part(4096, [KT, FEW])
    wtT = part(768, [SEQ])[0:NE, :]
    raw = part(2048, [2, 512])
    ysb = part(3072, [D])
    gt = part(15360, [KT, FEW])
    bg_raw = part(2048, [2 * FF])
    bd_raw = part(4096, [D])
    spare = sm[:, :, :].rearrange("p a b -> p (a b)")
    wr = spare[:, 512:768].rearrange("p (k e) -> p k e", k=KT)
    bgT = spare[:, 0:512].rearrange("p (e j) -> p e j", e=NE)
    sg = part(15872, [KT, FEW])
    ut = part(14336, [KT, FEW])
    gl = part(14848, [KT, FEW])
    gfin = gbig

    psum = ctx.enter_context(nc.psum_tensor("psum", [P, 8 * 512], F32))
    bank = [psum[:, 512 * b:512 * b + 512] for b in range(8)]

    def nmax(b, t):
        return tiny[:, 40 + 2 * b + t:41 + 2 * b + t]

    def rsum(b, t):
        return tiny[:, 32 + 2 * b + t:33 + 2 * b + t]

    def ntop(t):
        return tiny[:, 52 + t:53 + t]

    def tsum(t):
        return tiny[:, 44 + t:45 + t]

    def fz(i):
        return fgt[:, i, :]

    square_scratch = part(14336, [512])
    lg = part(14336, [TT, NE])
    top8 = part(14400, [TT, 8])
    topf = part(14416, [TT, 8])
    topw = part(14432, [TT, TOPK])
    chosen = part(14448, [TT, NE])
    hot = part(14528, [TT, TOPK, NE])

    def steps_of(rounds):
        return [(u, r) for u in range(UNROLL) for r in range(rounds)]

    halves = ((0, slice(0, FEW)), (1, slice(FEW, P)))
    gate_bank, up_bank, out_bank, turn_bank = bank[0], bank[1], bank[2], bank[3]

    kv_here = sem("kv_here")
    x_here = [sem(f"x_here{t}") for t in range(TT)]
    vec_here = sem("vec_here")
    late_here = sem("late_here")
    bias_here = sem("bias_here")
    gfin_here = sem("gfin_here")
    consts = sem("consts")
    slot_in = [sem(f"slot_in{s}") for s in range(AHEAD)]
    written = [sem(f"bank_written{b}") for b in range(8)]
    read = [sem(f"bank_read{b}") for b in range(8)]
    dve_step = sem("dve_step")
    moe_step = sem("moe_step")
    act_step = sem("act_step")
    sq_x = sem("sq_x")
    ms_x = sem("ms_x")
    rt_x = sem("rt_x")
    xn_ready = sem("xn_ready")
    f_abs = sem("f_abs")
    f_exp = sem("f_exp")
    f_one = sem("f_one")
    f_ln = sem("f_ln")
    logf_ready = sem("logf_ready")
    lat_sq = sem("lat_sq")
    lat_ms = sem("lat_ms")
    lat_rt = sem("lat_rt")
    lat_ready = sem("lat_ready")
    kpe_ready = sem("kpe_ready")
    angle_ready = sem("angle_ready")
    trig_ready = sem("trig_ready")
    q_roped = sem("q_roped")
    qm_ready = sem("qm_ready")
    max_ready = sem("max_ready")
    exp_ready = sem("exp_ready")
    prob_ready = sem("prob_ready")
    merged = sem("merged")
    gates_sig = sem("gates_sig")
    top_ready = sem("top_ready")
    top_exp = sem("top_exp")
    sel_ready = sem("sel_ready")
    wt_ready = sem("wt_ready")
    most_ready = sem("most_ready")
    s_ready = sem("s_ready")
    chunk_done = sem("chunk_done")
    gu_part = sem("gu_part")
    y_part = sem("y_part")
    raw_ready = sem("raw_ready")
    turned = sem("turned")
    gate_read = sem("gate_read")
    up_read = sem("up_read")
    g_ready = sem("g_ready")
    sig_ready = sem("sig_ready")
    av_ready = sem("av_ready")
    tr_done = sem("tr_done")
    p_ready = sem("p_ready")
    gather_done = sem("gather_done")
    xg_ready = sem("xg_ready")
    y_ready = sem("y_ready")
    scattered = sem("scattered")
    x_final = sem("x_final")
    out_ready = sem("out_ready")
    stored = sem("stored")

    def chunk_here(eng, c):
        eng.wait_ge(slot_in[c % RING], 16 * (c // RING + 1))

    def expert_chunk_here(eng, it, p):
        s = SLOT_AT[p]
        before = len([c for c in range(PRE) if c % RING == s]) + SLOT_AT[:p].count(s)
        eng.wait_ge(slot_in[s], it * (16 * SLOT_AT.count(s)) + 16 * (before + 1))

    def take_bank(eng, name):
        if NTH[name]:
            eng.wait_ge(read[BANK[name]], NTH[name])

    def bank_full(eng, name):
        eng.wait_ge(written[BANK[name]], NTH[name] + 1)

    def was_read(eng, name):
        eng.wait_ge(read[BANK[name]], NTH[name] + 1)

    def chunk(c):
        return ring[:, c % RING, :]

    wsm = chunk(C_SMALL)[:, 0:KT * N_SMALL].rearrange("p (k n) -> p k n", k=KT)
    wqb = chunk(C_QKV)[:, 0:2 * 768].rearrange("p (k n) -> p k n", k=2)
    wkvb = chunk(C_QKV)[:, 1536:1536 + 1024].rearrange("p (h n) -> p h n", h=HEADS)

    def cols(c):
        return chunk(c).rearrange("p (k n) -> p k n", k=KT)

    def rows(c):
        return chunk(c).rearrange("p (k n) -> p k n", k=4)

    def expert_slot(p):
        s = SLOT_AT[p]
        return ring[:, s, :] if s < RING else extra[s - RING]

    def gate_up(p):
        return expert_slot(p).rearrange("p (k n) -> p k n", k=2)

    def down_rows(p):
        return expert_slot(p).rearrange("p (k n) -> p k n", k=4)

    w_in_v = w_in[0].rearrange("(k p) n -> p k n", p=P)
    w_gu_v = w_gu[0].rearrange("e (k p) f -> p e k f", p=P)
    w_dn_v = w_down[0].rearrange("e (k p) n -> p e k n", p=P)

    block = ctx.enter_context(nc.Block())

    @block.sync
    def _(sp):
        x_v = x_in[0].rearrange("(t p) d -> p t d", p=P)
        for t in range(TT):
            sp.dma_start(x[:, t, :], x_v[:, t, :]).then_inc(x_here[t], 16)
        sp.wait_ge(x_here[0], 16)

        def load(c, pairs):
            for dst, src in pairs:
                sp.dma_start(dst, src).then_inc(slot_in[c % RING], 16)

        qkv = w_q_b[0].rearrange("(k p) n -> p k n", p=P)
        pre = [[(wsm, w_in_v[:, :, COL_SMALL:COL_GATE])], [(wqb, qkv)]]
        pre += [[(cols(2 + i), w_in_v[:, :, 512 * i:512 * i + 512])] for i in range(3)]
        pre += [[(cols(C_G + i), w_in_v[:, :, COL_GATE + 512 * i:COL_GATE + 512 * i + 512])] for i in range(4)]
        pre += [[(rows(C_FO), w_fox_out[0].rearrange("(k p) n -> p k n", p=P))],
                [(rows(C_MO), w_mla_out[0].rearrange("(k p) n -> p k n", p=P))]]
        wo_v = w_o[0].rearrange("(k p) n -> p k n", p=P)
        pre += [[(rows(C_O + i), wo_v[:, 4 * i:4 * i + 4, :])] for i in range(2)]
        for c in range(PRE):
            if c >= RING:
                bank_full(sp, CHUNK_END[c - RING])
            load(c, pre[c])
            if c == 1:
                sp.dma_start(wkvb, w_kv_b[0].rearrange("p (h n) -> p h n", h=HEADS)).then_inc(kv_here, 16)

        def load_expert(n, it=None):
            e, k = n // PER_E, n % PER_E
            p = n % BODY
            ee = e if it is None else it * UNROLL + e
            if k < 4:
                src = w_gu_v[:, bass.ds(ee, 1), 2 * k:2 * k + 2, :].rearrange("p a k f -> p (a k) f")
                dst = gate_up(p)
            else:
                src = w_dn_v[:, bass.ds(ee, 1), 4 * (k - 4):4 * (k - 4) + 4, :].rearrange("p a k n -> p (a k) n")
                dst = down_rows(p)
            sp.dma_start(dst, src).then_inc(slot_in[SLOT_AT[p]], 16)

        def last_in_slot(n):
            return next(q for q in range(n - 1, -1, -1) if SLOT_AT[q % BODY] == SLOT_AT[n % BODY])

        for n in range(AHEAD):
            bank_full(sp, CHUNK_END[PRE + n - RING] if n < RING else f"pv{HEADS - 1}")
            load_expert(n)
        turns = (NE * PER_E - AHEAD) // BODY
        with sp.Fori(0, turns) as it:
            for n in range(AHEAD, AHEAD + BODY):
                sp.wait_ge(chunk_done, it * BODY + (last_in_slot(n) + 1))
                load_expert(n, it)
        for n in range(AHEAD + turns * BODY, NE * PER_E):
            sp.wait_ge(chunk_done, last_in_slot(n) + 1)
            load_expert(n)

        out_v = out[0].rearrange("(t p) d -> p t d", p=P)
        for t in range(TT):
            sp.wait_ge(out_ready, t + 1)
            sp.dma_start(out_v[:, t, :], hn[:, t, :]).then_inc(stored, 16)
        sp.wait_ge(stored, 16 * TT)

    @block.gpsimd
    def _(pool):
        k = 0

        def step(ins):
            nonlocal k
            k += 1
            ins.then_inc(consts, 1)
            pool.wait_ge(consts, k)

        step(pool.memset(ident[:, :], 0.0))
        step(pool.affine_select(out=ident[:, :], in_=ident[:, :], compare_op=ALU.not_equal, fill=1.0,
                                base=0, pattern=[[-1, P]], channel_multiplier=1))
        step(pool.memset(ones[:, :], 1.0))
        step(pool.affine_select(out=upto[:, :], in_=ones[:, :], compare_op=ALU.is_ge, fill=0.0,
                                base=0, pattern=[[1, P]], channel_multiplier=-1))
        step(pool.affine_select(out=below[:, :], in_=ones[:, :], compare_op=ALU.is_gt, fill=0.0,
                                base=0, pattern=[[1, P]], channel_multiplier=-1))
        step(pool.memset(mask[:, :, :], 0.0))
        for b in (0, 2):
            step(pool.affine_select(out=mask[:, 0, b * P:(b + 1) * P], in_=mask[:, 0, b * P:(b + 1) * P],
                                    compare_op=ALU.is_ge, fill=MASKED, base=0, pattern=[[-1, P]],
                                    channel_multiplier=1))
            step(pool.memset(mask[0:64, 1, b * P + 64:(b + 1) * P], MASKED))
        step(pool.memset(kcat[:, :, :], 0.0))
        for lo in (0, HD):
            step(pool.tensor_scalar(negI[lo:lo + HEADS, :], ident[lo:lo + HEADS, lo:lo + HEADS], -8.0, 0.0,
                                    ALU.mult, ALU.add))
            step(pool.tensor_scalar(posI[lo:lo + HEADS, :], ident[lo:lo + HEADS, lo:lo + HEADS], 8.0, 0.0,
                                    ALU.mult, ALU.add))
        step(pool.iota(iota[:, :], [[1, SEQ]], base=0, channel_multiplier=0,
                       allow_small_or_imprecise_dtypes=True))
        for t in range(TT):
            for i in range(HALF):
                step(pool.memset(trig[:, 0, t * 2 * HALF + i:t * 2 * HALF + i + 1],
                                 float(np.float32(THETA ** (-i / HALF)))))
        step(pool.memset(posm[:, :, NE:NE + 2], -1.0))
        step(pool.memset(wt[:, :, NE:NE + 2], 0.0))
        assert k == CONSTS

    @block.scalar
    def _(act):
        act.dma_start(vec[0:8, :], g_attn[0].rearrange("(k p) -> k p", p=P)).then_inc(vec_here, 16)
        act.dma_start(vec[8:10, :], g_q_a[0].rearrange("(k p) -> k p", p=P)).then_inc(vec_here, 16)
        act.dma_start(vec[10:11, :], g_kv_a[0:1, :]).then_inc(vec_here, 16)
        act.dma_start(vec[11:27, :], b_merge[0].rearrange("b (k p) -> (b k) p", p=P)).then_inc(vec_here, 16)
        act.dma_start(bf[:, :], b_fgate[0:1, :].to_broadcast([P, HEADS])).then_inc(vec_here, 16)
        for t in range(TT):
            act.dma_start(pos_i[:, t:t + 1], pos_in[0, t * P:t * P + P].rearrange("(p a) -> p a", a=1))\
               .then_inc(vec_here, 16)

        def root_of_mean(t, n):
            act.wait_ge(ms_x, n + 1)
            nc.scalar.activation(tiny[:, 4 + t:5 + t], tiny[:, 2 + t:3 + t], ACT.Sqrt).then_inc(rt_x, 1)

        for t in range(TT):
            act.wait_ge(x_here[t], 16)
            nc.scalar.activation(hn[:, t, :], x[:, t, :], ACT.Square, accum_out=tiny[:, t:t + 1]).then_inc(sq_x, 1)
        root_of_mean(0, 0)
        root_of_mean(1, 1)

        def evac(name, dst, src, scale=None):
            bank_full(act, name)
            nc.scalar.activation(dst, src, ACT.Copy, **({} if scale is None else {"scale": scale}))\
              .then_inc(read[BANK[name]], 1)

        was_read(act, "vecT")
        for i in (2, 3):
            bank_full(act, f"xT{i}")
            nc.scalar.activation(hT[:, 2 * i, :], bank[i][:, 0:SEQ], ACT.Copy,
                                 scale=vecT[:, 2 * i:2 * i + 1]).then_inc(act_step, 1)
            nc.scalar.activation(hT[:, 2 * i + 1, :], bank[i][:, SEQ:512], ACT.Copy,
                                 scale=vecT[:, 2 * i + 1:2 * i + 2]).then_inc(read[i], 1)
        was_read(act, "small1")
        for t in range(TT):
            nc.scalar.activation(square_scratch[:, 0:Q_RANK], spj[:, t, 8:8 + Q_RANK], ACT.Square,
                                 accum_out=tiny[:, 8 + t:9 + t]).then_inc(lat_sq, 1)
            nc.scalar.activation(square_scratch[:, Q_RANK:Q_RANK + KV_RANK], spj[:, t, 264:264 + KV_RANK], ACT.Square,
                                 accum_out=tiny[:, 10 + t:11 + t]).then_inc(lat_sq, 1)
            act.wait_ge(lat_sq, 2 * t + 2)
        act.wait_ge(lat_ms, 1)
        nc.scalar.activation(tiny[:, 16:20], tiny[:, 12:16], ACT.Sqrt).then_inc(lat_rt, 1)
        for i in range(4):
            evac(f"qk{i}", qf[:, i, :], bank[6 + i % 2][:, 0:SEQ])
        act.wait_ge(f_abs, 1)
        nc.scalar.activation(fz(1), fz(0), ACT.Exp, scale=-1.0).then_inc(f_exp, 1)
        act.wait_ge(f_one, 1)
        nc.scalar.activation(fz(3), fz(2), ACT.Ln).then_inc(f_ln, 1)
        for i in range(4, 8):
            evac(f"qk{i}", kf[:, i - 4, :], bank[6 + i % 2][:, 0:SEQ])
        act.wait_ge(angle_ready, 1)
        nc.scalar.activation(trig[:, 2, :], trig[:, 0, :], ACT.Sin).then_inc(trig_ready, 1)
        for t in range(TT):
            evac(f"v{t}", vf[:, t, :], bank[t][:, :])
        bank_full(act, "cT")
        nc.scalar.activation(cT[0:HEADS, :], bank[2][0:HEADS, 0:SEQ], ACT.Copy).then_inc(act_step, 1)
        nc.scalar.activation(cT[HD:HD + HEADS, :], bank[2][HD:HD + HEADS, 0:SEQ], ACT.Copy).then_inc(read[2], 1)
        for t in range(TT):
            evac(f"qb{t}", qtok[:, t, 0:512], bank[2 * t][:, :])
            evac(f"qc{t}", qtok[:, t, 512:768], bank[2 * t + 1][:, 0:256])
        for i in range(4):
            bank_full(act, f"kn{i}")
            nc.scalar.activation(km[0:HD, 2 * i, :], bank[4 + i][0:HD, 0:SEQ], ACT.Copy).then_inc(act_step, 1)
            nc.scalar.activation(km[0:HD, 2 * i + 1, :], bank[4 + i][HD:P, 0:SEQ], ACT.Copy)\
              .then_inc(read[4 + i], 1)
        for t in range(TT):
            evac(f"vm{t}", vm[:, t, :], bank[4 + t][:, :])

        for i in range(2 * HEADS):
            b = i % 2
            act.wait_ge(max_ready, i + 1)
            nc.scalar.activation(sm[:, b, 0:P], sm[:, b, 0:P], ACT.Exp, bias=nmax(b, 0),
                                 accum_out=rsum(b, 0)).then_inc(exp_ready, 1)
            nc.scalar.activation(sm[:, b, P:3 * P], sm[:, b, P:3 * P], ACT.Exp, bias=nmax(b, 1),
                                 accum_out=rsum(b, 1)).then_inc(exp_ready, 1)
            bank_full(act, f"gate{i}")
            nc.scalar.activation(gates[:, i, :], bank[2 + b][:, 0:SEQ], ACT.Identity,
                                 bias=vecT[:, 11 + i:12 + i]).then_inc(read[2 + b], 1)
        was_read(act, f"gate{2 * HEADS - 1}")
        for i in (0, 2, 1, 3):
            nc.scalar.activation(gates[:, 4 * i:4 * i + 4, :], gates[:, 4 * i:4 * i + 4, :], ACT.Sigmoid)\
              .then_inc(gates_sig, 1)
        act.wait_ge(merged, 4)
        act.dma_start(gbig, g_ffn[0:1, :].to_broadcast([P, D])).then_inc(late_here, 16)
        act.dma_start(brt[:, :], b_router[0:1, :].to_broadcast([P, NE])).then_inc(late_here, 16)
        act.dma_start(wr, w_router[0].rearrange("(k p) n -> p k n", p=P)).then_inc(late_here, 16)
        act.dma_start(bg_raw[0:NE, :], b_gu[0]).then_inc(bias_here, 16)
        act.dma_start(bd_raw[0:NE, :], b_down[0]).then_inc(bias_here, 16)

        for t in range(TT):
            was_read(act, f"o{2 * t}")
            was_read(act, f"o{2 * t + 1}")
            nc.scalar.activation(hn[:, t, :], x[:, t, :], ACT.Square, accum_out=tiny[:, t:t + 1]).then_inc(sq_x, 1)
            root_of_mean(t, 2 + t)
        for i in (1, 3):
            evac(f"hT{i}", hT[:, 2 * i:2 * i + 2, :], bank[4 + i][:, :].rearrange("p (k s) -> p k s", k=2))
        for t in range(TT):
            act.wait_ge(top_ready, t + 1)
            nc.scalar.activation(topw[:, t, :], top8[:, t, 0:TOPK], ACT.Exp, bias=ntop(t),
                                 accum_out=tsum(t)).then_inc(top_exp, 1)
        bank_full(act, "bgT")
        nc.scalar.activation(bgT.rearrange("p e j -> p j e"),
                             bank[4][:, :].rearrange("p (j e) -> p j e", e=NE), ACT.Copy).then_inc(read[4], 1)

        def experts(rounds):
            body = steps_of(rounds)
            m = len(body)

            def take_gather(pair):
                for i, b in ((0, up_bank), (1, turn_bank)):
                    act.wait_ge(gather_done, pair * 2 + (i + 1))
                    nc.scalar.activation(xg[:, 4 * i:4 * i + 4, :], b.rearrange("p (k s) -> p k s", k=4),
                                         ACT.Copy).then_inc(xg_ready, 1)

            act.sem_inc(y_ready, 1)
            take_gather(0)
            with act.Fori(0, NE // UNROLL) as it:
                for i, (u, r) in enumerate(body):
                    n = it * m + i
                    if i % 2:
                        act.wait_ge(tr_done, it * (m // 2) + (i // 2 + 1))
                        nc.scalar.activation(pw, turn_bank[:, 0:SEQ], ACT.Copy).then_inc(p_ready, 1)
                    if r == rounds - 1:
                        act.wait_ge(chunk_done, it * (UNROLL * PER_E) + (u * PER_E + 4))
                    else:
                        act.wait_ge(gu_part, it * (UNROLL * (rounds - 1)) + (u * (rounds - 1) + r + 1))
                    for j, b in ((0, gate_bank), (1, up_bank)):
                        nc.scalar.activation(raw[:, j, :], b, ACT.Copy).then_inc(raw_ready, 1)
                    act.wait_ge(g_ready, n + 1)
                    nc.scalar.activation(sg, gt, ACT.Sigmoid, scale=ALPHA).then_inc(sig_ready, 1)
                    if i % 2:
                        take_gather(it * (m // 2) + (i // 2 + 1))
                    if r == rounds - 1:
                        act.wait_ge(chunk_done, it * (UNROLL * PER_E) + (u * PER_E + 6))
                    else:
                        act.wait_ge(y_part, it * (UNROLL * (rounds - 1)) + (u * (rounds - 1) + r + 1))
                    for c, lanes in halves:
                        nc.scalar.activation(ysb[halves[i % 2][1], c * 512:c * 512 + 512], out_bank[lanes, :],
                                             ACT.Copy).then_inc(y_ready, 1)

        act.wait_ge(xn_ready, 4)
        act.dma_start(gfin, g_final.rearrange("(a d) -> a d", a=1).to_broadcast([P, D])).then_inc(gfin_here, 16)
        act.wait_ge(most_ready, 1)
        n_most = act.value_load(most[0:1, 0:1], min_val=0, max_val=SEQ)
        with act.If(n_most <= FEW):
            experts(1)
        with act.Else():
            experts(SEQ // FEW)

        nc.scalar.activation(tiny[:, 56:57], tiny[:, 4:5], ACT.Sqrt).then_inc(act_step, 1)
        for t in range(TT):
            act.wait_ge(x_final, t + 1)
            nc.scalar.activation(hn[:, t, :], x[:, t, :], ACT.Square, accum_out=tiny[:, t:t + 1]).then_inc(sq_x, 1)
            root_of_mean(t, 4 + t)

    @block.vector
    def _(dve):
        n = [0]

        def step(ins):
            n[0] += 1
            ins.then_inc(dve_step, 1)
            dve.wait_ge(dve_step, n[0])

        def mean_square(t, n):
            dve.wait_ge(sq_x, n + 1)
            nc.vector.tensor_scalar(tiny[:, 2 + t:3 + t], tiny[:, t:t + 1], 1.0 / D, EPS, ALU.mult, ALU.add)\
              .then_inc(ms_x, 1)

        def rsqrt(t, n):
            dve.wait_ge(rt_x, n + 1)
            step(nc.vector.reciprocal(tiny[:, 6 + t:7 + t], tiny[:, 4 + t:5 + t]))

        for t in range(TT):
            mean_square(t, t)
        for t in range(TT):
            rsqrt(t, t)
            nc.vector.tensor_scalar(hn[:, t, :], x[:, t, :], tiny[:, 6 + t:7 + t], None, ALU.mult)\
              .then_inc(xn_ready, 1)
        bank_full(dve, "vecT")
        nc.vector.tensor_copy(vecT[:, :], bank[7][:, 0:27]).then_inc(read[7], 1)
        was_read(dve, "vecT")
        for i in (0, 1):
            bank_full(dve, f"xT{i}")
            nc.vector.tensor_scalar(hT[:, 2 * i, :], bank[i][:, 0:SEQ], vecT[:, 2 * i:2 * i + 1], None,
                                    ALU.mult).then_inc(dve_step, 1)
            nc.vector.tensor_scalar(hT[:, 2 * i + 1, :], bank[i][:, SEQ:512], vecT[:, 2 * i + 1:2 * i + 2], None,
                                    ALU.mult).then_inc(read[i], 1)
            n[0] += 1

        dve.wait_ge(vec_here, 16 * 7)
        dve.wait_ge(consts, CONSTS)
        step(nc.vector.tensor_copy(tiny[:, 20:22], pos_i[:, :]))
        ang = trig[:, 0, :].rearrange("p (t f) -> p t f", t=TT)
        trn = trig[:, 1, :].rearrange("p (t f) -> p t f", t=TT)
        for t in range(TT):
            step(nc.vector.tensor_scalar(ang[:, t, 0:HALF], ang[:, t, 0:HALF], tiny[:, 20 + t:21 + t], None,
                                         ALU.mult))
        step(nc.vector.tensor_copy(ang[:, :, HALF:2 * HALF], ang[:, :, 0:HALF]))
        step(nc.vector.tensor_scalar(trn[:, :, 0:HALF], ang[:, :, 0:HALF], 1.0 / (2.0 * float(np.pi)), None,
                                     ALU.mult))
        step(nc.vector.tensor_scalar(trn[:, :, HALF:2 * HALF], ang[:, :, HALF:2 * HALF],
                                     1.0 / (2.0 * float(np.pi)), 0.25, ALU.mult, ALU.add))
        step(nc.vector.tensor_scalar(trn, trn, MAGIC, None, ALU.add))
        step(nc.vector.tensor_scalar(trn, trn, -MAGIC, None, ALU.add))
        for c in TWO_PI:
            step(nc.vector.scalar_tensor_tensor(out=ang, in0=trn, scalar=-c, in1=ang, op0=ALU.mult, op1=ALU.add))
        step(nc.vector.tensor_scalar(ang[:, :, HALF:2 * HALF], ang[:, :, HALF:2 * HALF],
                                     float(np.pi) / 2.0, None, ALU.add))
        pi = float(np.nextafter(np.float32(np.pi), np.float32(0)))
        nc.vector.tensor_scalar(ang, ang, pi, -pi, ALU.min, ALU.max).then_inc(angle_ready, 1)

        for t in range(TT):
            bank_full(dve, f"small{t}")
            nc.vector.tensor_copy(spj[:, t, :], bank[4 + t][:, 0:N_SMALL]).then_inc(read[4 + t], 1)
        was_read(dve, "small0")
        was_read(dve, "small1")
        for t in range(TT):
            step(nc.vector.tensor_tensor(logf[:, t, :], spj[:, t, 0:HEADS], bf[:, :], ALU.add))
        lf = logf[:, :, :].rearrange("p t h -> p (t h)")
        nc.vector.scalar_tensor_tensor(out=fz(0), in0=lf, scalar=-1.0, in1=lf, op0=ALU.mult,
                                       op1=ALU.max).then_inc(f_abs, 1)
        dve.wait_ge(lat_sq, 4)
        step(nc.vector.tensor_scalar(tiny[:, 12:14], tiny[:, 8:10], 1.0 / Q_RANK, EPS, ALU.mult, ALU.add))
        nc.vector.tensor_scalar(tiny[:, 14:16], tiny[:, 10:12], 1.0 / KV_RANK, EPS, ALU.mult, ALU.add)\
          .then_inc(lat_ms, 1)
        dve.wait_ge(lat_rt, 1)
        step(nc.vector.reciprocal(tiny[:, 24:28], tiny[:, 16:20]))
        for t in range(TT):
            nc.vector.tensor_scalar(spj[:, t, 8:264], spj[:, t, 8:264], tiny[:, 24 + t:25 + t], None,
                                    ALU.mult).then_inc(lat_ready, 1)
            nc.vector.tensor_scalar(spj[:, t, 264:392], spj[:, t, 264:392], tiny[:, 26 + t:27 + t], None,
                                    ALU.mult).then_inc(lat_ready, 1)
        dve.wait_ge(f_exp, 1)
        nc.vector.tensor_scalar(fz(2), fz(1), 1.0, None, ALU.add).then_inc(f_one, 1)
        dve.wait_ge(f_one, 1)
        step(nc.vector.tensor_scalar(fz(4), fz(2), -1.0, None, ALU.add))
        step(nc.vector.tensor_tensor(fz(4), fz(1), fz(4), ALU.subtract))
        step(nc.vector.reciprocal(fz(5), fz(2)))
        step(nc.vector.tensor_tensor(fz(4), fz(4), fz(5), ALU.mult))
        dve.wait_ge(f_ln, 1)
        step(nc.vector.tensor_tensor(fz(4), fz(4), fz(3), ALU.add))
        nc.vector.scalar_tensor_tensor(out=lf, in0=lf, scalar=0.0, in1=fz(4), op0=ALU.min,
                                       op1=ALU.subtract).then_inc(logf_ready, 1)

        dve.wait_ge(trig_ready, 1)
        tr = trig[:, 2, :].rearrange("p (t f) -> p t f", t=TT)
        sin, cos = tr[:, :, 0:HALF], tr[:, :, HALF:2 * HALF]
        k1, k2 = spj[:, :, 392:392 + HALF], spj[:, :, 392 + HALF:392 + ROPE]
        m = [ropetmp[:, i, :, 0:HALF] for i in range(4)]
        nc.vector.tensor_tensor(m[0], k1, cos, ALU.mult).then_inc(dve_step, 1)
        nc.vector.tensor_tensor(m[1], k2, sin, ALU.mult).then_inc(dve_step, 1)
        nc.vector.tensor_tensor(m[2], k2, cos, ALU.mult).then_inc(dve_step, 1)
        n[0] += 3
        step(nc.vector.tensor_tensor(m[3], k1, sin, ALU.mult))
        step(nc.vector.tensor_tensor(kcat[:, :, HD:HD + HALF], m[0], m[1], ALU.subtract))
        nc.vector.tensor_tensor(kcat[:, :, HD + HALF:QK], m[2], m[3], ALU.add).then_inc(kpe_ready, 1)
        bank_full(dve, "qlT")
        step(nc.vector.tensor_scalar(qlT[:, 0, :], bank[3][:, 0:SEQ], vecT[:, 8:9], None, ALU.mult))
        nc.vector.tensor_scalar(qlT[:, 1, :], bank[3][:, SEQ:512], vecT[:, 9:10], None, ALU.mult)\
          .then_inc(read[3], 1)
        bank_full(dve, "ckT")
        nc.vector.tensor_scalar(ckT, bank[4][:, 0:SEQ], vecT[:, 10:11], None, ALU.mult).then_inc(read[4], 1)
        bank_full(dve, "kpT")
        nc.vector.tensor_copy(km[HD:QK, :, :], bank[5][HD:QK, None, 0:SEQ].to_broadcast([ROPE, HEADS, SEQ]))\
          .then_inc(read[5], 1)
        for t in range(TT):
            was_read(dve, f"qb{t}")
            was_read(dve, f"qc{t}")
        for t in range(TT):
            qh = qtok[:, t, :].rearrange("p (h c) -> p h c", h=HEADS)
            q1, q2 = qh[:, :, HD:HD + HALF], qh[:, :, HD + HALF:QK]
            ct = cos[:, t, None, :].to_broadcast([P, HEADS, HALF])
            st = sin[:, t, None, :].to_broadcast([P, HEADS, HALF])
            m = [ropetmp[:, i, t, :].rearrange("p (h c) -> p h c", h=HEADS) for i in range(4)]
            nc.vector.tensor_tensor(m[0], q1, ct, ALU.mult).then_inc(dve_step, 1)
            nc.vector.tensor_tensor(m[1], q2, st, ALU.mult).then_inc(dve_step, 1)
            nc.vector.tensor_tensor(m[2], q2, ct, ALU.mult).then_inc(dve_step, 1)
            n[0] += 3
            step(nc.vector.tensor_tensor(m[3], q1, st, ALU.mult))
            step(nc.vector.tensor_tensor(q1, m[0], m[1], ALU.subtract))
            nc.vector.tensor_tensor(q2, m[2], m[3], ALU.add).then_inc(q_roped, 1)

        def qm_copy(i):
            bank_full(dve, f"qmT{i}")
            nc.vector.tensor_copy(qm[0:QK, 2 * i:2 * i + 2, :],
                                  bank[6 + i % 2][0:QK, :].rearrange("p (h s) -> p h s", h=2))\
              .then_inc(read[6 + i % 2], 1)

        for i in range(4):
            qm_copy(i)

        def softmax_max(i):
            b = i % 2
            bank_full(dve, f"sc{i}")
            if i >= 2:
                dve.wait_ge(written[BANK[f"pT{i - 2}"]], NTH[f"pT{i - 2}"] + 1)
            nc.vector.scalar_tensor_tensor(out=sm[:, b, :], in0=bank[b][:, 0:3 * P],
                                           scalar=(HD if i < HEADS else QK) ** -0.5, in1=mask[:, i // HEADS, :],
                                           op0=ALU.mult, op1=ALU.add).then_inc(read[b], 1)
            was_read(dve, f"sc{i}")
            step(nc.vector.tensor_reduce(nmax(b, 0), sm[:, b, 0:P], AX_X, ALU.max, negate=True))
            nc.vector.tensor_reduce(nmax(b, 1), sm[:, b, P:3 * P], AX_X, ALU.max, negate=True).then_inc(max_ready, 1)

        def softmax_norm(i):
            b = i % 2
            dve.wait_ge(exp_ready, 2 * i + 2)
            step(nc.vector.reciprocal(tiny[:, 36 + 2 * b:38 + 2 * b], tiny[:, 32 + 2 * b:34 + 2 * b]))
            nc.vector.tensor_scalar(sm[:, b, 0:P], sm[:, b, 0:P], tiny[:, 36 + 2 * b:37 + 2 * b], None,
                                    ALU.mult).then_inc(prob_ready, 1)
            nc.vector.tensor_scalar(sm[:, b, P:3 * P], sm[:, b, P:3 * P], tiny[:, 37 + 2 * b:38 + 2 * b], None,
                                    ALU.mult).then_inc(prob_ready, 1)

        def probs_out(i):
            b = i % 2
            bank_full(dve, f"pT{i}")
            nc.vector.tensor_copy(pT[:, b, :], bank[4 + b][:, 0:3 * P]).then_inc(read[4 + b], 1)

        def heads_out(pair):
            y = yf if 2 * pair < HEADS else ym
            bank_full(dve, f"pv{pair}")
            nc.vector.tensor_copy(y[:, pair % 4, :], bank[6 + pair % 2][:, 0:SEQ]).then_inc(read[6 + pair % 2], 1)

        for i in range(2 * HEADS + 1):
            if i < 2 * HEADS:
                softmax_max(i)
            if i:
                probs_out(i - 1)
            if i < 2 * HEADS:
                softmax_norm(i)
            if i and i % 2 == 0:
                heads_out(i // 2 - 1)

        g4 = lambda a: gates[:, a:a + 2, :].rearrange("p k s -> p (k s)")
        for i in range(4):
            dve.wait_ge(gates_sig, 1 + (i >= 2) * 2)
            bank_full(dve, f"fo{i}")
            nc.vector.tensor_tensor(g4(2 * i), bank[i][:, :], g4(2 * i), ALU.mult).then_inc(read[i], 1)
        for i in range(4):
            dve.wait_ge(gates_sig, 4)
            bank_full(dve, f"mo{i}")
            nc.vector.tensor_tensor(g4(8 + 2 * i), bank[4 + i][:, :], g4(8 + 2 * i), ALU.mult).then_inc(read[4 + i], 1)
            was_read(dve, f"mo{i}")
            was_read(dve, f"fo{i}")
            nc.vector.tensor_tensor(hT[:, 2 * i:2 * i + 2, :].rearrange("p k s -> p (k s)"), g4(2 * i),
                                    g4(8 + 2 * i), ALU.add).then_inc(merged, 1)

        for i in range(4):
            t, c = i // 2, (i % 2) * 512
            bank_full(dve, f"o{i}")
            nc.vector.tensor_tensor(x[:, t, c:c + 512], bank[i][:, :], x[:, t, c:c + 512], ALU.add)\
              .then_inc(read[i], 1)
            if i % 2 == 0:
                continue
            mean_square(t, 2 + t)
            rsqrt(t, 2 + t)
            dve.wait_ge(late_here, 48)
            nc.vector.scalar_tensor_tensor(out=hn[:, t, :], in0=x[:, t, :], scalar=tiny[:, 6 + t:7 + t],
                                           in1=gbig, op0=ALU.mult, op1=ALU.mult).then_inc(xn_ready, 1)
        for i in (0, 2):
            bank_full(dve, f"hT{i}")
            nc.vector.tensor_copy(hT[:, 2 * i:2 * i + 2, :], bank[4 + i][:, :].rearrange("p (k s) -> p k s", k=2))\
              .then_inc(read[4 + i], 1)

        for t in range(TT):
            bank_full(dve, f"rl{t}")
            nc.vector.tensor_tensor(lg[:, t, :], bank[t][:, 0:NE], brt[:, :], ALU.add).then_inc(read[t], 1)
            was_read(dve, f"rl{t}")
            step(nc.vector.max(top8[:, t, :], lg[:, t, :]))
            nc.vector.tensor_scalar(ntop(t), top8[:, t, 0:1], -1.0, None, ALU.mult).then_inc(top_ready, 1)
            step(nc.vector.max_index(topi[:, t, :], top8[:, t, :], lg[:, t, :]))
            step(nc.vector.tensor_copy(topf[:, t, :], topi[:, t, :]))
            step(nc.vector.tensor_tensor(hot[:, t, :, :], iota[:, None, 0:NE].to_broadcast([P, TOPK, NE]),
                                         topf[:, t, 0:TOPK, None].to_broadcast([P, TOPK, NE]), ALU.is_equal))
            nc.vector.tensor_reduce(chosen[:, t, :], hot[:, t, :, :].rearrange("p k e -> p e k"), AX_X, ALU.add)\
              .then_inc(sel_ready, 1)
        dve.wait_ge(top_exp, TT)
        step(nc.vector.reciprocal(tiny[:, 46:48], tiny[:, 44:46]))
        for t in range(TT):
            step(nc.vector.tensor_scalar(topw[:, t, :], topw[:, t, :], tiny[:, 46 + t:47 + t], None, ALU.mult))
            step(nc.vector.tensor_tensor(hot[:, t, :, :], hot[:, t, :, :],
                                         topw[:, t, :, None].to_broadcast([P, TOPK, NE]), ALU.mult))
            nc.vector.tensor_reduce(wt[:, t, 0:NE], hot[:, t, :, :].rearrange("p k e -> p e k"), AX_X, ALU.add)\
              .then_inc(wt_ready, 1)
        bank_full(dve, "pos")
        nc.vector.reduce_max(tiny[0:1, 48:49], bank[2][0:1, 64:96], AX_X).then_inc(dve_step, 1)
        n[0] += 1
        for t in range(TT):
            ins = nc.vector.scalar_tensor_tensor(out=posm[:, t, 0:NE], in0=bank[2][:, 32 * t:32 * t + 32], scalar=1.0,
                                                 in1=chosen[:, t, :], op0=ALU.add, op1=ALU.mult)
            if t < TT - 1:
                step(ins)
            else:
                ins.then_inc(read[2], 1)
        was_read(dve, "pos")
        nc.vector.tensor_copy(most[:, :], tiny[0:1, 48:49]).then_inc(most_ready, 1)
        step(nc.vector.tensor_scalar(posm[:, :, 0:NE], posm[:, :, 0:NE], -1.0, None, ALU.add))
        dve.wait_ge(wt_ready, TT)
        bank_full(dve, "wT")
        nc.vector.tensor_copy(wtT[:, :], bank[3][0:NE, 0:SEQ]).then_inc(read[3], 1)
        was_read(dve, "bgT")
        dve.wait_ge(most_ready, 1)
        n_most = dve.value_load(most[0:1, 0:1], min_val=0, max_val=SEQ)

        def experts(rounds):
            body = steps_of(rounds)
            m = len(body)
            k = [0]

            def own(it, ins):
                k[0] += 1
                ins.then_inc(moe_step, 1)
                dve.wait_ge(moe_step, it * (2 * m) + k[0])

            def slots(it, i):
                for h in range(2):
                    u, r = (i + h) // rounds, (i + h) % rounds
                    e = bass.ds(u if it is None else it * UNROLL + u, 1)
                    at = iota[:, r * FEW:r * FEW + FEW]
                    for t in range(TT):
                        nc.vector.tensor_scalar(su[:, t, halves[h][1]], at, posm[:, t, e], None,
                                                ALU.is_equal).then_inc(s_ready, 1)
                        nc.vector.tensor_scalar(sw[:, t, halves[h][1]], at, posm[:, t, e], wt[:, t, e],
                                                ALU.is_equal, ALU.mult).then_inc(s_ready, 1)

            dve.sem_inc(gate_read, 1)
            dve.sem_inc(up_read, 1)
            slots(None, 0)
            turned_view = [b.rearrange("p (c s) -> p c s", c=KT) for b in (turn_bank, gate_bank)]
            with dve.Fori(0, NE // UNROLL) as it:
                for i, (u, r) in enumerate(body):
                    n_step = it * m + i
                    if i % 2:
                        dve.wait_ge(tr_done, it * (m // 2) + (i // 2 + 1))
                        slots(it, i + 1)

                    def bias(j):
                        return bgT[:, bass.ds(it * UNROLL + u, 1), j:j + KT].rearrange("p a j -> p (a j)")\
                            [:, :, None].to_broadcast([P, KT, FEW])

                    dve.wait_ge(turned, n_step * 2 + 1)
                    nc.vector.tensor_tensor(gt, turned_view[0], bias(0), ALU.add).then_inc(gate_read, 1)
                    dve.wait_ge(gate_read, n_step + 2)
                    nc.vector.tensor_scalar(gt, gt, LIMIT, None, ALU.min).then_inc(g_ready, 1)
                    dve.wait_ge(turned, n_step * 2 + 2)
                    nc.vector.tensor_tensor(ut, turned_view[1], bias(KT), ALU.add).then_inc(up_read, 1)
                    dve.wait_ge(up_read, n_step + 2)
                    own(it, nc.vector.tensor_scalar(ut, ut, LIMIT, -LIMIT, ALU.min, ALU.max))
                    dve.wait_ge(sig_ready, n_step + 1)
                    own(it, nc.vector.tensor_tensor(gl, gt, sg, ALU.mult))
                    nc.vector.scalar_tensor_tensor(out=av, in0=ut, scalar=1.0, in1=gl, op0=ALU.add,
                                                   op1=ALU.mult).then_inc(av_ready, 1)
                    dve.wait_ge(av_ready, n_step + 1)
            assert k[0] == 2 * m
            dve.wait_ge(scattered, NE * rounds // 2)

        with dve.If(n_most <= FEW):
            experts(1)
        with dve.Else():
            experts(SEQ // FEW)

        dve.wait_ge(gfin_here, 16)
        for t in range(TT):
            step(nc.vector.tensor_tensor(x[:, t, 0:512], bank[4 + 2 * t][:, :], x[:, t, 0:512], ALU.add))
            nc.vector.tensor_tensor(x[:, t, 512:1024], bank[5 + 2 * t][:, :], x[:, t, 512:1024], ALU.add)\
              .then_inc(x_final, 1)
        for t in range(TT):
            mean_square(t, 4 + t)
            rsqrt(t, 4 + t)
            nc.vector.scalar_tensor_tensor(out=hn[:, t, :], in0=x[:, t, :], scalar=tiny[:, 6 + t:7 + t],
                                           in1=gfin, op0=ALU.mult, op1=ALU.mult).then_inc(out_ready, 1)

    @block.tensor
    def _(pe):
        def mm(o, lhsT, rhs, start=True, stop=True):
            return nc.tensor.matmul(o, lhsT, rhs, start=start, stop=stop, skip_group_check=True)

        def filled(name, ins):
            ins.then_inc(written[BANK[name]], 1)

        def to_features(prefix, banks, norm):
            for t in range(TT):
                pe.wait_ge(xn_ready, norm * TT + t + 1)
                for i in range(4):
                    if t == 0:
                        take_bank(pe, f"{prefix}{i}")
                    for k in (2 * i, 2 * i + 1):
                        ins = nc.tensor.transpose(bank[banks + i][:, (k % 2) * SEQ + t * P:(k % 2) * SEQ + t * P + P],
                                                  hn[:, t, k * P:k * P + P], ident[:, :])
                    if t == TT - 1:
                        filled(f"{prefix}{i}", ins)

        pe.wait_ge(consts, CONSTS_PE)
        to_features("xT", 0, 0)
        pe.wait_ge(vec_here, 16 * 7)
        filled("vecT", nc.tensor.transpose(bank[7][:, 0:27], vec[0:27, :], ident[0:27, 0:27]))

        for i in range(4):
            was_read(pe, f"xT{i}")
        chunk_here(pe, C_SMALL)
        for t in range(TT):
            for k in range(KT):
                ins = mm(bank[4 + t][:, 0:N_SMALL], hT[:, k, t * P:t * P + P], wsm[:, k, :], k == 0, k == KT - 1)
            filled(f"small{t}", ins)
        for i in range(8):
            if i % 4 == 0:
                chunk_here(pe, C_Q + i // 4)
            take_bank(pe, f"qk{i}")
            for k in range(KT):
                ins = mm(bank[6 + i % 2][:, 0:SEQ], cols(C_Q + i // 4)[:, k, (i % 4) * P:(i % 4) * P + P],
                         hT[:, k, :], k == 0, k == KT - 1)
            filled(f"qk{i}", ins)
        chunk_here(pe, C_V)
        for t in range(TT):
            take_bank(pe, f"v{t}")
            for k in range(KT):
                ins = mm(bank[t][:, :], hT[:, k, t * P:t * P + P], cols(C_V)[:, k, :], k == 0, k == KT - 1)
            filled(f"v{t}", ins)
        pe.wait_ge(logf_ready, 1)
        take_bank(pe, "cT")
        for lo in (0, HD):
            mm(bank[2][lo:lo + HEADS, 0:P], logf[:, 0, :], upto[:, :])
            mm(bank[2][lo:lo + HEADS, P:SEQ], logf[:, 0, :], ones[:, :], True, False)
            ins = mm(bank[2][lo:lo + HEADS, P:SEQ], logf[:, 1, :], upto[:, :], False, True)
        filled("cT", ins)
        pe.wait_ge(lat_ready, 4)
        take_bank(pe, "qlT")
        for r in range(2):
            for t in range(TT):
                ins = nc.tensor.transpose(bank[3][:, r * SEQ + t * P:r * SEQ + t * P + P],
                                          spj[:, t, 8 + r * P:8 + r * P + P], ident[:, :])
        filled("qlT", ins)
        take_bank(pe, "ckT")
        for t in range(TT):
            ins = nc.tensor.transpose(bank[4][:, t * P:t * P + P], spj[:, t, 264:392], ident[:, :])
        filled("ckT", ins)
        pe.wait_ge(kpe_ready, 1)
        take_bank(pe, "kpT")
        for t in range(TT):
            ins = nc.tensor.transpose(bank[5][0:QK, t * P:t * P + P], kcat[:, t, :], ident[:, :])
        filled("kpT", ins)
        was_read(pe, "qlT")
        chunk_here(pe, C_QKV)
        for t in range(TT):
            for name, b, lo, w in ((f"qb{t}", 2 * t, 0, 512), (f"qc{t}", 2 * t + 1, 512, 256)):
                take_bank(pe, name)
                for r in range(2):
                    ins = mm(bank[b][:, 0:w], qlT[:, r, t * P:t * P + P], wqb[:, r, lo:lo + w], r == 0, r == 1)
                filled(name, ins)
        was_read(pe, "ckT")
        pe.wait_ge(kv_here, 16)
        for i in range(4):
            take_bank(pe, f"kn{i}")
            for h in (2 * i, 2 * i + 1):
                ins = mm(bank[4 + i][HD * (h % 2):HD * (h % 2) + HD, 0:SEQ], wkvb[:, h, 0:HD], ckT)
            filled(f"kn{i}", ins)
        for t in range(TT):
            take_bank(pe, f"vm{t}")
            filled(f"vm{t}", mm(bank[4 + t].rearrange("p (h c) -> p h c", h=HEADS), ckT[:, t * P:t * P + P],
                                wkvb[:, :, HD:2 * HD]))
        pe.wait_ge(q_roped, TT)
        for i in range(4):
            take_bank(pe, f"qmT{i}")
            for h in (2 * i, 2 * i + 1):
                for t in range(TT):
                    ins = nc.tensor.transpose(bank[6 + i % 2][0:QK, (h % 2) * SEQ + t * P:(h % 2) * SEQ + t * P + P],
                                              qtok[:, t, h * QK:h * QK + QK], ident[:, :])
            filled(f"qmT{i}", ins)

        def scores(i):
            b, h = i % 2, i % HEADS
            take_bank(pe, f"sc{i}")
            for t in range(TT):
                o = bank[b][:, t * P:t * P + (t + 1) * P]
                tq, tk = slice(t * P, t * P + P), slice(0, (t + 1) * P)
                if i < HEADS:
                    lo = HD * (h % 2)
                    hd, hs = slice(lo, lo + HD), slice(lo, lo + HEADS)
                    mm(o, qf[hd, h // 2, tq], kf[hd, h // 2, tk], True, False)
                    mm(o, negI[hs, h:h + 1].to_broadcast([HEADS, P]), cT[hs, tk], False, False)
                    ins = mm(o, cT[hs, tq], posI[hs, h:h + 1].to_broadcast([HEADS, (t + 1) * P]), False, True)
                else:
                    ins = mm(o, qm[0:QK, h, tq], km[0:QK, h, tk])
            filled(f"sc{i}", ins)

        def turn_probs(i):
            b = i % 2
            pe.wait_ge(prob_ready, 2 * i + 2)
            take_bank(pe, f"pT{i}")
            for c in range(3):
                ins = nc.tensor.transpose(bank[4 + b][:, c * P:c * P + P], sm[:, b, c * P:c * P + P], ident[:, :])
            filled(f"pT{i}", ins)

        def gate_tile(i):
            if i % 4 == 0:
                chunk_here(pe, C_G + i // 4)
            take_bank(pe, f"gate{i}")
            for k in range(KT):
                ins = mm(bank[2 + i % 2][:, 0:SEQ], cols(C_G + i // 4)[:, k, (i % 4) * P:(i % 4) * P + P],
                         hT[:, k, :], k == 0, k == KT - 1)
            filled(f"gate{i}", ins)

        def mix_values(pair):
            v = vf if 2 * pair < HEADS else vm
            was_read(pe, f"pT{2 * pair}")
            was_read(pe, f"pT{2 * pair + 1}")
            take_bank(pe, f"pv{pair}")
            o = bank[6 + pair % 2]
            for k, q, p in ((0, slice(0, SEQ), slice(0, SEQ)), (1, slice(P, SEQ), slice(SEQ, 3 * P))):
                for b in range(2):
                    c = ((2 * pair) % HEADS + b) * HD
                    ins = mm(o[HD * b:HD * b + HD, q], v[:, k, c:c + HD], pT[:, b, p], k == 0, k == 1)
            filled(f"pv{pair}", ins)

        for name in ("qk6", "qk7", "v1", "cT", "vm1", "qmT3", "kn3", "kpT"):
            was_read(pe, name)
        for i in range(2 * HEADS + 1):
            if i < 2 * HEADS:
                scores(i)
            if i:
                turn_probs(i - 1)
            if i < 2 * HEADS:
                gate_tile(i)
            if i and i % 2 == 0:
                mix_values(i // 2 - 1)

        for tag, c, y, b0, first in (("fo", C_FO, yf, 0, 0), ("mo", C_MO, ym, 4, HEADS)):
            chunk_here(pe, c)
            was_read(pe, f"pv{(first + HEADS) // 2 - 2}")
            was_read(pe, f"pv{(first + HEADS) // 2 - 1}")
            for i in range(4):
                take_bank(pe, f"{tag}{i}")
                for j in (2 * i, 2 * i + 1):
                    for k in range(4):
                        ins = mm(bank[b0 + i][:, (j % 2) * SEQ:(j % 2) * SEQ + SEQ], rows(c)[:, k, j * P:j * P + P],
                                 y[:, k, :], k == 0, k == 3)
                filled(f"{tag}{i}", ins)
        pe.wait_ge(merged, 4)
        chunk_here(pe, C_O)
        chunk_here(pe, C_O + 1)
        for i in range(4):
            t, c = i // 2, (i % 2) * 512
            take_bank(pe, f"o{i}")
            for k in range(KT):
                ins = mm(bank[i][:, :], hT[:, k, t * P:t * P + P], rows(C_O + k // 4)[:, k % 4, c:c + 512],
                         k == 0, k == KT - 1)
            filled(f"o{i}", ins)
        to_features("hT", 4, 1)
        for i in range(4):
            was_read(pe, f"hT{i}")
        pe.wait_ge(late_here, 48)
        for t in range(TT):
            take_bank(pe, f"rl{t}")
            for k in range(KT):
                ins = mm(bank[t][:, 0:NE], hT[:, k, t * P:t * P + P], wr[:, k, :], k == 0, k == KT - 1)
            filled(f"rl{t}", ins)
        pe.wait_ge(bias_here, 32)
        take_bank(pe, "bgT")
        for j in range(2 * FF // P):
            tile = KT * (j // KT) + 4 * (j % 2) + (j % KT) // 2
            ins = nc.tensor.transpose(bank[4][:, NE * j:NE * j + NE], bg_raw[0:NE, tile * P:tile * P + P],
                                      ident[0:NE, 0:NE])
        filled("bgT", ins)
        pe.wait_ge(sel_ready, TT)
        take_bank(pe, "pos")
        mm(bank[2][:, 0:NE], below[:, :], chosen[:, 0, :])
        mm(bank[2][:, NE:2 * NE], ones[:, :], chosen[:, 0, :], True, False)
        mm(bank[2][:, NE:2 * NE], below[:, :], chosen[:, 1, :], False, True)
        mm(bank[2][0:1, 64:96], ones[:, 0:1], chosen[:, 0, :], True, False)
        filled("pos", mm(bank[2][0:1, 64:96], ones[:, 0:1], chosen[:, 1, :], False, True))
        pe.wait_ge(wt_ready, TT)
        take_bank(pe, "wT")
        for t in range(TT):
            ins = nc.tensor.transpose(bank[3][0:NE, t * P:t * P + P], wt[:, t, 0:NE], ident[:, :])
        filled("wT", ins)
        was_read(pe, "wT")
        was_read(pe, "bgT")
        for t in range(TT):
            for half in range(2):
                mm(bank[4 + 2 * t + half][:, :], wtT[:, t * P:t * P + P], bd_raw[0:NE, half * 512:half * 512 + 512],
                   True, False)
        pe.wait_ge(most_ready, 1)
        n_most = pe.value_load(most[0:1, 0:1], min_val=0, max_val=SEQ)

        def experts(rounds):
            body = steps_of(rounds)
            m = len(body)

            def gather(pair, i):
                pe.wait_ge(s_ready, pair * 8 + 8)
                b = (up_bank, turn_bank)[i]
                for k in range(4):
                    f = (4 * i + k) * P
                    for t in range(TT):
                        ins = mm(b[:, k * P:k * P + P], hn[:, t, f:f + P], su[:, t, :], t == 0, t == TT - 1)
                ins.then_inc(gather_done, 1)

            def scatter(it, i):
                pe.wait_ge(y_ready, it * (2 * m) + (2 * i + 3))
                pe.wait_ge(p_ready, it * (m // 2) + (i // 2 + 1))
                for half in range(2):
                    for t in range(TT):
                        ins = mm(bank[4 + 2 * t + half], pw[:, t * P:t * P + P],
                                 ysb[:, half * 512:half * 512 + 512], False, False)
                ins.then_inc(scattered, 1)

            gather(0, 0)
            gather(0, 1)
            with pe.Fori(0, NE // UNROLL) as it:
                for i, (u, r) in enumerate(body):
                    n = it * m + i
                    own = halves[i % 2][1]
                    last = r == rounds - 1
                    if i % 2 == 0:
                        pe.wait_ge(xg_ready, it * m + (i + 2))
                    pe.wait_ge(up_read, n + 1)
                    if i % 2 == 0:
                        pe.wait_ge(gate_read, n + 1)
                    for ch in range(4):
                        if r == 0:
                            expert_chunk_here(pe, it, u * PER_E + ch)
                        for k in range(2):
                            f = 2 * ch + k
                            for j, b in ((0, gate_bank), (1, up_bank)):
                                for c, lanes in halves:
                                    ins = mm(b[lanes, :], xg[:, f, own],
                                             gate_up(u * PER_E + ch)[:, k, j * FF + c * 512:j * FF + c * 512 + 512],
                                             f == 0, f == KT - 1)
                        if last:
                            ins.then_inc(chunk_done, 1)
                        elif ch == 3:
                            ins.then_inc(gu_part, 1)
                        if ch == 0 and i % 2:
                            pe.wait_ge(gate_read, n + 1)
                            for t in range(TT):
                                ins = nc.tensor.transpose(turn_bank[:, t * P:t * P + P], sw[:, t, :], ident[:, :])
                            ins.then_inc(tr_done, 1)
                    if i % 2 == 0 and i:
                        scatter(it, i - 1)
                    if i % 2:
                        pe.wait_ge(p_ready, it * (m // 2) + (i // 2 + 1))
                    for j, b in ((0, turn_bank), (1, gate_bank)):
                        pe.wait_ge(raw_ready, n * 2 + (j + 1))
                        for c in range(4):
                            ins = nc.tensor.transpose(b[:, c * P:c * P + P], raw[:, j, c * P:c * P + P], ident[:, :])
                        ins.then_inc(turned, 1)
                    if i % 2:
                        gather(it * (m // 2) + (i // 2 + 1), 0)
                    pe.wait_ge(av_ready, n + 1)
                    pe.wait_ge(y_ready, it * (2 * m) + (2 * i + 1))
                    for half in range(2):
                        if half and i % 2:
                            pe.wait_ge(gate_read, n + 2)
                            gather(it * (m // 2) + (i // 2 + 1), 1)
                        if r == 0:
                            expert_chunk_here(pe, it, u * PER_E + 4 + half)
                        for j in range(4):
                            for c, lanes in halves:
                                ins = mm(out_bank[lanes, :], av[:, 2 * j + half, :],
                                         down_rows(u * PER_E + 4 + half)[:, j, c * 512:c * 512 + 512],
                                         half == 0 and j == 0, half == 1 and j == 3)
                        if last:
                            ins.then_inc(chunk_done, 1)
                        elif half:
                            ins.then_inc(y_part, 1)
                scatter(it, m - 1)

        with pe.If(n_most <= FEW):
            experts(1)
        with pe.Else():
            experts(SEQ // FEW)

    ctx.close()


_INS = ["x", "positions", "g_attn_norm", "w_in", "b_fgate", "g_q_a", "w_q_b", "g_kv_a", "w_kv_b", "w_fox_out",
        "w_mla_out", "b_merge", "w_o", "g_ffn_norm", "w_router", "b_router", "w_gu", "b_gu", "w_down", "b_down",
        "g_final"]


def kernel(**inputs):
    import numpy as _np
    import concourse.bacc as _bacc
    from concourse import mybir as _mybir
    from concourse.bass_utils import run_bass_kernel_spmd as _run

    nc = _bacc.Bacc("TRN2", target_bir_lowering=False, num_devices=1, dynamic_dma_scratch_size=1024)
    arrays, args = {}, []
    for name in _INS:
        a = _np.ascontiguousarray(inputs[name])
        arrays[f"in_{name}"] = a
        args.append(nc.dram_tensor(f"in_{name}", a.shape, _mybir.dt.from_np(a.dtype), kind="ExternalInput").ap())
    args.append(nc.dram_tensor("out_0", (1, 256, 1024), _mybir.dt.float32, kind="ExternalOutput").ap())
    build(nc, *args)
    r = _run(nc, [arrays], core_ids=[0])
    return r.results[0]["out_0"]
```

```python
from contextlib import ExitStack

import numpy as np

import concourse.bass as bass
from concourse import mybir

F32 = mybir.dt.float32
F32R = mybir.dt.float32r
BF16 = mybir.dt.bfloat16
I32 = mybir.dt.int32
U32 = mybir.dt.uint32
ALU = mybir.AluOpType
ACT = mybir.ActivationFunctionType
AX_X = mybir.AxisListType.X

P = 128
D = 1024
SEQ = 256
TT = SEQ // P
KT = D // P
HEADS = 8
HD = 64
FOX = HEADS * HD
ROPE = 32
HALF = ROPE // 2
QK = HD + ROPE
Q_RANK = 256
KV_RANK = 128
NE = 32
TOPK = 4
FF = 1024
LIMIT = 7.0
ALPHA = 1.702
EPS = 1e-6
THETA = 10000.0
MASKED = -1e30
COL_SMALL = 3 * FOX
N_SMALL = HEADS + Q_RANK + KV_RANK + ROPE
COL_GATE = COL_SMALL + N_SMALL

SLOT = 4096
RING = 8
PRE = 13
PER_E = 6
UNROLL = 4
BODY = UNROLL * PER_E
AHEAD = RING + 2
PRE_RING = 5
SLOT_AT = [3, 8, 9, 4, 0, 1, 2, 5, 6, 7]
SLOT_AT += [SLOT_AT[_q] for _q in (0, 1, 2, 3, 4, 5, 6, 7, 0, 1, 2, 3, 8, 9)]
FEW = 64

TWO_PI = [6.28125, 0.001934051513671875, 1.2509822845458984e-06, 3.1886e-09]
TWO_PI[3] = 2.0 * float(np.pi) - sum(TWO_PI[:3])
MAGIC = 12582912.0

USES = ([(f"xT{i}", i) for i in range(4)] + [("vecT", 7)] + [("small0", 4), ("small1", 5)]
        + [(f"qk{i}", 6 + i % 2) for i in range(8)] + [("v0", 0), ("v1", 1)]
        + [("cT", 2), ("qlT", 3), ("ckT", 4), ("kpT", 5)]
        + [("qb0", 0), ("qc0", 1), ("qb1", 2), ("qc1", 3)]
        + [(f"kn{i}", 4 + i) for i in range(4)] + [("vm0", 4), ("vm1", 5)]
        + [(f"qmT{i}", 6 + i % 2) for i in range(4)])
for _i in range(2 * HEADS + 1):
    if _i < 2 * HEADS:
        USES += [(f"sc{_i}", _i % 2), (f"gate{_i}", 2 + _i % 2)]
    if _i:
        USES += [(f"pT{_i - 1}", 4 + (_i - 1) % 2)]
    if _i and _i % 2 == 0:
        USES += [(f"pv{_i // 2 - 1}", 6 + (_i // 2 - 1) % 2)]
USES += ([(f"fo{i}", i) for i in range(4)] + [(f"mo{i}", 4 + i) for i in range(4)]
         + [(f"o{i}", i) for i in range(4)] + [(f"hT{i}", 4 + i) for i in range(4)]
         + [("rl0", 0), ("rl1", 1), ("pos", 2), ("wT", 3), ("bgT", 4)])
BANK, NTH = {}, {}
_n = [0] * 8
for _name, _b in USES:
    BANK[_name], NTH[_name] = _b, _n[_b]
    _n[_b] += 1
BANK_USES = list(_n)
C_SMALL, C_Q, C_K, C_V, C_QKV, C_G, C_FO, C_MO, C_O = 0, 1, 2, 3, 4, 5, 9, 10, 11
SPLIT = [C_Q, C_K, C_V] + [C_G + _i for _i in range(4)] + [C_FO, C_MO, C_O, C_O + 1]
HALF_OF = {_c: 2 * _i for _i, _c in enumerate(SPLIT)}
HALF_END = (["qk1", "qk3", "qk5", "qk7", 1, "v1"] + [f"gate{_i}" for _i in range(1, 16, 2)]
            + ["fo1", "fo3", "mo1", "mo3", 2, 3, 4, "o3"])
CONSTS = 53
CONSTS_PE = 19


def build(nc, x_in, pos_in, g_attn, w_in, b_fgate, g_q_a, w_q_b, g_kv_a, w_kv_b, w_fox_out, w_mla_out,
          b_merge, w_o, g_ffn, w_router, b_router, w_gu, b_gu, w_down, b_down, g_final, out):
    ctx = ExitStack()

    def sb(name, shape, dt=F32):
        return ctx.enter_context(nc.sbuf_tensor(name, shape, dt))

    def sem(name):
        return ctx.enter_context(nc.semaphore(name))

    with ExitStack() as first:
        def early(name, shape, dt=F32R):
            return first.enter_context(nc.sbuf_tensor(name, shape, dt))

        early("first_slots", [P, PRE_RING * SLOT], F32)
        hs = [early("h_hi", [P, KT, SEQ]), early("h_lo", [P, KT, SEQ])]
        ws = [early("w_hi", [P, 2, SLOT // 2]), early("w_lo", [P, 2, SLOT // 2])]
        y_hi = early("y_hi", [P, KT, SEQ])
        early("between", [P, 14336 - KT * SEQ], F32)
        ys = [y_hi, early("y_lo", [P, KT, SEQ])]
    ring = sb("ring", [P, RING, SLOT])
    arena = sb("arena", [P, 16384])
    x = sb("x", [P, TT, D])
    hn = sb("hn", [P, TT, D])
    ident = sb("ident", [P, P])
    upto = sb("upto", [P, P])
    below = sb("below", [P, P])
    ones = sb("ones", [P, P])
    mask = sb("mask", [P, 2, 3 * P])
    iota = sb("iota", [P, SEQ])
    sm = sb("sm", [P, 2, 3 * P])
    pT = sb("pT", [P, 2, 3 * P])
    tiny = sb("tiny", [P, 64])
    zeros = sb("zeros", [1, 512], BF16)
    vecT = sb("vecT", [P, 27])
    bf = sb("bf", [P, HEADS])
    brt = sb("brt", [P, NE])
    pos_i = sb("pos_i", [P, TT], I32)
    logf = sb("logf", [P, TT, HEADS])
    logf2 = sb("logf2", [P, TT, 2 * HEADS])
    BR = 2 * HEADS
    cT = hn[0:HD + BR, 0, 768:1024]
    negI = sb("negI", [HD + BR, HEADS])
    posI = sb("posI", [HD + BR, HEADS])
    last8 = sb("last8", [HD + BR, 1])
    fgt = hn[:, 1, 768:768 + 6 * TT * HEADS].rearrange("p (i c) -> p i c", i=6)
    topi = sb("topi", [P, TT, 8], U32)
    most = sb("most", [1, 1], I32)
    posm = sb("posm", [P, TT, NE + 2])
    wt = sb("wt", [P, TT, NE + 2])

    def part(off, shape):
        n = int(np.prod(shape))
        v = arena[:, off:off + n]
        if len(shape) == 2:
            return v.rearrange("p (a b) -> p a b", a=shape[0])
        if len(shape) == 3:
            return v.rearrange("p (a b c) -> p a b c", a=shape[0], b=shape[1])
        return v

    hT = part(0, [KT, SEQ])
    gates = part(2048, [2 * KT, SEQ])
    qf = part(6144, [4, SEQ])
    kf = part(7168, [4, SEQ])
    vf = part(8192, [TT, FOX])
    qm = part(9216, [HEADS, SEQ])
    km = part(11264, [HEADS, SEQ])
    vm = part(13312, [TT, FOX])
    ropetmp = part(14336, [4, TT, HEADS * HALF])
    qlT = part(15360, [2, SEQ])
    ckT = part(15872, [SEQ])
    trig = part(16128, [4, TT * 2 * HALF])
    qtok = hn[:, :, 0:768]
    spj = part(9216, [TT, N_SMALL])
    kcat = part(9216 + TT * N_SMALL, [TT, QK])
    vec = part(9216 + TT * N_SMALL + TT * QK, [P])
    bias_q = part(4096, [HEADS // 2, SEQ])
    bias_k = part(5120, [HEADS // 2, SEQ])
    gbig = part(5120, [D])
    extra = [arena[:, 6144 + SLOT * i:6144 + SLOT * (i + 1)] for i in range(2)]
    su = part(0, [TT, P])
    sw = part(256, [TT, P])
    pw = part(512, [SEQ])
    xg = part(1024, [KT, P])
    av = part(4096, [KT, FEW])
    raw = part(2048, [2, 512])
    ysb = part(3072, [D])
    bg_raw = part(14336, [2 * FF])
    gt = part(15360, [KT, FEW])
    spare = sm[:, :, :].rearrange("p a b -> p (a b)")
    wr = spare[:, 512:768].rearrange("p (k e) -> p k e", k=KT)
    bgT = spare[:, 0:512].rearrange("p (e j) -> p e j", e=NE)
    sg = part(15872, [KT, FEW])
    ut = part(14336, [KT, FEW])
    gl = part(14848, [KT, FEW])
    squares = part(2048, [D])
    gfin = gbig

    psum = ctx.enter_context(nc.psum_tensor("psum", [P, 8 * 512], F32))
    bank = [psum[:, 512 * b:512 * b + 512] for b in range(8)]

    def nmax(b, t):
        return tiny[:, 40 + 2 * b + t:41 + 2 * b + t]

    def rsum(b, t):
        return tiny[:, 32 + 2 * b + t:33 + 2 * b + t]

    def ntop(t):
        return tiny[:, 52 + t:53 + t]

    def tsum(t):
        return tiny[:, 44 + t:45 + t]

    def fz(i):
        return fgt[:, i, :]

    square_scratch = part(14336, [512])
    lg = part(2048, [TT, NE])
    top8 = part(2112, [TT, 8])
    topf = part(2128, [TT, 8])
    topw = part(2144, [TT, TOPK])
    chosen = part(2160, [TT, NE])
    hot = part(2240, [TT, TOPK, NE])

    def steps_of(rounds):
        return [(u, r) for u in range(UNROLL) for r in range(rounds)]

    halves = ((0, slice(0, FEW)), (1, slice(FEW, P)))
    gate_bank, up_bank, out_bank, turn_bank = bank[0], bank[1], bank[2], bank[3]

    kv_here = sem("kv_here")
    x_here = [sem(f"x_here{t}") for t in range(TT)]
    vec_here = sem("vec_here")
    late_here = sem("late_here")
    bias_here = sem("bias_here")
    gfin_here = sem("gfin_here")
    consts = sem("consts")
    slot_in = [sem(f"slot_in{s}") for s in range(AHEAD)]
    written = [sem(f"bank_written{b}") for b in range(8)]
    read = [sem(f"bank_read{b}") for b in range(8)]
    dve_step = sem("dve_step")
    moe_step = sem("moe_step")
    act_step = sem("act_step")
    sq_x = sem("sq_x")
    ms_x = sem("ms_x")
    rt_x = sem("rt_x")
    xn_ready = sem("xn_ready")
    f_abs = sem("f_abs")
    f_exp = sem("f_exp")
    f_one = sem("f_one")
    f_ln = sem("f_ln")
    logf_ready = sem("logf_ready")
    lat_sq = sem("lat_sq")
    lat_ms = sem("lat_ms")
    lat_rt = sem("lat_rt")
    lat_ready = sem("lat_ready")
    kpe_ready = sem("kpe_ready")
    angle_ready = sem("angle_ready")
    trig_ready = sem("trig_ready")
    q_roped = sem("q_roped")
    qm_ready = sem("qm_ready")
    max_ready = sem("max_ready")
    exp_ready = sem("exp_ready")
    prob_ready = sem("prob_ready")
    merged = sem("merged")
    gates_sig = sem("gates_sig")
    top_ready = sem("top_ready")
    top_exp = sem("top_exp")
    sel_ready = sem("sel_ready")
    wt_ready = sem("wt_ready")
    most_ready = sem("most_ready")
    rest_zero = sem("rest_zero")
    bias_ready = sem("bias_ready")
    h_hi = sem("h_hi")
    h_split = sem("h_split")
    w_hi = sem("w_hi")
    w_split = sem("w_split")
    w_used = sem("w_used")
    merged_hi = sem("merged_hi")
    merged_split = sem("merged_split")
    s_ready = sem("s_ready")
    chunk_done = sem("chunk_done")
    gu_part = sem("gu_part")
    y_part = sem("y_part")
    raw_ready = sem("raw_ready")
    turned = sem("turned")
    gate_read = sem("gate_read")
    up_read = sem("up_read")
    g_ready = sem("g_ready")
    sig_ready = sem("sig_ready")
    av_ready = sem("av_ready")
    tr_done = sem("tr_done")
    p_ready = sem("p_ready")
    gather_done = sem("gather_done")
    xg_ready = sem("xg_ready")
    y_ready = sem("y_ready")
    scattered = sem("scattered")
    x_half = sem("x_half")
    x_final = sem("x_final")
    x_gained = sem("x_gained")
    rstd_ready = sem("rstd_ready")
    out_ready = [sem(f"out_ready{t}") for t in range(TT)]
    stored = sem("stored")

    def chunk_here(eng, c):
        eng.wait_ge(slot_in[c % PRE_RING], 16 * (c // PRE_RING + 1))

    def half_used(eng, j):
        if isinstance(HALF_END[j], str):
            bank_full(eng, HALF_END[j])
        else:
            eng.wait_ge(w_used, HALF_END[j])

    def half_raw(j):
        c, h = SPLIT[j // 2], j % 2
        if c == C_V:
            return cols(c)[:, 4 * h:4 * h + 4, :]
        if c >= C_O:
            return rows(c)[:, 2 * h:2 * h + 2, :]
        if c >= C_FO:
            return rows(c)[:, :, 512 * h:512 * h + 512]
        return cols(c)[:, :, 256 * h:256 * h + 256]

    def half_split(j):
        k = half_raw(j).shape[1]
        return [w[:, j % 2, :].rearrange("p (k n) -> p k n", k=k) for w in ws]

    def expert_chunk_here(eng, it, p):
        s = SLOT_AT[p]
        before = len([c for c in range(PRE) if c % PRE_RING == s]) + SLOT_AT[:p].count(s)
        eng.wait_ge(slot_in[s], it * (16 * SLOT_AT.count(s)) + 16 * (before + 1))

    def take_bank(eng, name):
        if NTH[name]:
            eng.wait_ge(read[BANK[name]], NTH[name])

    def bank_full(eng, name):
        eng.wait_ge(written[BANK[name]], NTH[name] + 1)

    def was_read(eng, name):
        eng.wait_ge(read[BANK[name]], NTH[name] + 1)

    def chunk(c):
        return ring[:, c % PRE_RING, :]

    wsm = chunk(C_SMALL)[:, 0:KT * N_SMALL].rearrange("p (k n) -> p k n", k=KT)
    wqb = chunk(C_QKV)[:, 0:2 * 768].rearrange("p (k n) -> p k n", k=2)
    wkvb = chunk(C_QKV)[:, 1536:1536 + 1024].rearrange("p (h n) -> p h n", h=HEADS)

    def cols(c):
        return chunk(c).rearrange("p (k n) -> p k n", k=KT)

    def rows(c):
        return chunk(c).rearrange("p (k n) -> p k n", k=4)

    def expert_slot(p):
        s = SLOT_AT[p]
        return ring[:, s, :] if s < RING else extra[s - RING]

    def gate_up(p):
        return expert_slot(p).rearrange("p (k n) -> p k n", k=2)

    def down_rows(p):
        return expert_slot(p).rearrange("p (k n) -> p k n", k=4)

    w_in_v = w_in[0].rearrange("(k p) n -> p k n", p=P)
    w_gu_v = w_gu[0].rearrange("e (k p) f -> p e k f", p=P)
    w_dn_v = w_down[0].rearrange("e (k p) n -> p e k n", p=P)

    block = ctx.enter_context(nc.Block())

    @block.sync
    def _(sp):
        x_v = x_in[0].rearrange("(t p) d -> p t d", p=P)
        for t in range(TT):
            sp.dma_start(x[:, t, :], x_v[:, t, :]).then_inc(x_here[t], 16)
        sp.wait_ge(x_here[0], 16)

        def load(c, pairs):
            for dst, src in pairs:
                sp.dma_start(dst, src).then_inc(slot_in[c % PRE_RING], 16)

        qkv = w_q_b[0].rearrange("(k p) n -> p k n", p=P)
        pre = [[(wsm, w_in_v[:, :, COL_SMALL:COL_GATE])]]
        pre += [[(cols(C_Q + i), w_in_v[:, :, 512 * i:512 * i + 512])] for i in range(3)]
        pre += [[(wqb, qkv)]]
        pre += [[(cols(C_G + i), w_in_v[:, :, COL_GATE + 512 * i:COL_GATE + 512 * i + 512])] for i in range(4)]
        pre += [[(rows(C_FO), w_fox_out[0].rearrange("(k p) n -> p k n", p=P))],
                [(rows(C_MO), w_mla_out[0].rearrange("(k p) n -> p k n", p=P))]]
        wo_v = w_o[0].rearrange("(k p) n -> p k n", p=P)
        pre += [[(rows(C_O + i), wo_v[:, 4 * i:4 * i + 4, :])] for i in range(2)]

        def chunk_read(c):
            if c in HALF_OF:
                sp.wait_ge(w_split, HALF_OF[c] + 2)
            else:
                bank_full(sp, {C_SMALL: "small1", C_QKV: "vm1"}[c])

        for c in range(PRE):
            if c >= PRE_RING:
                chunk_read(c - PRE_RING)
            load(c, pre[c])
            if c == C_QKV:
                sp.dma_start(wkvb, w_kv_b[0].rearrange("p (h n) -> p h n", h=HEADS)).then_inc(kv_here, 16)

        def load_expert(n, it=None):
            e, k = n // PER_E, n % PER_E
            p = n % BODY
            ee = e if it is None else it * UNROLL + e
            if k < 4:
                src = w_gu_v[:, bass.ds(ee, 1), 2 * k:2 * k + 2, :].rearrange("p a k f -> p (a k) f")
                dst = gate_up(p)
            else:
                src = w_dn_v[:, bass.ds(ee, 1), 4 * (k - 4):4 * (k - 4) + 4, :].rearrange("p a k n -> p (a k) n")
                dst = down_rows(p)
            sp.dma_start(dst, src).then_inc(slot_in[SLOT_AT[p]], 16)

        def last_in_slot(n):
            return next(q for q in range(n - 1, -1, -1) if SLOT_AT[q % BODY] == SLOT_AT[n % BODY])

        for n in range(AHEAD):
            s = SLOT_AT[n]
            if s < PRE_RING:
                chunk_read(next(c for c in range(PRE - 1, -1, -1) if c % PRE_RING == s))
            elif s < RING:
                bank_full(sp, "o3")
            else:
                bank_full(sp, f"pv{HEADS - 1}")
            load_expert(n)
        turns = (NE * PER_E - AHEAD) // BODY
        with sp.Fori(0, turns) as it:
            for n in range(AHEAD, AHEAD + BODY):
                sp.wait_ge(chunk_done, it * BODY + (last_in_slot(n) + 1))
                load_expert(n, it)
        for n in range(AHEAD + turns * BODY, NE * PER_E):
            sp.wait_ge(chunk_done, last_in_slot(n) + 1)
            load_expert(n)

        out_v = out[0].rearrange("(t p) d -> p t d", p=P)
        for t in range(TT):
            sp.wait_ge(out_ready[t], 2)
            sp.dma_start(out_v[:, t, :], hn[:, t, :]).then_inc(stored, 16)
        sp.wait_ge(stored, 16 * TT)

    @block.gpsimd
    def _(pool):
        k = 0

        def step(ins):
            nonlocal k
            k += 1
            ins.then_inc(consts, 1)
            pool.wait_ge(consts, k)

        step(pool.memset(ident[:, :], 0.0))
        step(pool.affine_select(out=ident[:, :], in_=ident[:, :], compare_op=ALU.not_equal, fill=1.0,
                                base=0, pattern=[[-1, P]], channel_multiplier=1))
        step(pool.memset(ones[:, :], 1.0))
        step(pool.affine_select(out=upto[:, :], in_=ones[:, :], compare_op=ALU.is_ge, fill=0.0,
                                base=0, pattern=[[1, P]], channel_multiplier=-1))
        step(pool.affine_select(out=below[:, :], in_=ones[:, :], compare_op=ALU.is_gt, fill=0.0,
                                base=0, pattern=[[1, P]], channel_multiplier=-1))
        step(pool.memset(zeros[:, :], 0.0))
        step(pool.memset(mask[:, :, :], 0.0))
        for b in (0, 2):
            step(pool.affine_select(out=mask[:, 0, b * P:(b + 1) * P], in_=mask[:, 0, b * P:(b + 1) * P],
                                    compare_op=ALU.is_ge, fill=MASKED, base=0, pattern=[[-1, P]],
                                    channel_multiplier=1))
            step(pool.memset(mask[0:64, 1, b * P + 64:(b + 1) * P], MASKED))
        step(pool.memset(kcat[:, :, :], 0.0))
        for lo in (0, HD):
            rows16 = slice(lo, lo + BR)
            step(pool.tensor_scalar(negI[rows16, :], ident[rows16, lo:lo + HEADS], -8.0, 0.0, ALU.mult, ALU.add))
            step(pool.tensor_scalar(posI[rows16, :], ident[rows16, lo + HEADS:lo + BR], 8.0, 0.0,
                                    ALU.mult, ALU.add))
            step(pool.tensor_scalar(last8[rows16, :], upto[rows16, lo + HEADS - 1:lo + HEADS], -1.0, 1.0,
                                    ALU.mult, ALU.add))
        step(pool.iota(iota[:, :], [[1, SEQ]], base=0, channel_multiplier=0,
                       allow_small_or_imprecise_dtypes=True))
        for t in range(TT):
            for i in range(HALF):
                step(pool.memset(trig[:, 0, t * 2 * HALF + i:t * 2 * HALF + i + 1],
                                 float(np.float32(THETA ** (-i / HALF)))))
        step(pool.memset(posm[:, :, NE:NE + 2], -1.0))
        step(pool.memset(wt[:, :, NE:NE + 2], 0.0))
        assert k == CONSTS

        was_read(pool, "cT")
        for h in range(HEADS):
            lo = HD * (h % 2)
            r = slice(lo, lo + BR)
            pool.tensor_scalar(bias_q[r, h // 2, :], cT[r, :], last8[r, :], negI[r, h:h + 1],
                               ALU.mult, ALU.add).then_inc(bias_ready, 1)
            pool.tensor_scalar(bias_k[r, h // 2, :], cT[r, :], upto[r, lo + HEADS - 1:lo + HEADS],
                               posI[r, h:h + 1], ALU.mult, ALU.add).then_inc(bias_ready, 1)

        pool.wait_ge(merged_split, 4)
        for lo in (NE, 2 * NE):
            pool.memset(ysb[lo:2 * lo, :], 0.0).then_inc(rest_zero, 1)
        bank_full(pool, "rl1")
        for lo in (NE, 2 * NE):
            pool.memset(pw[lo:2 * lo, :], 0.0).then_inc(rest_zero, 1)

    @block.scalar
    def _(act):
        act.dma_start(vec[0:8, :], g_attn[0].rearrange("(k p) -> k p", p=P)).then_inc(vec_here, 16)
        act.dma_start(vec[8:10, :], g_q_a[0].rearrange("(k p) -> k p", p=P)).then_inc(vec_here, 16)
        act.dma_start(vec[10:11, :], g_kv_a[0:1, :]).then_inc(vec_here, 16)
        act.dma_start(vec[11:27, :], b_merge[0].rearrange("b (k p) -> (b k) p", p=P)).then_inc(vec_here, 16)
        act.dma_start(bf[:, :], b_fgate[0:1, :].to_broadcast([P, HEADS])).then_inc(vec_here, 16)
        for t in range(TT):
            act.dma_start(pos_i[:, t:t + 1], pos_in[0, t * P:t * P + P].rearrange("(p a) -> p a", a=1))\
               .then_inc(vec_here, 16)

        def root_of_mean(t, n):
            act.wait_ge(ms_x, n + 1)
            nc.scalar.activation(tiny[:, 4 + t:5 + t], tiny[:, 2 + t:3 + t], ACT.Sqrt).then_inc(rt_x, 1)

        for t in range(TT):
            act.wait_ge(x_here[t], 16)
            nc.scalar.activation(hn[:, t, :], x[:, t, :], ACT.Square, accum_out=tiny[:, t:t + 1]).then_inc(sq_x, 1)
        root_of_mean(0, 0)
        root_of_mean(1, 1)

        def evac(name, dst, src, scale=None):
            bank_full(act, name)
            nc.scalar.activation(dst, src, ACT.Copy, **({} if scale is None else {"scale": scale}))\
              .then_inc(read[BANK[name]], 1)

        was_read(act, "vecT")
        for i in (2, 3):
            bank_full(act, f"xT{i}")
            nc.scalar.activation(hT[:, 2 * i, :], bank[i][:, 0:SEQ], ACT.Copy,
                                 scale=vecT[:, 2 * i:2 * i + 1]).then_inc(act_step, 1)
            nc.scalar.activation(hT[:, 2 * i + 1, :], bank[i][:, SEQ:512], ACT.Copy,
                                 scale=vecT[:, 2 * i + 1:2 * i + 2]).then_inc(read[i], 1)

        def split_hi(j, pieces=(0, 1)):
            chunk_here(act, SPLIT[j // 2])
            if j >= 2:
                half_used(act, j - 2)
            for i in pieces:
                hi, raw_half = half_split(j)[0], half_raw(j)
                k = hi.shape[1] // 2
                nc.scalar.activation(hi[:, i * k:i * k + k, :], raw_half[:, i * k:i * k + k, :], ACT.Copy)\
                  .then_inc(w_hi, 1)

        for i in range(4):
            was_read(act, f"xT{i}")
        nc.scalar.activation(hs[0][:, :, :], hT[:, :, :], ACT.Copy).then_inc(h_hi, 1)
        split_hi(0)
        split_hi(1)
        was_read(act, "small1")
        for t in range(TT):
            nc.scalar.activation(square_scratch[:, 0:Q_RANK], spj[:, t, 8:8 + Q_RANK], ACT.Square,
                                 accum_out=tiny[:, 8 + t:9 + t]).then_inc(lat_sq, 1)
            nc.scalar.activation(square_scratch[:, Q_RANK:Q_RANK + KV_RANK], spj[:, t, 264:264 + KV_RANK], ACT.Square,
                                 accum_out=tiny[:, 10 + t:11 + t]).then_inc(lat_sq, 1)
            act.wait_ge(lat_sq, 2 * t + 2)
        act.wait_ge(lat_ms, 1)
        nc.scalar.activation(tiny[:, 16:20], tiny[:, 12:16], ACT.Sqrt).then_inc(lat_rt, 1)
        for i in range(4):
            evac(f"qk{i}", qf[:, i, :], bank[6 + i % 2][:, 0:SEQ])
            if i % 2:
                split_hi(2 + i // 2)
        act.wait_ge(f_abs, 1)
        nc.scalar.activation(fz(1), fz(0), ACT.Exp, scale=-1.0).then_inc(f_exp, 1)
        act.wait_ge(f_one, 1)
        nc.scalar.activation(fz(3), fz(2), ACT.Ln).then_inc(f_ln, 1)
        for i in range(4, 8):
            evac(f"qk{i}", kf[:, i - 4, :], bank[6 + i % 2][:, 0:SEQ])
            if i % 2:
                split_hi(2 + i // 2)
        act.wait_ge(angle_ready, 1)
        nc.scalar.activation(trig[:, 2, :], trig[:, 0, :], ACT.Sin).then_inc(trig_ready, 1)
        split_hi(6)
        for t in range(TT):
            evac(f"v{t}", vf[:, t, :], bank[t][:, :])
        bank_full(act, "cT")
        nc.scalar.activation(cT[0:BR, :], bank[2][0:BR, 0:SEQ], ACT.Copy).then_inc(act_step, 1)
        nc.scalar.activation(cT[HD:HD + BR, :], bank[2][HD:HD + BR, 0:SEQ], ACT.Copy).then_inc(read[2], 1)
        for t in range(TT):
            evac(f"qb{t}", qtok[:, t, 0:512], bank[2 * t][:, :])
            evac(f"qc{t}", qtok[:, t, 512:768], bank[2 * t + 1][:, 0:256])
        for i in range(4):
            bank_full(act, f"kn{i}")
            nc.scalar.activation(km[0:HD, 2 * i, :], bank[4 + i][0:HD, 0:SEQ], ACT.Copy).then_inc(act_step, 1)
            nc.scalar.activation(km[0:HD, 2 * i + 1, :], bank[4 + i][HD:P, 0:SEQ], ACT.Copy)\
              .then_inc(read[4 + i], 1)
        for t in range(TT):
            evac(f"vm{t}", vm[:, t, :], bank[4 + t][:, :])
        split_hi(7, (0,))

        for i in range(2 * HEADS):
            b = i % 2
            act.wait_ge(max_ready, i + 1)
            nc.scalar.activation(sm[:, b, 0:P], sm[:, b, 0:P], ACT.Exp, bias=nmax(b, 0),
                                 accum_out=rsum(b, 0)).then_inc(exp_ready, 1)
            nc.scalar.activation(sm[:, b, P:3 * P], sm[:, b, P:3 * P], ACT.Exp, bias=nmax(b, 1),
                                 accum_out=rsum(b, 1)).then_inc(exp_ready, 1)
            bank_full(act, f"gate{i}")
            nc.scalar.activation(gates[:, i, :], bank[2 + b][:, 0:SEQ], ACT.Identity,
                                 bias=vecT[:, 11 + i:12 + i]).then_inc(read[2 + b], 1)
            split_hi(7 + (i + 1) // 2, (1 - i % 2,))
        was_read(act, f"gate{2 * HEADS - 1}")
        for i in (0, 2, 1, 3):
            nc.scalar.activation(gates[:, 4 * i:4 * i + 4, :], gates[:, 4 * i:4 * i + 4, :], ACT.Sigmoid)\
              .then_inc(gates_sig, 1)
        split_hi(15, (1,))
        split_hi(16)
        split_hi(17)
        for i in range(4):
            if i % 2:
                split_hi(18 + i // 2)
            act.wait_ge(merged, i + 1)
            nc.scalar.activation(hs[0][:, 2 * i:2 * i + 2, :], gates[:, 2 * i:2 * i + 2, :], ACT.Copy)\
              .then_inc(merged_hi, 1)
        act.wait_ge(merged_split, 4)
        act.dma_start(gbig, g_ffn[0:1, :].to_broadcast([P, D])).then_inc(late_here, 16)
        act.dma_start(brt[:, :], b_router[0:1, :].to_broadcast([P, NE])).then_inc(late_here, 16)
        act.dma_start(wr, w_router[0].rearrange("(k p) n -> p k n", p=P)).then_inc(late_here, 16)
        act.dma_start(bg_raw[0:NE, :], b_gu[0]).then_inc(bias_here, 16)
        act.dma_start(ysb[0:NE, :], b_down[0]).then_inc(bias_here, 16)
        split_hi(20)
        split_hi(21)

        for t in range(TT):
            was_read(act, f"o{2 * t}")
            was_read(act, f"o{2 * t + 1}")
            nc.scalar.activation(hn[:, t, :], x[:, t, :], ACT.Square, accum_out=tiny[:, t:t + 1]).then_inc(sq_x, 1)
            root_of_mean(t, 2 + t)
        for i in (1, 3):
            evac(f"hT{i}", hT[:, 2 * i:2 * i + 2, :], bank[4 + i][:, :].rearrange("p (k s) -> p k s", k=2))
        for t in range(TT):
            act.wait_ge(top_ready, t + 1)
            nc.scalar.activation(topw[:, t, :], top8[:, t, 0:TOPK], ACT.Exp, bias=ntop(t),
                                 accum_out=tsum(t)).then_inc(top_exp, 1)
        bank_full(act, "bgT")
        nc.scalar.activation(bgT.rearrange("p e j -> p j e"),
                             bank[4][:, :].rearrange("p (j e) -> p j e", e=NE), ACT.Copy).then_inc(read[4], 1)

        def experts(rounds):
            body = steps_of(rounds)
            m = len(body)

            def take_gather(pair):
                for i, b in ((0, up_bank), (1, turn_bank)):
                    act.wait_ge(gather_done, pair * 2 + (i + 1))
                    nc.scalar.activation(xg[:, 4 * i:4 * i + 4, :], b.rearrange("p (k s) -> p k s", k=4),
                                         ACT.Copy).then_inc(xg_ready, 1)

            act.sem_inc(y_ready, 1)
            take_gather(0)
            with act.Fori(0, NE // UNROLL) as it:
                for i, (u, r) in enumerate(body):
                    n = it * m + i
                    if i % 2:
                        act.wait_ge(tr_done, it * (m // 2) + (i // 2 + 1))
                        nc.scalar.activation(pw, turn_bank[:, 0:SEQ], ACT.Copy).then_inc(p_ready, 1)
                    if r == rounds - 1:
                        act.wait_ge(chunk_done, it * (UNROLL * PER_E) + (u * PER_E + 4))
                    else:
                        act.wait_ge(gu_part, it * (UNROLL * (rounds - 1)) + (u * (rounds - 1) + r + 1))
                    for j, b in ((0, gate_bank), (1, up_bank)):
                        nc.scalar.activation(raw[:, j, :], b, ACT.Copy).then_inc(raw_ready, 1)
                    act.wait_ge(g_ready, n + 1)
                    nc.scalar.activation(sg, gt, ACT.Sigmoid, scale=ALPHA).then_inc(sig_ready, 1)
                    if i % 2:
                        take_gather(it * (m // 2) + (i // 2 + 1))
                    if r == rounds - 1:
                        act.wait_ge(chunk_done, it * (UNROLL * PER_E) + (u * PER_E + 6))
                    else:
                        act.wait_ge(y_part, it * (UNROLL * (rounds - 1)) + (u * (rounds - 1) + r + 1))
                    for c, lanes in halves:
                        nc.scalar.activation(ysb[halves[i % 2][1], c * 512:c * 512 + 512], out_bank[lanes, :],
                                             ACT.Copy).then_inc(y_ready, 1)

        act.wait_ge(xn_ready, 4)
        act.dma_start(gfin, g_final.rearrange("(a d) -> a d", a=1).to_broadcast([P, D])).then_inc(gfin_here, 16)
        act.wait_ge(most_ready, 1)
        n_most = act.value_load(most[0:1, 0:1], min_val=0, max_val=SEQ)
        with act.If(n_most <= FEW):
            experts(1)
        with act.Else():
            experts(SEQ // FEW)

        nc.scalar.activation(tiny[:, 56:57], tiny[:, 4:5], ACT.Sqrt).then_inc(act_step, 1)
        for t in range(TT):
            act.wait_ge(x_final, t + 1)
            nc.scalar.activation(squares, x[:, t, :], ACT.Square, accum_out=tiny[:, t:t + 1]).then_inc(sq_x, 1)
            act.wait_ge(sq_x, t + 5)
        root_of_mean(0, 4)
        root_of_mean(1, 5)
        for t in range(TT):
            act.wait_ge(x_gained, t + 1)
            act.wait_ge(rstd_ready, t + 1)
            nc.scalar.activation(hn[:, t, 512:1024], hn[:, t, 512:1024], ACT.Copy, scale=tiny[:, 6 + t:7 + t])\
              .then_inc(out_ready[t], 1)

    @block.vector
    def _(dve):
        n = [0]

        def step(ins):
            n[0] += 1
            ins.then_inc(dve_step, 1)
            dve.wait_ge(dve_step, n[0])

        def mean_square(t, n):
            dve.wait_ge(sq_x, n + 1)
            nc.vector.tensor_scalar(tiny[:, 2 + t:3 + t], tiny[:, t:t + 1], 1.0 / D, EPS, ALU.mult, ALU.add)\
              .then_inc(ms_x, 1)

        def rsqrt(t, n):
            dve.wait_ge(rt_x, n + 1)
            step(nc.vector.reciprocal(tiny[:, 6 + t:7 + t], tiny[:, 4 + t:5 + t]))

        for t in range(TT):
            mean_square(t, t)
        for t in range(TT):
            rsqrt(t, t)
            nc.vector.tensor_scalar(hn[:, t, :], x[:, t, :], tiny[:, 6 + t:7 + t], None, ALU.mult)\
              .then_inc(xn_ready, 1)
        bank_full(dve, "vecT")
        nc.vector.tensor_copy(vecT[:, :], bank[7][:, 0:27]).then_inc(read[7], 1)
        was_read(dve, "vecT")
        for i in (0, 1):
            bank_full(dve, f"xT{i}")
            nc.vector.tensor_scalar(hT[:, 2 * i, :], bank[i][:, 0:SEQ], vecT[:, 2 * i:2 * i + 1], None,
                                    ALU.mult).then_inc(dve_step, 1)
            nc.vector.tensor_scalar(hT[:, 2 * i + 1, :], bank[i][:, SEQ:512], vecT[:, 2 * i + 1:2 * i + 2], None,
                                    ALU.mult).then_inc(read[i], 1)
            n[0] += 1

        def rest(out, whole, hi):
            return nc.vector.tensor_tensor(out, whole, hi.bitcast(F32), ALU.subtract)

        def split_lo(j):
            split_lo_piece(j, 0)
            split_lo_piece(j, 1)

        def split_lo_piece(j, i, part=None):
            dve.wait_ge(w_hi, 2 * j + (i + 1))
            hi, lo = half_split(j)
            k, n = hi.shape[1] // 2, hi.shape[2]
            at = slice(0, n) if part is None else slice(part * (n // 2), (part + 1) * (n // 2))
            ins = rest(lo[:, i * k:i * k + k, at], half_raw(j)[:, i * k:i * k + k, at], hi[:, i * k:i * k + k, at])
            if i == 1 and part != 0:
                ins.then_inc(w_split, 1)

        dve.wait_ge(h_hi, 1)
        rest(hs[1][:, :, :], hT[:, :, :], hs[0][:, :, :]).then_inc(h_split, 1)
        split_lo(0)
        split_lo(1)

        dve.wait_ge(vec_here, 16 * 7)
        dve.wait_ge(consts, CONSTS)
        step(nc.vector.tensor_copy(tiny[:, 20:22], pos_i[:, :]))
        ang = trig[:, 0, :].rearrange("p (t f) -> p t f", t=TT)
        trn = trig[:, 1, :].rearrange("p (t f) -> p t f", t=TT)
        for t in range(TT):
            step(nc.vector.tensor_scalar(ang[:, t, 0:HALF], ang[:, t, 0:HALF], tiny[:, 20 + t:21 + t], None,
                                         ALU.mult))
        step(nc.vector.tensor_copy(ang[:, :, HALF:2 * HALF], ang[:, :, 0:HALF]))
        step(nc.vector.tensor_scalar(trn[:, :, 0:HALF], ang[:, :, 0:HALF], 1.0 / (2.0 * float(np.pi)), None,
                                     ALU.mult))
        step(nc.vector.tensor_scalar(trn[:, :, HALF:2 * HALF], ang[:, :, HALF:2 * HALF],
                                     1.0 / (2.0 * float(np.pi)), 0.25, ALU.mult, ALU.add))
        step(nc.vector.tensor_scalar(trn, trn, MAGIC, None, ALU.add))
        step(nc.vector.tensor_scalar(trn, trn, -MAGIC, None, ALU.add))
        for c in TWO_PI:
            step(nc.vector.scalar_tensor_tensor(out=ang, in0=trn, scalar=-c, in1=ang, op0=ALU.mult, op1=ALU.add))
        step(nc.vector.tensor_scalar(ang[:, :, HALF:2 * HALF], ang[:, :, HALF:2 * HALF],
                                     float(np.pi) / 2.0, None, ALU.add))
        pi = float(np.nextafter(np.float32(np.pi), np.float32(0)))
        nc.vector.tensor_scalar(ang, ang, pi, -pi, ALU.min, ALU.max).then_inc(angle_ready, 1)

        for t in range(TT):
            bank_full(dve, f"small{t}")
            nc.vector.tensor_copy(spj[:, t, :], bank[4 + t][:, 0:N_SMALL]).then_inc(read[4 + t], 1)
        was_read(dve, "small0")
        was_read(dve, "small1")
        for t in range(TT):
            step(nc.vector.tensor_tensor(logf[:, t, :], spj[:, t, 0:HEADS], bf[:, :], ALU.add))
        lf = logf[:, :, :].rearrange("p t h -> p (t h)")
        nc.vector.scalar_tensor_tensor(out=fz(0), in0=lf, scalar=-1.0, in1=lf, op0=ALU.mult,
                                       op1=ALU.max).then_inc(f_abs, 1)
        dve.wait_ge(lat_sq, 4)
        step(nc.vector.tensor_scalar(tiny[:, 12:14], tiny[:, 8:10], 1.0 / Q_RANK, EPS, ALU.mult, ALU.add))
        nc.vector.tensor_scalar(tiny[:, 14:16], tiny[:, 10:12], 1.0 / KV_RANK, EPS, ALU.mult, ALU.add)\
          .then_inc(lat_ms, 1)
        dve.wait_ge(lat_rt, 1)
        step(nc.vector.reciprocal(tiny[:, 24:28], tiny[:, 16:20]))
        for t in range(TT):
            nc.vector.tensor_scalar(spj[:, t, 8:264], spj[:, t, 8:264], tiny[:, 24 + t:25 + t], None,
                                    ALU.mult).then_inc(lat_ready, 1)
            nc.vector.tensor_scalar(spj[:, t, 264:392], spj[:, t, 264:392], tiny[:, 26 + t:27 + t], None,
                                    ALU.mult).then_inc(lat_ready, 1)
        split_lo(2)
        split_lo(3)
        dve.wait_ge(f_exp, 1)
        nc.vector.tensor_scalar(fz(2), fz(1), 1.0, None, ALU.add).then_inc(f_one, 1)
        dve.wait_ge(f_one, 1)
        step(nc.vector.tensor_scalar(fz(4), fz(2), -1.0, None, ALU.add))
        step(nc.vector.tensor_tensor(fz(4), fz(1), fz(4), ALU.subtract))
        step(nc.vector.reciprocal(fz(5), fz(2)))
        step(nc.vector.tensor_tensor(fz(4), fz(4), fz(5), ALU.mult))
        dve.wait_ge(f_ln, 1)
        step(nc.vector.tensor_tensor(fz(4), fz(4), fz(3), ALU.add))
        step(nc.vector.scalar_tensor_tensor(out=lf, in0=lf, scalar=0.0, in1=fz(4), op0=ALU.min,
                                            op1=ALU.subtract))
        nc.vector.tensor_copy(logf2[:, :, :].rearrange("p t (a h) -> p t a h", a=2),
                              logf[:, :, None, :].to_broadcast([P, TT, 2, HEADS])).then_inc(logf_ready, 1)
        split_lo(4)
        split_lo(5)

        dve.wait_ge(trig_ready, 1)
        tr = trig[:, 2, :].rearrange("p (t f) -> p t f", t=TT)
        sin, cos = tr[:, :, 0:HALF], tr[:, :, HALF:2 * HALF]
        k1, k2 = spj[:, :, 392:392 + HALF], spj[:, :, 392 + HALF:392 + ROPE]
        m = [ropetmp[:, i, :, 0:HALF] for i in range(4)]
        nc.vector.tensor_tensor(m[0], k1, cos, ALU.mult).then_inc(dve_step, 1)
        nc.vector.tensor_tensor(m[1], k2, sin, ALU.mult).then_inc(dve_step, 1)
        nc.vector.tensor_tensor(m[2], k2, cos, ALU.mult).then_inc(dve_step, 1)
        n[0] += 3
        step(nc.vector.tensor_tensor(m[3], k1, sin, ALU.mult))
        step(nc.vector.tensor_tensor(kcat[:, :, HD:HD + HALF], m[0], m[1], ALU.subtract))
        nc.vector.tensor_tensor(kcat[:, :, HD + HALF:QK], m[2], m[3], ALU.add).then_inc(kpe_ready, 1)
        bank_full(dve, "qlT")
        step(nc.vector.tensor_scalar(qlT[:, 0, :], bank[3][:, 0:SEQ], vecT[:, 8:9], None, ALU.mult))
        nc.vector.tensor_scalar(qlT[:, 1, :], bank[3][:, SEQ:512], vecT[:, 9:10], None, ALU.mult)\
          .then_inc(read[3], 1)
        bank_full(dve, "ckT")
        nc.vector.tensor_scalar(ckT, bank[4][:, 0:SEQ], vecT[:, 10:11], None, ALU.mult).then_inc(read[4], 1)
        bank_full(dve, "kpT")
        nc.vector.tensor_copy(km[HD:QK, :, :], bank[5][HD:QK, None, 0:SEQ].to_broadcast([ROPE, HEADS, SEQ]))\
          .then_inc(read[5], 1)
        split_lo(6)
        for t in range(TT):
            was_read(dve, f"qb{t}")
            was_read(dve, f"qc{t}")
        for t in range(TT):
            qh = qtok[:, t, :].rearrange("p (h c) -> p h c", h=HEADS)
            q1, q2 = qh[:, :, HD:HD + HALF], qh[:, :, HD + HALF:QK]
            ct = cos[:, t, None, :].to_broadcast([P, HEADS, HALF])
            st = sin[:, t, None, :].to_broadcast([P, HEADS, HALF])
            m = [ropetmp[:, i, t, :].rearrange("p (h c) -> p h c", h=HEADS) for i in range(4)]
            nc.vector.tensor_tensor(m[0], q1, ct, ALU.mult).then_inc(dve_step, 1)
            nc.vector.tensor_tensor(m[1], q2, st, ALU.mult).then_inc(dve_step, 1)
            nc.vector.tensor_tensor(m[2], q2, ct, ALU.mult).then_inc(dve_step, 1)
            n[0] += 3
            step(nc.vector.tensor_tensor(m[3], q1, st, ALU.mult))
            step(nc.vector.tensor_tensor(q1, m[0], m[1], ALU.subtract))
            nc.vector.tensor_tensor(q2, m[2], m[3], ALU.add).then_inc(q_roped, 1)

        def qm_copy(i):
            bank_full(dve, f"qmT{i}")
            nc.vector.tensor_copy(qm[0:QK, 2 * i:2 * i + 2, :],
                                  bank[6 + i % 2][0:QK, :].rearrange("p (h s) -> p h s", h=2))\
              .then_inc(read[6 + i % 2], 1)

        for i in range(4):
            qm_copy(i)

        def softmax_max(i):
            b = i % 2
            bank_full(dve, f"sc{i}")
            if i >= 2:
                dve.wait_ge(written[BANK[f"pT{i - 2}"]], NTH[f"pT{i - 2}"] + 1)
            nc.vector.scalar_tensor_tensor(out=sm[:, b, :], in0=bank[b][:, 0:3 * P],
                                           scalar=(HD if i < HEADS else QK) ** -0.5, in1=mask[:, i // HEADS, :],
                                           op0=ALU.mult, op1=ALU.add).then_inc(read[b], 1)
            was_read(dve, f"sc{i}")
            step(nc.vector.tensor_reduce(nmax(b, 0), sm[:, b, 0:P], AX_X, ALU.max, negate=True))
            nc.vector.tensor_reduce(nmax(b, 1), sm[:, b, P:3 * P], AX_X, ALU.max, negate=True).then_inc(max_ready, 1)

        def softmax_norm(i):
            b = i % 2
            dve.wait_ge(exp_ready, 2 * i + 2)
            step(nc.vector.reciprocal(tiny[:, 36 + 2 * b:38 + 2 * b], tiny[:, 32 + 2 * b:34 + 2 * b]))
            nc.vector.tensor_scalar(sm[:, b, 0:P], sm[:, b, 0:P], tiny[:, 36 + 2 * b:37 + 2 * b], None,
                                    ALU.mult).then_inc(prob_ready, 1)
            nc.vector.tensor_scalar(sm[:, b, P:3 * P], sm[:, b, P:3 * P], tiny[:, 37 + 2 * b:38 + 2 * b], None,
                                    ALU.mult).then_inc(prob_ready, 1)

        def probs_out(i):
            b = i % 2
            bank_full(dve, f"pT{i}")
            nc.vector.tensor_copy(pT[:, b, :], bank[4 + b][:, 0:3 * P]).then_inc(read[4 + b], 1)

        def heads_out(pair):
            bank_full(dve, f"pv{pair}")
            o = bank[6 + pair % 2][:, 0:SEQ]
            step(nc.vector.tensor_copy(ys[0][:, pair, :], o))
            rest(ys[1][:, pair, :], o, ys[0][:, pair, :]).then_inc(read[6 + pair % 2], 1)

        for i in range(2 * HEADS + 1):
            if i < 2 * HEADS:
                softmax_max(i)
            if i:
                probs_out(i - 1)
            split_lo_piece(7 + i // 2, i % 2, 0)
            if i < 2 * HEADS:
                softmax_norm(i)
            if i and i % 2 == 0:
                heads_out(i // 2 - 1)
            split_lo_piece(7 + i // 2, i % 2, 1)

        split_lo_piece(15, 1)

        g4 = lambda a: gates[:, a:a + 2, :].rearrange("p k s -> p (k s)")
        for i in range(4):
            dve.wait_ge(gates_sig, 1 + (i >= 2) * 2)
            bank_full(dve, f"fo{i}")
            nc.vector.tensor_tensor(g4(2 * i), bank[i][:, :], g4(2 * i), ALU.mult).then_inc(read[i], 1)
            if i % 2:
                split_lo(16 + i // 2)
        for i in range(4):
            dve.wait_ge(gates_sig, 4)
            bank_full(dve, f"mo{i}")
            nc.vector.tensor_tensor(g4(8 + 2 * i), bank[4 + i][:, :], g4(8 + 2 * i), ALU.mult).then_inc(read[4 + i], 1)
            was_read(dve, f"mo{i}")
            was_read(dve, f"fo{i}")
            nc.vector.tensor_tensor(g4(2 * i), g4(2 * i), g4(8 + 2 * i), ALU.add).then_inc(merged, 1)
            if i % 2:
                split_lo(18 + i // 2)
            dve.wait_ge(merged_hi, i + 1)
            rest(hs[1][:, 2 * i:2 * i + 2, :], gates[:, 2 * i:2 * i + 2, :], hs[0][:, 2 * i:2 * i + 2, :])\
                .then_inc(merged_split, 1)
        split_lo(20)
        split_lo(21)

        for i in range(4):
            t, c = i // 2, (i % 2) * 512
            bank_full(dve, f"o{i}")
            nc.vector.tensor_tensor(x[:, t, c:c + 512], bank[i][:, :], x[:, t, c:c + 512], ALU.add)\
              .then_inc(read[i], 1)
            if i % 2 == 0:
                continue
            mean_square(t, 2 + t)
            rsqrt(t, 2 + t)
            dve.wait_ge(late_here, 48)
            nc.vector.scalar_tensor_tensor(out=hn[:, t, :], in0=x[:, t, :], scalar=tiny[:, 6 + t:7 + t],
                                           in1=gbig, op0=ALU.mult, op1=ALU.mult).then_inc(xn_ready, 1)
        for i in (0, 2):
            bank_full(dve, f"hT{i}")
            nc.vector.tensor_copy(hT[:, 2 * i:2 * i + 2, :], bank[4 + i][:, :].rearrange("p (k s) -> p k s", k=2))\
              .then_inc(read[4 + i], 1)

        for t in range(TT):
            bank_full(dve, f"rl{t}")
            nc.vector.tensor_tensor(lg[:, t, :], bank[t][:, 0:NE], brt[:, :], ALU.add).then_inc(read[t], 1)
            was_read(dve, f"rl{t}")
            step(nc.vector.max(top8[:, t, :], lg[:, t, :]))
            nc.vector.tensor_scalar(ntop(t), top8[:, t, 0:1], -1.0, None, ALU.mult).then_inc(top_ready, 1)
            step(nc.vector.max_index(topi[:, t, :], top8[:, t, :], lg[:, t, :]))
            step(nc.vector.tensor_copy(topf[:, t, :], topi[:, t, :]))
            step(nc.vector.tensor_tensor(hot[:, t, :, :], iota[:, None, 0:NE].to_broadcast([P, TOPK, NE]),
                                         topf[:, t, 0:TOPK, None].to_broadcast([P, TOPK, NE]), ALU.is_equal))
            nc.vector.tensor_reduce(chosen[:, t, :], hot[:, t, :, :].rearrange("p k e -> p e k"), AX_X, ALU.add)\
              .then_inc(sel_ready, 1)
        dve.wait_ge(top_exp, TT)
        step(nc.vector.reciprocal(tiny[:, 46:48], tiny[:, 44:46]))
        for t in range(TT):
            step(nc.vector.tensor_scalar(topw[:, t, :], topw[:, t, :], tiny[:, 46 + t:47 + t], None, ALU.mult))
            step(nc.vector.tensor_tensor(hot[:, t, :, :], hot[:, t, :, :],
                                         topw[:, t, :, None].to_broadcast([P, TOPK, NE]), ALU.mult))
            nc.vector.tensor_reduce(wt[:, t, 0:NE], hot[:, t, :, :].rearrange("p k e -> p e k"), AX_X, ALU.add)\
              .then_inc(wt_ready, 1)
        bank_full(dve, "pos")
        nc.vector.reduce_max(tiny[0:1, 48:49], bank[2][0:1, 64:96], AX_X).then_inc(dve_step, 1)
        n[0] += 1
        for t in range(TT):
            ins = nc.vector.scalar_tensor_tensor(out=posm[:, t, 0:NE], in0=bank[2][:, 32 * t:32 * t + 32], scalar=1.0,
                                                 in1=chosen[:, t, :], op0=ALU.add, op1=ALU.mult)
            if t < TT - 1:
                step(ins)
            else:
                ins.then_inc(read[2], 1)
        was_read(dve, "pos")
        nc.vector.tensor_copy(most[:, :], tiny[0:1, 48:49]).then_inc(most_ready, 1)
        step(nc.vector.tensor_scalar(posm[:, :, 0:NE], posm[:, :, 0:NE], -1.0, None, ALU.add))
        dve.wait_ge(wt_ready, TT)
        bank_full(dve, "wT")
        nc.vector.tensor_copy(pw[0:NE, :], bank[3][0:NE, 0:SEQ]).then_inc(read[3], 1)
        was_read(dve, "wT")
        dve.sem_inc(p_ready, 1)
        was_read(dve, "bgT")
        dve.wait_ge(most_ready, 1)
        n_most = dve.value_load(most[0:1, 0:1], min_val=0, max_val=SEQ)

        def experts(rounds):
            body = steps_of(rounds)
            m = len(body)
            k = [0]

            def own(it, ins):
                k[0] += 1
                ins.then_inc(moe_step, 1)
                dve.wait_ge(moe_step, it * (2 * m) + k[0])

            def slots(it, i):
                for h in range(2):
                    u, r = (i + h) // rounds, (i + h) % rounds
                    e = bass.ds(u if it is None else it * UNROLL + u, 1)
                    at = iota[:, r * FEW:r * FEW + FEW]
                    for t in range(TT):
                        nc.vector.tensor_scalar(su[:, t, halves[h][1]], at, posm[:, t, e], None,
                                                ALU.is_equal).then_inc(s_ready, 1)
                        nc.vector.tensor_scalar(sw[:, t, halves[h][1]], at, posm[:, t, e], wt[:, t, e],
                                                ALU.is_equal, ALU.mult).then_inc(s_ready, 1)

            dve.sem_inc(gate_read, 1)
            dve.sem_inc(up_read, 1)
            slots(None, 0)
            turned_view = [b.rearrange("p (c s) -> p c s", c=KT) for b in (turn_bank, gate_bank)]
            with dve.Fori(0, NE // UNROLL) as it:
                for i, (u, r) in enumerate(body):
                    n_step = it * m + i
                    if i % 2:
                        dve.wait_ge(tr_done, it * (m // 2) + (i // 2 + 1))
                        slots(it, i + 1)

                    def bias(j):
                        return bgT[:, bass.ds(it * UNROLL + u, 1), j:j + KT].rearrange("p a j -> p (a j)")\
                            [:, :, None].to_broadcast([P, KT, FEW])

                    dve.wait_ge(turned, n_step * 2 + 1)
                    nc.vector.tensor_tensor(gt, turned_view[0], bias(0), ALU.add).then_inc(gate_read, 1)
                    dve.wait_ge(gate_read, n_step + 2)
                    nc.vector.tensor_scalar(gt, gt, LIMIT, None, ALU.min).then_inc(g_ready, 1)
                    dve.wait_ge(turned, n_step * 2 + 2)
                    nc.vector.tensor_tensor(ut, turned_view[1], bias(KT), ALU.add).then_inc(up_read, 1)
                    dve.wait_ge(up_read, n_step + 2)
                    own(it, nc.vector.tensor_scalar(ut, ut, LIMIT, -LIMIT, ALU.min, ALU.max))
                    dve.wait_ge(sig_ready, n_step + 1)
                    own(it, nc.vector.tensor_tensor(gl, gt, sg, ALU.mult))
                    nc.vector.scalar_tensor_tensor(out=av, in0=ut, scalar=1.0, in1=gl, op0=ALU.add,
                                                   op1=ALU.mult).then_inc(av_ready, 1)
                    dve.wait_ge(av_ready, n_step + 1)
            assert k[0] == 2 * m

        def residual(t):
            nc.vector.tensor_tensor(x[:, t, 0:512], bank[4 + 2 * t][:, :], x[:, t, 0:512], ALU.add)\
              .then_inc(x_half, 1)
            dve.wait_ge(x_half, t + 1)
            nc.vector.tensor_tensor(x[:, t, 512:1024], bank[5 + 2 * t][:, :], x[:, t, 512:1024], ALU.add)\
              .then_inc(x_final, 1)
            dve.wait_ge(x_final, t + 1)

        def gained(t):
            nc.vector.tensor_tensor(hn[:, t, :], x[:, t, :], gfin, ALU.mult).then_inc(x_gained, 1)

        def run(rounds):
            experts(rounds)
            dve.wait_ge(scattered, NE * rounds + 1)
            residual(0)
            dve.wait_ge(gfin_here, 16)
            gained(0)
            dve.wait_ge(scattered, NE * rounds + 2)
            residual(1)

        with dve.If(n_most <= FEW):
            run(1)
        with dve.Else():
            run(SEQ // FEW)

        mean_square(0, 4)
        gained(1)
        mean_square(1, 5)
        for t in range(TT):
            dve.wait_ge(rt_x, t + 5)
            nc.vector.reciprocal(tiny[:, 6 + t:7 + t], tiny[:, 4 + t:5 + t]).then_inc(rstd_ready, 1)
            dve.wait_ge(rstd_ready, t + 1)
            dve.wait_ge(x_gained, t + 1)
            nc.vector.tensor_scalar(hn[:, t, 0:512], hn[:, t, 0:512], tiny[:, 6 + t:7 + t], None, ALU.mult)\
              .then_inc(out_ready[t], 1)

    @block.tensor
    def _(pe):
        def mm(o, lhsT, rhs, start=True, stop=True):
            return nc.tensor.matmul(o, lhsT, rhs, start=start, stop=stop, skip_group_check=True)

        def split(parts, *at):
            return [part[at] for part in parts]

        def mm_split(o, lhsT, rhs, start, stop):
            mm(o, lhsT[0], rhs[0], start, False)
            mm(o, lhsT[0], rhs[1], False, False)
            return mm(o, lhsT[1], rhs[0], False, stop)

        def filled(name, ins):
            ins.then_inc(written[BANK[name]], 1)

        def to_features(prefix, banks, norm):
            for t in range(TT):
                pe.wait_ge(xn_ready, norm * TT + t + 1)
                for i in range(4):
                    if t == 0:
                        take_bank(pe, f"{prefix}{i}")
                    for k in (2 * i, 2 * i + 1):
                        ins = nc.tensor.transpose(bank[banks + i][:, (k % 2) * SEQ + t * P:(k % 2) * SEQ + t * P + P],
                                                  hn[:, t, k * P:k * P + P], ident[:, :])
                    if t == TT - 1:
                        filled(f"{prefix}{i}", ins)

        pe.wait_ge(consts, CONSTS_PE)
        to_features("xT", 0, 0)
        pe.wait_ge(vec_here, 16 * 7)
        filled("vecT", nc.tensor.transpose(bank[7][:, 0:27], vec[0:27, :], ident[0:27, 0:27]))

        for i in range(4):
            was_read(pe, f"xT{i}")
        chunk_here(pe, C_SMALL)
        for t in range(TT):
            for k in range(KT):
                ins = mm(bank[4 + t][:, 0:N_SMALL], hT[:, k, t * P:t * P + P], wsm[:, k, :], k == 0, k == KT - 1)
            filled(f"small{t}", ins)
        every = slice(None)

        def columns(o, i, first_half):
            j = first_half + i // 2
            pe.wait_ge(w_split, j + 1)
            for k in range(KT):
                ins = mm_split(o, split(half_split(j), every, k, slice((i % 2) * P, (i % 2) * P + P)),
                               split(hs, every, k), k == 0, k == KT - 1)
            return ins

        pe.wait_ge(h_split, 1)
        for i in range(8):
            take_bank(pe, f"qk{i}")
            filled(f"qk{i}", columns(bank[6 + i % 2][:, 0:SEQ], i, HALF_OF[C_Q]))
        for half in range(2):
            j = HALF_OF[C_V] + half
            pe.wait_ge(w_split, j + 1)
            for t in range(TT):
                if half == 0:
                    take_bank(pe, f"v{t}")
                for k in range(4):
                    ins = mm_split(bank[t][:, :], split(hs, every, 4 * half + k, slice(t * P, t * P + P)),
                                   split(half_split(j), every, k), half + k == 0, 4 * half + k == KT - 1)
                if half:
                    filled(f"v{t}", ins)
            if half == 0:
                ins.then_inc(w_used, 1)
        pe.wait_ge(logf_ready, 1)
        take_bank(pe, "cT")
        for lo in (0, HD):
            mm(bank[2][lo:lo + BR, 0:P], logf2[:, 0, :], upto[:, :])
            mm(bank[2][lo:lo + BR, P:SEQ], logf2[:, 0, :], ones[:, :], True, False)
            ins = mm(bank[2][lo:lo + BR, P:SEQ], logf2[:, 1, :], upto[:, :], False, True)
        filled("cT", ins)
        pe.wait_ge(lat_ready, 4)
        take_bank(pe, "qlT")
        for r in range(2):
            for t in range(TT):
                ins = nc.tensor.transpose(bank[3][:, r * SEQ + t * P:r * SEQ + t * P + P],
                                          spj[:, t, 8 + r * P:8 + r * P + P], ident[:, :])
        filled("qlT", ins)
        take_bank(pe, "ckT")
        for t in range(TT):
            ins = nc.tensor.transpose(bank[4][:, t * P:t * P + P], spj[:, t, 264:392], ident[:, :])
        filled("ckT", ins)
        pe.wait_ge(kpe_ready, 1)
        take_bank(pe, "kpT")
        for t in range(TT):
            ins = nc.tensor.transpose(bank[5][0:QK, t * P:t * P + P], kcat[:, t, :], ident[:, :])
        filled("kpT", ins)
        was_read(pe, "qlT")
        chunk_here(pe, C_QKV)
        for t in range(TT):
            for name, b, lo, w in ((f"qb{t}", 2 * t, 0, 512), (f"qc{t}", 2 * t + 1, 512, 256)):
                take_bank(pe, name)
                for r in range(2):
                    ins = mm(bank[b][:, 0:w], qlT[:, r, t * P:t * P + P], wqb[:, r, lo:lo + w], r == 0, r == 1)
                filled(name, ins)
        was_read(pe, "ckT")
        pe.wait_ge(kv_here, 16)
        for i in range(4):
            take_bank(pe, f"kn{i}")
            for h in (2 * i, 2 * i + 1):
                ins = mm(bank[4 + i][HD * (h % 2):HD * (h % 2) + HD, 0:SEQ], wkvb[:, h, 0:HD], ckT)
            filled(f"kn{i}", ins)
        for t in range(TT):
            take_bank(pe, f"vm{t}")
            filled(f"vm{t}", mm(bank[4 + t].rearrange("p (h c) -> p h c", h=HEADS), ckT[:, t * P:t * P + P],
                                wkvb[:, :, HD:2 * HD]))
        pe.wait_ge(q_roped, TT)
        for i in range(4):
            take_bank(pe, f"qmT{i}")
            for h in (2 * i, 2 * i + 1):
                for t in range(TT):
                    ins = nc.tensor.transpose(bank[6 + i % 2][0:QK, (h % 2) * SEQ + t * P:(h % 2) * SEQ + t * P + P],
                                              qtok[:, t, h * QK:h * QK + QK], ident[:, :])
            filled(f"qmT{i}", ins)

        def scores(i):
            b, h = i % 2, i % HEADS
            take_bank(pe, f"sc{i}")
            for t in range(TT):
                o = bank[b][:, t * P:t * P + (t + 1) * P]
                tq, tk = slice(t * P, t * P + P), slice(0, (t + 1) * P)
                if i < HEADS:
                    lo = HD * (h % 2)
                    hd, r = slice(lo, lo + HD), slice(lo, lo + BR)
                    mm(o, qf[hd, h // 2, tq], kf[hd, h // 2, tk], True, False)
                    pe.wait_ge(bias_ready, 2 * h + 2)
                    ins = mm(o, bias_q[r, h // 2, tq], bias_k[r, h // 2, tk], False, True)
                else:
                    ins = mm(o, qm[0:QK, h, tq], km[0:QK, h, tk])
            filled(f"sc{i}", ins)

        def turn_probs(i):
            b = i % 2
            pe.wait_ge(prob_ready, 2 * i + 2)
            take_bank(pe, f"pT{i}")
            for c in range(3):
                ins = nc.tensor.transpose(bank[4 + b][:, c * P:c * P + P], sm[:, b, c * P:c * P + P], ident[:, :])
            filled(f"pT{i}", ins)

        def gate_tile(i):
            take_bank(pe, f"gate{i}")
            filled(f"gate{i}", columns(bank[2 + i % 2][:, 0:SEQ], i, HALF_OF[C_G]))

        def mix_values(pair):
            v = vf if 2 * pair < HEADS else vm
            was_read(pe, f"pT{2 * pair}")
            was_read(pe, f"pT{2 * pair + 1}")
            take_bank(pe, f"pv{pair}")
            o = bank[6 + pair % 2]
            for k, q, p in ((0, slice(0, SEQ), slice(0, SEQ)), (1, slice(P, SEQ), slice(SEQ, 3 * P))):
                for b in range(2):
                    c = ((2 * pair) % HEADS + b) * HD
                    ins = mm(o[HD * b:HD * b + HD, q], v[:, k, c:c + HD], pT[:, b, p], k == 0, k == 1)
            filled(f"pv{pair}", ins)

        for name in ("qk6", "qk7", "v1", "cT", "vm1", "qmT3", "kn3", "kpT"):
            was_read(pe, name)
        for i in range(2 * HEADS + 1):
            if i < 2 * HEADS:
                scores(i)
            if i:
                turn_probs(i - 1)
            if i < 2 * HEADS:
                gate_tile(i)
            if i and i % 2 == 0:
                mix_values(i // 2 - 1)

        for tag, c, b0, first in (("fo", C_FO, 0, 0), ("mo", C_MO, 4, HEADS // 2)):
            was_read(pe, f"pv{first + HEADS // 2 - 2}")
            was_read(pe, f"pv{first + HEADS // 2 - 1}")
            for i in range(4):
                half = HALF_OF[c] + i // 2
                pe.wait_ge(w_split, half + 1)
                take_bank(pe, f"{tag}{i}")
                for j in range(2):
                    at = (2 * (i % 2) + j) * P
                    for k in range(4):
                        ins = mm_split(bank[b0 + i][:, j * SEQ:j * SEQ + SEQ],
                                       split(half_split(half), every, k, slice(at, at + P)),
                                       split(ys, every, first + k), k == 0, k == 3)
                filled(f"{tag}{i}", ins)
        for part in range(4):
            half = HALF_OF[C_O] + part
            pe.wait_ge(merged_split, part + 1)
            pe.wait_ge(w_split, half + 1)
            for i in range(4):
                t, c = i // 2, (i % 2) * 512
                if part == 0:
                    take_bank(pe, f"o{i}")
                for k in range(2):
                    ins = mm_split(bank[i][:, :], split(hs, every, 2 * part + k, slice(t * P, t * P + P)),
                                   split(half_split(half), every, k, slice(c, c + 512)),
                                   part + k == 0, 2 * part + k == KT - 1)
                if part == 3:
                    filled(f"o{i}", ins)
            if part < 3:
                ins.then_inc(w_used, 1)
        to_features("hT", 4, 1)
        for i in range(4):
            was_read(pe, f"hT{i}")
        pe.wait_ge(late_here, 48)
        for t in range(TT):
            take_bank(pe, f"rl{t}")
            for k in range(KT):
                ins = mm(bank[t][:, 0:NE], hT[:, k, t * P:t * P + P], wr[:, k, :], k == 0, k == KT - 1)
            filled(f"rl{t}", ins)
        pe.wait_ge(bias_here, 32)
        take_bank(pe, "bgT")
        for j in range(2 * FF // P):
            tile = KT * (j // KT) + 4 * (j % 2) + (j % KT) // 2
            ins = nc.tensor.transpose(bank[4][:, NE * j:NE * j + NE], bg_raw[0:NE, tile * P:tile * P + P],
                                      ident[0:NE, 0:NE])
        filled("bgT", ins)
        pe.wait_ge(sel_ready, TT)
        take_bank(pe, "pos")
        mm(bank[2][:, 0:NE], below[:, :], chosen[:, 0, :])
        mm(bank[2][:, NE:2 * NE], ones[:, :], chosen[:, 0, :], True, False)
        mm(bank[2][:, NE:2 * NE], below[:, :], chosen[:, 1, :], False, True)
        mm(bank[2][0:1, 64:96], ones[:, 0:1], chosen[:, 0, :], True, False)
        filled("pos", mm(bank[2][0:1, 64:96], ones[:, 0:1], chosen[:, 1, :], False, True))
        pe.wait_ge(wt_ready, TT)
        take_bank(pe, "wT")
        for t in range(TT):
            ins = nc.tensor.transpose(bank[3][0:NE, t * P:t * P + P], wt[:, t, 0:NE], ident[:, :])
        filled("wT", ins)
        was_read(pe, "bgT")
        for b in range(4, 8):
            mm(bank[b][:, :], zeros[:, 0:P], zeros[:, :], True, False)
        pe.wait_ge(rest_zero, 4)
        pe.wait_ge(most_ready, 1)
        n_most = pe.value_load(most[0:1, 0:1], min_val=0, max_val=SEQ)

        def experts(rounds):
            body = steps_of(rounds)
            m = len(body)

            def gather(pair, i):
                pe.wait_ge(s_ready, pair * 8 + 8)
                b = (up_bank, turn_bank)[i]
                for k in range(4):
                    f = (4 * i + k) * P
                    for t in range(TT):
                        ins = mm(b[:, k * P:k * P + P], hn[:, t, f:f + P], su[:, t, :], t == 0, t == TT - 1)
                ins.then_inc(gather_done, 1)

            def scatter(it, i, t):
                pe.wait_ge(y_ready, it * (2 * m) + (2 * i + 1))
                pe.wait_ge(p_ready, it * (m // 2) + (i // 2 + 1))
                for half in range(2):
                    ins = mm(bank[4 + 2 * t + half], pw[:, t * P:t * P + P],
                             ysb[:, half * 512:half * 512 + 512], False, False)
                ins.then_inc(scattered, 1)

            gather(0, 0)
            gather(0, 1)
            with pe.Fori(0, NE // UNROLL) as it:
                for i, (u, r) in enumerate(body):
                    n = it * m + i
                    own = halves[i % 2][1]
                    last = r == rounds - 1
                    if i % 2 == 0:
                        pe.wait_ge(xg_ready, it * m + (i + 2))
                    pe.wait_ge(up_read, n + 1)
                    if i % 2 == 0:
                        pe.wait_ge(gate_read, n + 1)
                    for ch in range(4):
                        if r == 0:
                            expert_chunk_here(pe, it, u * PER_E + ch)
                        for k in range(2):
                            f = 2 * ch + k
                            for j, b in ((0, gate_bank), (1, up_bank)):
                                for c, lanes in halves:
                                    ins = mm(b[lanes, :], xg[:, f, own],
                                             gate_up(u * PER_E + ch)[:, k, j * FF + c * 512:j * FF + c * 512 + 512],
                                             f == 0, f == KT - 1)
                        if last:
                            ins.then_inc(chunk_done, 1)
                        elif ch == 3:
                            ins.then_inc(gu_part, 1)
                        if ch == 0 and i % 2:
                            pe.wait_ge(gate_read, n + 1)
                            for t in range(TT):
                                ins = nc.tensor.transpose(turn_bank[:, t * P:t * P + P], sw[:, t, :], ident[:, :])
                            ins.then_inc(tr_done, 1)
                    if i % 2 == 0:
                        scatter(it, i, 0)
                    if i % 2:
                        pe.wait_ge(p_ready, it * (m // 2) + (i // 2 + 2))
                    for j, b in ((0, turn_bank), (1, gate_bank)):
                        pe.wait_ge(raw_ready, n * 2 + (j + 1))
                        for c in range(4):
                            ins = nc.tensor.transpose(b[:, c * P:c * P + P], raw[:, j, c * P:c * P + P], ident[:, :])
                        ins.then_inc(turned, 1)
                    if i % 2 == 0:
                        scatter(it, i, 1)
                    if i % 2:
                        gather(it * (m // 2) + (i // 2 + 1), 0)
                        pe.wait_ge(gate_read, n + 2)
                        gather(it * (m // 2) + (i // 2 + 1), 1)
                    pe.wait_ge(av_ready, n + 1)
                    pe.wait_ge(y_ready, it * (2 * m) + (2 * i + 1))
                    for half in range(2):
                        if r == 0:
                            expert_chunk_here(pe, it, u * PER_E + 4 + half)
                        for j in range(4):
                            for c, lanes in halves:
                                ins = mm(out_bank[lanes, :], av[:, 2 * j + half, :],
                                         down_rows(u * PER_E + 4 + half)[:, j, c * 512:c * 512 + 512],
                                         half == 0 and j == 0, half == 1 and j == 3)
                        if last:
                            ins.then_inc(chunk_done, 1)
                        elif half:
                            ins.then_inc(y_part, 1)
            for t in range(TT):
                scatter(NE // UNROLL, 0, t)

        with pe.If(n_most <= FEW):
            experts(1)
        with pe.Else():
            experts(SEQ // FEW)

    ctx.close()


_INS = ["x", "positions", "g_attn_norm", "w_in", "b_fgate", "g_q_a", "w_q_b", "g_kv_a", "w_kv_b", "w_fox_out",
        "w_mla_out", "b_merge", "w_o", "g_ffn_norm", "w_router", "b_router", "w_gu", "b_gu", "w_down", "b_down",
        "g_final"]


def kernel(**inputs):
    import numpy as _np
    import concourse.bacc as _bacc
    from concourse import mybir as _mybir
    from concourse.bass_utils import run_bass_kernel_spmd as _run

    nc = _bacc.Bacc("TRN2", target_bir_lowering=False, num_devices=1, dynamic_dma_scratch_size=1024)
    arrays, args = {}, []
    for name in _INS:
        a = _np.ascontiguousarray(inputs[name])
        arrays[f"in_{name}"] = a
        args.append(nc.dram_tensor(f"in_{name}", a.shape, _mybir.dt.from_np(a.dtype), kind="ExternalInput").ap())
    args.append(nc.dram_tensor("out_0", (1, 256, 1024), _mybir.dt.float32, kind="ExternalOutput").ap())
    build(nc, *args)
    r = _run(nc, [arrays], core_ids=[0])
    return r.results[0]["out_0"]
```
